# Optimizing a Trainium2 kernel written in Bass

```python
import math
import jax
import jax.numpy as jnp
from jax import lax
import numpy as np
import jax, jax.numpy as jnp

D_MODEL = 1024
BATCH = 1
SEQ = 1024
DEPTH = 1

GRID_W = 64
CTX_LEN = 256
MIX_W = D_MODEL
GDN_W = MIX_W // 2
GDN_DK = 128
GDN_DV = 128
GDN_HEADS = GDN_W // GDN_DV
SSM_W = MIX_W - GDN_W
SSM_HEADDIM = 64
SSM_HEADS = SSM_W // SSM_HEADDIM
SSM_GROUPS = 2
SSM_STATE = 128
SHORT_CONV = 3
CHUNK = 64
D_FF = ((8 * D_MODEL // 3 + 127) // 128) * 128
FFN_CONV = 3
EPS = 1e-6

GDN_SPLITS = (GDN_HEADS * GDN_DK, GDN_HEADS * GDN_DK, GDN_HEADS * GDN_DV, GDN_W, 2 * GDN_HEADS, 2 * GDN_HEADS)
SSM_SPLITS = (SSM_W, SSM_W, SSM_GROUPS * SSM_STATE, SSM_GROUPS * SSM_STATE, 2 * SSM_HEADS)
IN_DIM = sum(GDN_SPLITS) + sum(SSM_SPLITS)
GDN_CONV_CH = 2 * GDN_HEADS * GDN_DK + GDN_HEADS * GDN_DV
SSM_CONV_CH = SSM_W + 2 * SSM_GROUPS * SSM_STATE


def _split(t, sizes):
    idx = np.cumsum(sizes)[:-1].tolist()
    return jnp.split(t, idx, axis=-1)

def _flip(t):
    return t[:, ::-1]

def rmsnorm(x, g):
    x32 = x.astype(jnp.float32)
    y = x32 * lax.rsqrt(jnp.mean(x32 * x32, axis=-1, keepdims=True) + EPS)
    return (y * g.astype(jnp.float32)).astype(x.dtype)

def l2norm(t):
    t32 = t.astype(jnp.float32)
    return t32 * lax.rsqrt(jnp.sum(t32 * t32, axis=-1, keepdims=True) + EPS)

def modulate(h, shift, scale):
    return h * (1 + scale) + shift

def dwconv1d(u, w, b=None):
    C = u.shape[-1]
    K = w.shape[0]
    out = lax.conv_general_dilated(u, w.reshape(K, 1, C).astype(u.dtype), window_strides=(1,),
                                   padding=((K // 2, K // 2),), dimension_numbers=('NWC', 'WIO', 'NWC'),
                                   feature_group_count=C)
    if b is not None:
        out = out + b
    return out

def dwconv2d_grid(u, w, b):
    Bsz, L, F = u.shape
    rows = L // GRID_W
    img = u.reshape(Bsz, rows, GRID_W, F)
    out = lax.conv_general_dilated(img, w.reshape(FFN_CONV, FFN_CONV, 1, F).astype(u.dtype), window_strides=(1, 1),
                                   padding=((FFN_CONV // 2, FFN_CONV // 2), (FFN_CONV // 2, FFN_CONV // 2)),
                                   dimension_numbers=('NHWC', 'HWIO', 'NHWC'), feature_group_count=F)
    return out.reshape(Bsz, L, F) + b

def gated_delta_chunked(q, k, v, g, beta, S0):
    Bsz, L, H, DK = q.shape
    DV = v.shape[-1]
    NC = L // CHUNK

    def blocks(t):
        t = jnp.moveaxis(t.astype(jnp.float32), 2, 1)
        return t.reshape(Bsz, H, NC, CHUNK, *t.shape[3:])

    q, k, v, g, beta = (blocks(t) for t in (q, k, v, g, beta))
    gc = jnp.cumsum(g, axis=-1)
    pos = jnp.arange(CHUNK)
    lower = pos[:, None] >= pos[None, :]
    decay = jnp.exp(jnp.where(lower, gc[..., :, None] - gc[..., None, :], -jnp.inf))
    kb = k * beta[..., None]
    kk = jnp.einsum('bhnid,bhnjd->bhnij', kb, k) * decay
    rhs = jnp.concatenate([v * beta[..., None], kb * jnp.exp(gc)[..., None]], axis=-1)
    sol = lax.linalg.triangular_solve(kk, rhs, left_side=True, lower=True, unit_diagonal=True)
    u, w = sol[..., :DV], sol[..., DV:]
    qk = jnp.einsum('bhnid,bhnjd->bhnij', q, k) * decay
    q_dec = q * jnp.exp(gc)[..., None]
    k_dec = k * jnp.exp(gc[..., -1:] - gc)[..., None]
    g_last = jnp.exp(gc[..., -1])
    xs = tuple(jnp.moveaxis(t, 2, 0) for t in (u, w, qk, q_dec, k_dec, g_last))

    def step(S, inp):
        u_c, w_c, qk_c, qd_c, kd_c, gl_c = inp
        v_new = u_c - jnp.einsum('bhcd,bhde->bhce', w_c, S)
        o_c = jnp.einsum('bhcd,bhde->bhce', qd_c, S) + jnp.einsum('bhij,bhje->bhie', qk_c, v_new)
        S = S * gl_c[..., None, None] + jnp.einsum('bhcd,bhce->bhde', kd_c, v_new)
        return S, o_c

    S, o = lax.scan(step, S0.astype(jnp.float32), xs)
    o = jnp.moveaxis(o, 0, 2).reshape(Bsz, H, L, DV)
    return jnp.moveaxis(o, 1, 2), S

def ssd_chunked(x, dt, A, Bm, Cm, h0):
    Bsz, L, H, P = x.shape
    G, N = Bm.shape[2], Bm.shape[3]
    R = H // G
    NC = L // CHUNK
    f32 = jnp.float32
    xc = x.astype(f32).reshape(Bsz, NC, CHUNK, G, R, P)
    dtc = dt.astype(f32).reshape(Bsz, NC, CHUNK, G, R)
    Bc = Bm.astype(f32).reshape(Bsz, NC, CHUNK, G, N)
    Cc = Cm.astype(f32).reshape(Bsz, NC, CHUNK, G, N)
    cum = jnp.cumsum(dtc * A.astype(f32).reshape(G, R), axis=2)
    pos = jnp.arange(CHUNK)
    lower = (pos[:, None] >= pos[None, :])[:, :, None, None]
    seg = jnp.exp(jnp.where(lower, cum[:, :, :, None] - cum[:, :, None, :], -jnp.inf))
    cb = jnp.einsum('bnigs,bnjgs->bnijg', Cc, Bc)
    y_diag = jnp.einsum('bnijg,bnijgr,bnjgrp->bnigrp', cb, seg, dtc[..., None] * xc)
    xdt_end = (jnp.exp(cum[:, :, -1:] - cum) * dtc)[..., None] * xc
    states = jnp.einsum('bnjgs,bnjgrp->bngrps', Bc, xdt_end)
    chunk_decay = jnp.exp(cum[:, :, -1])

    def step(h, inp):
        st, dc = inp
        return h * dc[..., None, None] + st, h

    h_fin, h_in = lax.scan(step, h0.astype(f32).reshape(Bsz, G, R, P, N),
                           (jnp.moveaxis(states, 1, 0), jnp.moveaxis(chunk_decay, 1, 0)))
    h_in = jnp.moveaxis(h_in, 0, 1)
    y_off = jnp.einsum('bnigs,bngrps,bnigr->bnigrp', Cc, h_in, jnp.exp(cum))
    y = (y_diag + y_off).reshape(Bsz, L, H, P)
    return y, h_fin.reshape(Bsz, H, P, N)

def token_mixers(h, w_in, gdn_conv_w, gdn_A_log, gdn_dt_bias, gdn_norm_g, ssm_conv_w, ssm_conv_b,
                 ssm_A_log, ssm_dt_bias, ssm_D, ssm_norm_g, states, with_output):
    f32 = jnp.float32
    Bsz, L = h.shape[0], h.shape[1]
    proj = h @ w_in
    q, k, v, z_g, a_g, b_g, z_s, x_s, B_s, C_s, dt_s = _split(proj, GDN_SPLITS + SSM_SPLITS)
    S_gf0, S_gb0, S_sf0, S_sb0 = states

    qkv = jax.nn.silu(dwconv1d(jnp.concatenate([q, k, v], axis=-1), gdn_conv_w))
    q, k, v = _split(qkv, (GDN_HEADS * GDN_DK, GDN_HEADS * GDN_DK, GDN_HEADS * GDN_DV))
    q = l2norm(q.reshape(Bsz, L, GDN_HEADS, GDN_DK)) * (GDN_DK ** -0.5)
    k = l2norm(k.reshape(Bsz, L, GDN_HEADS, GDN_DK))
    v = v.reshape(Bsz, L, GDN_HEADS, GDN_DV)
    a = a_g.reshape(Bsz, L, 2, GDN_HEADS).astype(f32)
    g_log = -jnp.exp(gdn_A_log.astype(f32)) * jax.nn.softplus(a + gdn_dt_bias.astype(f32))
    beta = jax.nn.sigmoid(b_g.reshape(Bsz, L, 2, GDN_HEADS).astype(f32))
    o_f, S_gf = gated_delta_chunked(q, k, v, g_log[:, :, 0], beta[:, :, 0], S_gf0)
    o_b, S_gb = gated_delta_chunked(_flip(q), _flip(k), _flip(v), _flip(g_log[:, :, 1]), _flip(beta[:, :, 1]), S_gb0)

    xBC = jax.nn.silu(dwconv1d(jnp.concatenate([x_s, B_s, C_s], axis=-1), ssm_conv_w, ssm_conv_b))
    xs, Bm, Cm = _split(xBC, (SSM_W, SSM_GROUPS * SSM_STATE, SSM_GROUPS * SSM_STATE))
    xs = xs.reshape(Bsz, L, SSM_HEADS, SSM_HEADDIM)
    Bm = Bm.reshape(Bsz, L, SSM_GROUPS, SSM_STATE)
    Cm = Cm.reshape(Bsz, L, SSM_GROUPS, SSM_STATE)
    dt = jax.nn.softplus(dt_s.reshape(Bsz, L, 2, SSM_HEADS).astype(f32) + ssm_dt_bias.astype(f32))
    A = -jnp.exp(ssm_A_log.astype(f32))
    y_f, S_sf = ssd_chunked(xs, dt[:, :, 0], A[0], Bm, Cm, S_sf0)
    y_b, S_sb = ssd_chunked(_flip(xs), _flip(dt[:, :, 1]), A[1], _flip(Bm), _flip(Cm), S_sb0)
    new_states = (S_gf, S_gb, S_sf, S_sb)
    if not with_output:
        return None, new_states

    o = o_f + _flip(o_b)
    o = rmsnorm(o, gdn_norm_g) * jax.nn.silu(z_g.reshape(Bsz, L, GDN_HEADS, GDN_DV).astype(f32))
    o = o.reshape(Bsz, L, GDN_W)
    y = y_f + _flip(y_b) + ssm_D.astype(f32)[:, None] * xs.astype(f32)
    y = rmsnorm(y.reshape(Bsz, L, SSM_W) * jax.nn.silu(z_s.astype(f32)), ssm_norm_g)
    mix = jnp.concatenate([o, y.astype(f32)], axis=-1).astype(h.dtype)
    return mix, new_states

def conv_glu(h, w_gate, w_up, conv_w, conv_b, w_down, on_grid):
    a = h @ w_gate
    if on_grid:
        a = dwconv2d_grid(a, conv_w, conv_b)
    else:
        a = dwconv1d(a, conv_w[FFN_CONV // 2], conv_b)
    return (jax.nn.silu(a) * (h @ w_up)) @ w_down

def first_inputs(seed: int = 0) -> dict:
    key = jax.random.key(seed)
    ks = jax.random.split(key, 32)
    f32 = jnp.float32

    def nrm(k, shape, scale):
        return jax.random.normal(k, shape, f32) * scale

    def gain(k, shape):
        return 1.0 + 0.05 * jax.random.normal(k, shape, f32)

    def a_log(k, shape):
        return jnp.log(jax.random.uniform(k, shape, f32, 1.0, 16.0))

    def dt_bias(k, shape):
        dtv = jnp.exp(jax.random.uniform(k, shape, f32, math.log(1e-3), math.log(1e-1)))
        return dtv + jnp.log(-jnp.expm1(-dtv))

    return {
        'x': nrm(ks[0], (BATCH, SEQ, D_MODEL), 1.0),
        'c': nrm(ks[1], (BATCH, D_MODEL), 1.0),
        'ctx': nrm(ks[2], (BATCH, CTX_LEN, D_MODEL), 1.0),
        'c_ctx': nrm(ks[3], (D_MODEL,), 1.0),
        'w_ada': nrm(ks[4], (DEPTH, D_MODEL, 6 * D_MODEL), 0.5 * D_MODEL ** -0.5),
        'b_ada': nrm(ks[5], (DEPTH, 6 * D_MODEL), 0.01),
        'norm1_g': gain(ks[6], (DEPTH, D_MODEL)),
        'w_in': nrm(ks[7], (DEPTH, D_MODEL, IN_DIM), D_MODEL ** -0.5),
        'gdn_conv_w': nrm(ks[8], (DEPTH, SHORT_CONV, GDN_CONV_CH), SHORT_CONV ** -0.5),
        'gdn_A_log': a_log(ks[9], (DEPTH, 2, GDN_HEADS)),
        'gdn_dt_bias': dt_bias(ks[10], (DEPTH, 2, GDN_HEADS)),
        'gdn_norm_g': gain(ks[11], (DEPTH, GDN_DV)),
        'ssm_conv_w': nrm(ks[12], (DEPTH, SHORT_CONV, SSM_CONV_CH), SHORT_CONV ** -0.5),
        'ssm_conv_b': nrm(ks[13], (DEPTH, SSM_CONV_CH), 0.02),
        'ssm_A_log': a_log(ks[14], (DEPTH, 2, SSM_HEADS)),
        'ssm_dt_bias': dt_bias(ks[15], (DEPTH, 2, SSM_HEADS)),
        'ssm_D': 1.0 + 0.1 * jax.random.normal(ks[16], (DEPTH, SSM_HEADS), f32),
        'ssm_norm_g': gain(ks[17], (DEPTH, SSM_W)),
        'w_out': nrm(ks[18], (DEPTH, MIX_W, D_MODEL), MIX_W ** -0.5),
        'norm2_g': gain(ks[19], (DEPTH, D_MODEL)),
        'ffn_w_gate': nrm(ks[20], (DEPTH, D_MODEL, D_FF), D_MODEL ** -0.5),
        'ffn_w_up': nrm(ks[21], (DEPTH, D_MODEL, D_FF), D_MODEL ** -0.5),
        'ffn_conv_w': nrm(ks[22], (DEPTH, FFN_CONV, FFN_CONV, D_FF), 1.0 / FFN_CONV),
        'ffn_conv_b': nrm(ks[23], (DEPTH, D_FF), 0.02),
        'ffn_w_down': nrm(ks[24], (DEPTH, D_FF, D_MODEL), D_FF ** -0.5),
        'final_norm_g': gain(ks[25], (D_MODEL,)),
    }

def first_block(x, c, ctx, c_ctx, w_ada, b_ada, norm1_g, w_in, gdn_conv_w, gdn_A_log, gdn_dt_bias, gdn_norm_g,
              ssm_conv_w, ssm_conv_b, ssm_A_log, ssm_dt_bias, ssm_D, ssm_norm_g, w_out, norm2_g,
              ffn_w_gate, ffn_w_up, ffn_conv_w, ffn_conv_b, ffn_w_down, final_norm_g):
    f32 = jnp.float32
    Bsz = x.shape[0]
    for l in range(DEPTH):
        last = l == DEPTH - 1
        mod = jax.nn.silu(c) @ w_ada[l] + b_ada[l]
        mod_c = jax.nn.silu(c_ctx) @ w_ada[l] + b_ada[l]
        sh1, sc1, g1, sh2, sc2, g2 = jnp.split(mod[:, None, :], 6, axis=-1)
        sh1c, sc1c, g1c, sh2c, sc2c, g2c = jnp.split(mod_c, 6, axis=-1)
        mixer_params = (w_in[l], gdn_conv_w[l], gdn_A_log[l], gdn_dt_bias[l], gdn_norm_g[l], ssm_conv_w[l],
                        ssm_conv_b[l], ssm_A_log[l], ssm_dt_bias[l], ssm_D[l], ssm_norm_g[l])
        ffn_params = (ffn_w_gate[l], ffn_w_up[l], ffn_conv_w[l], ffn_conv_b[l], ffn_w_down[l])
        zero_states = (jnp.zeros((Bsz, GDN_HEADS, GDN_DK, GDN_DV), f32),
                       jnp.zeros((Bsz, GDN_HEADS, GDN_DK, GDN_DV), f32),
                       jnp.zeros((Bsz, SSM_HEADS, SSM_HEADDIM, SSM_STATE), f32),
                       jnp.zeros((Bsz, SSM_HEADS, SSM_HEADDIM, SSM_STATE), f32))
        hc = modulate(rmsnorm(ctx, norm1_g[l]), sh1c, sc1c)
        mix_c, ctx_states = token_mixers(hc, *mixer_params, zero_states, not last)
        hx = modulate(rmsnorm(x, norm1_g[l]), sh1, sc1)
        mix_x, _ = token_mixers(hx, *mixer_params, ctx_states, True)
        x = x + g1 * (mix_x @ w_out[l])
        x = x + g2 * conv_glu(modulate(rmsnorm(x, norm2_g[l]), sh2, sc2), *ffn_params, True)
        if not last:
            ctx = ctx + g1c * (mix_c @ w_out[l])
            ctx = ctx + g2c * conv_glu(modulate(rmsnorm(ctx, norm2_g[l]), sh2c, sc2c), *ffn_params, False)
    return rmsnorm(x, final_norm_g)


D_RNN = 1024
RNN_BLOCKS = 8
RNN_BLOCK_W = D_RNN // RNN_BLOCKS
CONV_W = 4
LRU_C = 8.0
N_HEADS = 8
QK_NOPE = 128
QK_ROPE = 64
QK_DIM = QK_NOPE + QK_ROPE
V_DIM = 128
Q_LORA = 256
KV_LORA = 256
ROPE_THETA = 10000.0
Q_BLOCK = 128
N_GROUPS = 8
EXPERTS_PER_GROUP = 8
N_EXPERTS = N_GROUPS * EXPERTS_PER_GROUP
TOP_K = 2
D_EXPERT = 256
MOE_BLOCK = 128

IN_SPLITS = (D_RNN, D_RNN, Q_LORA, KV_LORA, QK_ROPE, D_MODEL, D_MODEL)
D_IN = D_RNN + D_RNN + Q_LORA + KV_LORA + QK_ROPE + D_MODEL + D_MODEL


def rmsnorm_2(x, g):
    xf = x.astype(jnp.float32)
    y = xf * lax.rsqrt(jnp.mean(xf * xf, axis=-1, keepdims=True) + EPS)
    return (y * g.astype(jnp.float32)).astype(x.dtype)

def causal_depthwise_conv(x, w, b):
    y = lax.conv_general_dilated(
        x, w[:, None, :].astype(x.dtype), window_strides=(1,),
        padding=[(CONV_W - 1, 0)], dimension_numbers=("NWC", "WIO", "NWC"),
        feature_group_count=x.shape[-1])
    return y + b.astype(x.dtype)

def rg_lru(x, wa, ba, wx, bx, lam):
    B, S, C = x.shape
    xb = x.reshape(B, S, RNN_BLOCKS, RNN_BLOCK_W)
    r = jax.nn.sigmoid(jnp.einsum("bsnk,nkj->bsnj", xb, wa).reshape(B, S, C) + ba)
    i = jax.nn.sigmoid(jnp.einsum("bsnk,nkj->bsnj", xb, wx).reshape(B, S, C) + bx)
    log_a = -LRU_C * r.astype(jnp.float32) * jax.nn.softplus(-lam.astype(jnp.float32))
    a = jnp.exp(log_a)
    mult = jnp.sqrt(-jnp.expm1(2.0 * log_a))
    b_in = x.astype(jnp.float32) * i.astype(jnp.float32) * mult

    def combine(left, right):
        a1, b1 = left
        a2, b2 = right
        return a1 * a2, a2 * b1 + b2

    _, h = lax.associative_scan(combine, (a, b_in), axis=1)
    return h.astype(x.dtype)

def apply_rope(x, cos, sin):
    half = x.shape[-1] // 2
    x1, x2 = x[..., :half], x[..., half:]
    return jnp.concatenate([x1 * cos - x2 * sin, x2 * cos + x1 * sin], axis=-1)

def mla_attention(c_q, c_kv, k_pe, positions, q_norm_g, w_uq, kv_norm_g, w_ukv,
                  qk_q_g, qk_k_g, w_mla_o):
    B, S, _ = c_q.shape
    q = (rmsnorm_2(c_q, q_norm_g) @ w_uq).reshape(B, S, N_HEADS, QK_DIM)
    kv = (rmsnorm_2(c_kv, kv_norm_g) @ w_ukv).reshape(B, S, N_HEADS, QK_NOPE + V_DIM)
    k_nope, v = kv[..., :QK_NOPE], kv[..., QK_NOPE:]
    k_pe_h = jnp.broadcast_to(k_pe[:, :, None, :], (B, S, N_HEADS, QK_ROPE))
    k = jnp.concatenate([k_nope, k_pe_h], axis=-1)
    q = rmsnorm_2(q, qk_q_g)
    k = rmsnorm_2(k, qk_k_g)
    inv_freq = ROPE_THETA ** (-jnp.arange(0, QK_ROPE, 2, dtype=jnp.float32) / QK_ROPE)
    ang = positions.astype(jnp.float32)[..., None] * inv_freq
    cos = jnp.cos(ang)[:, :, None, :].astype(q.dtype)
    sin = jnp.sin(ang)[:, :, None, :].astype(q.dtype)
    q = jnp.concatenate([q[..., :QK_NOPE], apply_rope(q[..., QK_NOPE:], cos, sin)], axis=-1)
    k = jnp.concatenate([k[..., :QK_NOPE], apply_rope(k[..., QK_NOPE:], cos, sin)], axis=-1)
    scale = QK_DIM ** -0.5
    outs = []
    for s0 in range(0, S, Q_BLOCK):
        e = s0 + Q_BLOCK
        s = jnp.einsum("bqhd,bkhd->bhqk", q[:, s0:e], k[:, :e]).astype(jnp.float32) * scale
        mask = jnp.arange(e)[None, :] <= (s0 + jnp.arange(Q_BLOCK))[:, None]
        p = jax.nn.softmax(jnp.where(mask, s, -jnp.inf), axis=-1).astype(v.dtype)
        outs.append(jnp.einsum("bhqk,bkhd->bqhd", p, v[:, :e]))
    o = jnp.concatenate(outs, axis=1).reshape(B, S, N_HEADS * V_DIM)
    return o @ w_mla_o

def hier_moe(u, wg, bg, we, be, w1, w3, w2):
    B, S, D = u.shape
    N = B * S
    xf = u.reshape(N, D)
    g_logits = (xf @ wg).astype(jnp.float32) + bg.astype(jnp.float32)
    g_prob = jax.nn.softmax(g_logits, axis=-1)
    g_sel = jnp.argmax(g_logits, axis=-1).astype(jnp.int32)
    e_logits = ((xf @ we).astype(jnp.float32) + be.astype(jnp.float32)).reshape(N, N_GROUPS, EXPERTS_PER_GROUP)
    e_in_group = jnp.take_along_axis(e_logits, g_sel[:, None, None], axis=1)[:, 0]
    e_prob = jax.nn.softmax(e_in_group, axis=-1)
    top_p, top_j = lax.top_k(e_prob, TOP_K)
    gate = jnp.take_along_axis(g_prob, g_sel[:, None], axis=1) * top_p / jnp.sum(top_p, axis=-1, keepdims=True)
    expert_id = g_sel[:, None] * EXPERTS_PER_GROUP + top_j.astype(jnp.int32)
    M = N * TOP_K
    flat_e = expert_id.reshape(M)
    flat_tok = jnp.repeat(jnp.arange(N, dtype=jnp.int32), TOP_K)
    flat_w = gate.reshape(M)
    order = jnp.argsort(flat_e)
    sorted_e = flat_e[order]
    counts = jnp.bincount(flat_e, length=N_EXPERTS)
    padded = ((counts + MOE_BLOCK - 1) // MOE_BLOCK) * MOE_BLOCK
    start = jnp.cumsum(counts) - counts
    pad_end = jnp.cumsum(padded)
    pad_start = pad_end - padded
    dest = pad_start[sorted_e] + (jnp.arange(M, dtype=jnp.int32) - start[sorted_e])
    m_pad = M + N_EXPERTS * MOE_BLOCK
    n_blocks = m_pad // MOE_BLOCK
    tok_buf = jnp.full((m_pad,), N, dtype=jnp.int32).at[dest].set(flat_tok[order])
    w_buf = jnp.zeros((m_pad,), dtype=jnp.float32).at[dest].set(flat_w[order])
    block_e = jnp.minimum(
        jnp.searchsorted(pad_end, jnp.arange(n_blocks, dtype=jnp.int32) * MOE_BLOCK, side="right"),
        N_EXPERTS - 1).astype(jnp.int32)
    x_pad = jnp.concatenate([xf, jnp.zeros((1, D), xf.dtype)], axis=0)[tok_buf]
    x_pad = x_pad.reshape(n_blocks, MOE_BLOCK, D)

    def expert_block(args):
        xb, e = args
        h = jax.nn.silu(xb @ w1[e]) * (xb @ w3[e])
        return h @ w2[e]

    y_pad = lax.map(expert_block, (x_pad, block_e)).reshape(m_pad, D)
    y = jax.ops.segment_sum(y_pad * w_buf[:, None].astype(y_pad.dtype), tok_buf, num_segments=N + 1)[:N]
    return y.reshape(B, S, D)

def second_inputs(seed: int = 0) -> dict:
    key = jax.random.key(seed)
    ks = jax.random.split(key, 32)
    L, D, f32 = DEPTH, D_MODEL, jnp.float32

    def nrm(k, shape, fan_in):
        return jax.random.normal(k, shape, f32) * (fan_in ** -0.5)

    def gain(k, shape):
        return 1.0 + 0.1 * jax.random.normal(k, shape, f32)

    def bias(k, shape):
        return 0.01 * jax.random.normal(k, shape, f32)

    x = jax.random.normal(ks[0], (BATCH, SEQ, D), f32)
    offset = jax.random.randint(ks[1], (BATCH, 1), 0, 4096, dtype=jnp.int32)
    positions = offset + jnp.arange(SEQ, dtype=jnp.int32)[None, :]
    a0 = jax.random.uniform(ks[2], (L, D_RNN), f32, 0.9, 0.999)
    s0 = a0 ** (1.0 / LRU_C)
    lru_lambda = jnp.log(s0) - jnp.log1p(-s0)
    return {
        "x": x,
        "positions": positions,
        "norm1_g": gain(ks[3], (L, D)),
        "w_in": nrm(ks[4], (L, D, D_IN), D),
        "conv_w": nrm(ks[5], (L, CONV_W, D_RNN), CONV_W),
        "conv_b": bias(ks[6], (L, D_RNN)),
        "lru_wa": nrm(ks[7], (L, RNN_BLOCKS, RNN_BLOCK_W, RNN_BLOCK_W), RNN_BLOCK_W),
        "lru_ba": bias(ks[8], (L, D_RNN)),
        "lru_wx": nrm(ks[9], (L, RNN_BLOCKS, RNN_BLOCK_W, RNN_BLOCK_W), RNN_BLOCK_W),
        "lru_bx": bias(ks[10], (L, D_RNN)),
        "lru_lambda": lru_lambda,
        "w_rnn_o": nrm(ks[11], (L, D_RNN, D), D_RNN),
        "q_norm_g": gain(ks[12], (L, Q_LORA)),
        "w_uq": nrm(ks[13], (L, Q_LORA, N_HEADS * QK_DIM), Q_LORA),
        "kv_norm_g": gain(ks[14], (L, KV_LORA)),
        "w_ukv": nrm(ks[15], (L, KV_LORA, N_HEADS * (QK_NOPE + V_DIM)), KV_LORA),
        "qk_norm_q_g": gain(ks[16], (L, QK_DIM)),
        "qk_norm_k_g": gain(ks[17], (L, QK_DIM)),
        "w_mla_o": nrm(ks[18], (L, N_HEADS * V_DIM, D), N_HEADS * V_DIM),
        "w_out": nrm(ks[19], (L, D, D), D),
        "norm2_g": gain(ks[20], (L, D)),
        "router_wg": nrm(ks[21], (L, D, N_GROUPS), D),
        "router_bg": bias(ks[22], (L, N_GROUPS)),
        "router_we": nrm(ks[23], (L, D, N_EXPERTS), D),
        "router_be": bias(ks[24], (L, N_EXPERTS)),
        "exp_w1": nrm(ks[25], (L, N_EXPERTS, D, D_EXPERT), D),
        "exp_w3": nrm(ks[26], (L, N_EXPERTS, D, D_EXPERT), D),
        "exp_w2": nrm(ks[27], (L, N_EXPERTS, D_EXPERT, D), D_EXPERT),
    }

def second_block(x, positions, norm1_g, w_in, conv_w, conv_b, lru_wa, lru_ba, lru_wx, lru_bx,
              lru_lambda, w_rnn_o, q_norm_g, w_uq, kv_norm_g, w_ukv, qk_norm_q_g, qk_norm_k_g,
              w_mla_o, w_out, norm2_g, router_wg, router_bg, router_we, router_be,
              exp_w1, exp_w3, exp_w2):
    split_points = [int(p) for p in np.cumsum(IN_SPLITS)[:-1]]
    h = x
    for l in range(DEPTH):
        u = rmsnorm_2(h, norm1_g[l])
        proj = u @ w_in[l]
        x_r, y_r, c_q, c_kv, k_pe, g_a, g_b = jnp.split(proj, split_points, axis=-1)
        x_r = causal_depthwise_conv(x_r, conv_w[l], conv_b[l])
        h_r = rg_lru(x_r, lru_wa[l], lru_ba[l], lru_wx[l], lru_bx[l], lru_lambda[l])
        branch_a = (h_r * jax.nn.gelu(y_r, approximate=True)) @ w_rnn_o[l]
        branch_b = mla_attention(c_q, c_kv, k_pe, positions, q_norm_g[l], w_uq[l], kv_norm_g[l],
                                 w_ukv[l], qk_norm_q_g[l], qk_norm_k_g[l], w_mla_o[l])
        merged = jax.nn.sigmoid(g_a) * branch_a + jax.nn.sigmoid(g_b) * branch_b
        h = h + merged @ w_out[l]
        h = h + hier_moe(rmsnorm_2(h, norm2_g[l]), router_wg[l], router_bg[l], router_we[l],
                         router_be[l], exp_w1[l], exp_w3[l], exp_w2[l])
    return h


def setup_inputs(seed=0):
    out = dict(first_inputs(seed))
    for name, value in second_inputs(seed + 1).items():
        if name != "x":
            out[name + "_2"] = value
    return out


def reference(
    x, c, ctx, c_ctx, w_ada, b_ada, norm1_g, w_in, gdn_conv_w, gdn_A_log, gdn_dt_bias,
    gdn_norm_g, ssm_conv_w, ssm_conv_b, ssm_A_log, ssm_dt_bias, ssm_D, ssm_norm_g, w_out,
    norm2_g, ffn_w_gate, ffn_w_up, ffn_conv_w, ffn_conv_b, ffn_w_down, final_norm_g,
    positions_2, norm1_g_2, w_in_2, conv_w_2, conv_b_2, lru_wa_2, lru_ba_2, lru_wx_2, lru_bx_2,
    lru_lambda_2, w_rnn_o_2, q_norm_g_2, w_uq_2, kv_norm_g_2, w_ukv_2, qk_norm_q_g_2,
    qk_norm_k_g_2, w_mla_o_2, w_out_2, norm2_g_2, router_wg_2, router_bg_2, router_we_2,
    router_be_2, exp_w1_2, exp_w3_2, exp_w2_2,
):
    x = first_block(
        x, c, ctx, c_ctx, w_ada, b_ada, norm1_g, w_in, gdn_conv_w, gdn_A_log, gdn_dt_bias,
        gdn_norm_g, ssm_conv_w, ssm_conv_b, ssm_A_log, ssm_dt_bias, ssm_D, ssm_norm_g, w_out,
        norm2_g, ffn_w_gate, ffn_w_up, ffn_conv_w, ffn_conv_b, ffn_w_down, final_norm_g,
    )
    return second_block(
        x, positions_2, norm1_g_2, w_in_2, conv_w_2, conv_b_2, lru_wa_2, lru_ba_2, lru_wx_2,
        lru_bx_2, lru_lambda_2, w_rnn_o_2, q_norm_g_2, w_uq_2, kv_norm_g_2, w_ukv_2,
        qk_norm_q_g_2, qk_norm_k_g_2, w_mla_o_2, w_out_2, norm2_g_2, router_wg_2, router_bg_2,
        router_we_2, router_be_2, exp_w1_2, exp_w3_2, exp_w2_2,
    )


_drawn_inputs = setup_inputs


def setup_inputs(seed=0):
    import zlib

    import numpy as np

    out = dict(_drawn_inputs(seed))
    spreads = {}
    factors = {'ctx': 3.374,
     'c_ctx': 3.836,
     'gdn_norm_g': 2.763,
     'ssm_conv_b': 3.003,
     'ssm_norm_g': 2.704,
     'ffn_conv_b': 3.46,
     'lru_ba_2': 64.0,
     'lru_bx_2': 38.251,
     'q_norm_g_2': 4.246,
     'kv_norm_g_2': 2.754,
     'qk_norm_q_g_2': 4.05,
     'qk_norm_k_g_2': 4.253,
     'router_bg_2': 18.594,
     'router_be_2': 15.554,
     'conv_b_2': 4.267}
    for name, (base, spread) in spreads.items():
        noise = np.random.default_rng([zlib.crc32(name.encode()), seed]).standard_normal(out[name].shape)
        drawn = base * np.exp(spread * noise) if base else spread * noise
        out[name] = jnp.asarray(drawn.astype(out[name].dtype))
    for name, factor in factors.items():
        out[name] = (out[name] * factor).astype(out[name].dtype)
    return out
```

```python
import numpy as np
from contextlib import ExitStack, contextmanager

import concourse.bass as bass
from concourse import mybir
from concourse.alu_op_type import AluOpType as ALU

F32 = mybir.dt.float32
I32 = mybir.dt.int32
U32 = mybir.dt.uint32
ACT = mybir.ActivationFunctionType
AX = mybir.AxisListType

P = 128
BANK = 512
D = 1024
KT = D // P
SEQ, CTX = 1024, 256
NX, NC = SEQ // P, CTX // P
NT = NX + NC
T = SEQ + CTX
EPS = 1e-6

GH, SH, SG = 4, 8, 2
SP = 64
GW = GH * P
IN_QKV, IN_ZG, IN_AB, IN_ZS, IN_XBC, IN_DT = 0, 1536, 2048, 2064, 2576, 3600
NQKV, NXBC = 12, 8
NCONV = NQKV + NXBC
DFF = 2816
FT = DFF // P
GRID = 64

NH, NOPE, ROPE, DV = 8, 128, 64, 128
QK = NOPE + ROPE
LORA = 256
LT = LORA // P
NG, EPG = 8, 8
NE = NG * EPG
DE = 256
MOE_BLOCKS = 2 * SEQ // P + NE

VEC = {}
_n = 0
for _name, _w in [("c", 8), ("c_ctx", 8), ("b_ada", 48), ("norm1_g", 8), ("norm2_g", 8), ("final_norm_g", 8),
                  ("gdn_conv_w", 36), ("ssm_conv_w", 24), ("ssm_conv_b", 8), ("gdn_norm_g", 1), ("ssm_norm_g", 4),
                  ("ffn_conv_w", 9 * FT), ("ffn_conv_b", FT), ("norm1_g_2", 8), ("conv_w_2", 32), ("conv_b_2", 8),
                  ("lru_ba_2", 8), ("lru_bx_2", 8), ("lru_lambda_2", 8), ("q_norm_g_2", 2), ("kv_norm_g_2", 2),
                  ("q_g_nope", 1), ("q_g_rope", 1), ("k_g_nope", 1), ("k_g_rope", 1), ("norm2_g_2", 8),
                  ("eps", 1), ("inv_freq", 1)]:
    VEC[_name] = (_n, _w)
    _n += _w
NVEC = _n

ROW = {}
_n = 0
for _name, _w in [("gdn_dt_bias", 8), ("ssm_dt_bias", 16), ("gdn_A_log", 8), ("ssm_A_log", 16), ("ssm_D", 8),
                  ("router_b", NG + NE), ("expert_iota", NE), ("block_start", MOE_BLOCKS)]:
    ROW[_name] = (_n, _w)
    _n += _w
NROW = _n

MAT = {n: i for i, n in enumerate(
    ["ident", "ones", "tri0", "tri1", "neg0", "neg1", "before", "rope"] + [f"lvl{d}_{l}" for d in range(2) for l in range(7)])}
NMAT = len(MAT)


class Shared:
    pass


class Chain:

    def __init__(self, eng, sem, base=0):
        self.eng, self.sem, self.base, self.n = eng, sem, base, 0

    def __call__(self, instruction):
        instruction.then_inc(self.sem, 1)
        self.n += 1
        self.eng.wait_ge(self.sem, self.base + self.n)


STAGE_NUMBERS = iter(range(1 << 30))


@contextmanager
def stage(nc, *names):
    number = next(STAGE_NUMBERS)
    sems = [nc.alloc_semaphore(f"{n}_s{number}") for n in names]
    yield sems
    nc.clear_and_free_semaphores(sems)
    nc.all_engine_barrier(sem_only=True)


def chunks_of(total, first=0):
    out = [(0, first)] if first else []
    at = first
    while at < total:
        out.append((at, min(BANK, total - at)))
        at += out[-1][1]
    return out


def load_constants(nc, S, io):
    with stage(nc, "consts_in") as (consts_in,):
        with nc.Block() as block:
            @block.sync
            def _(sp):
                sp.dma_start(S.mat[:, :, :], io["mats"]).then_inc(consts_in, 16)
                sp.dma_start(S.vec[:, :], io["vecs"]).then_inc(consts_in, 16)
                sp.dma_start(S.row[:, :], io["rows"].partition_broadcast(P)).then_inc(consts_in, 16)
                sp.wait_ge(consts_in, 48)


def modulation(nc, S, io):
    GROUP, PAIRS = 4 * P, 6
    with ExitStack() as ctx, stage(nc, "w_in0", "w_in1", "w_used0", "w_used1", "silu_done", "chain") as (
            w_in0, w_in1, w_used0, w_used1, silu_done, chain):
        w_in, w_used = [w_in0, w_in1], [w_used0, w_used1]
        w = [ctx.enter_context(nc.sbuf_tensor(f"ada{b}", [P, KT, GROUP], F32)) for b in range(2)]
        sc = ctx.enter_context(nc.sbuf_tensor("silu_c", [P, KT, 2], F32))
        ps = ctx.enter_context(nc.psum_tensor("ps_mod", [P, 48, 2], F32))
        view = io["w_ada"].rearrange("(k p) m -> p k m", p=P)
        with nc.Block() as block:
            @block.sync
            def _(sp):
                sp.sem_inc(w_used0, 1)
                sp.sem_inc(w_used1, 1)
                with sp.Fori(0, PAIRS) as i:
                    for b in range(2):
                        sp.wait_ge(w_used[b], i + 1)
                        sp.dma_start(w[b][:, :, :], view[:, :, bass.ds((i * 2 + b) * GROUP, GROUP)]).then_inc(w_in[b], 16)

            @block.scalar
            def _(act):
                c0, _w = VEC["c"]
                nc.scalar.activation(sc[:, :, 0], S.vec[:, c0:c0 + KT], ACT.Silu).then_inc(silu_done, 1)
                nc.scalar.activation(sc[:, :, 1], S.vec[:, c0 + KT:c0 + 2 * KT], ACT.Silu).then_inc(silu_done, 1)

            @block.tensor
            def _(pe):
                pe.wait_ge(silu_done, 2)
                with pe.Fori(0, PAIRS) as i:
                    for b in range(2):
                        pe.wait_ge(w_in[b], i * 16 + 16)
                        for m in range(4):
                            for k in range(KT):
                                last = nc.tensor.matmul(ps[:, bass.ds((i * 2 + b) * 4 + m, 1), :],
                                                        w[b][:, k, m * P:(m + 1) * P], sc[:, k, :],
                                                        start=(k == 0), stop=(k == KT - 1))
                        last.then_inc(w_used[b], 1)

            @block.vector
            def _(dve):
                link = Chain(dve, chain)
                b0, _w = VEC["b_ada"]
                dve.wait_ge(w_used1, PAIRS + 1)
                for t in range(2):
                    link(nc.vector.tensor_tensor(S.mod[:, t, :], ps[:, :, t], S.vec[:, b0:b0 + 48], ALU.add))
                for t, at, g, to in ((0, 8, "norm1_g", 0), (1, 8, "norm1_g", 1), (0, 32, "norm2_g", 2)):
                    g0, _w = VEC[g]
                    link(nc.vector.scalar_tensor_tensor(S.fac[:, to, :], S.mod[:, t, at:at + KT], 1.0,
                                                        S.vec[:, g0:g0 + KT], ALU.add, ALU.mult))


def load_transposed(nc, S, io, xT):
    with ExitStack() as ctx, stage(nc, "rows_in0", "rows_in1", "transposed", "evacuated") as (in0, in1, transposed, evacuated):
        rows_in = [in0, in1]
        rows = [ctx.enter_context(nc.sbuf_tensor(f"rows{b}", [P, D], F32)) for b in range(2)]
        ps = [ctx.enter_context(nc.psum_tensor(f"ps_t{b}", [P, KT, P], F32)) for b in range(2)]
        with nc.Block() as block:
            @block.sync
            def _(sp):
                for t in range(NT):
                    if t >= 2:
                        sp.wait_ge(transposed, t - 1)
                    src = io["ctx"][t * P:(t + 1) * P, :] if t < NC else io["x"][(t - NC) * P:(t - NC + 1) * P, :]
                    sp.dma_start(rows[t % 2][:, :], src).then_inc(rows_in[t % 2], 16)

            @block.tensor
            def _(pe):
                for t in range(NT):
                    pe.wait_ge(rows_in[t % 2], 16 * (t // 2 + 1))
                    if t >= 2:
                        pe.wait_ge(evacuated, t - 1)
                    for k in range(KT):
                        last = nc.tensor.transpose(ps[t % 2][:, k, :], rows[t % 2][:, k * P:(k + 1) * P], S.ident)
                    last.then_inc(transposed, 1)

            @block.vector
            def _(dve):
                for t in range(NT):
                    dve.wait_ge(transposed, t + 1)
                    nc.vector.tensor_copy(xT[:, :, t * P:(t + 1) * P], ps[t % 2][:, :, :]).then_inc(evacuated, 1)


def rms_features(nc, S, tag, src, dst, kt, sizes, mul, add=None, divisor=None):
    n_c, w = len(sizes), max(sizes)
    divisor = divisor or kt * P
    e0, _w = VEC["eps"]
    with ExitStack() as ctx, stage(nc, "squared", "sq_used", "rooted", "scaled", "chain") as (
            squared, sq_used, rooted, scaled, chain):
        sq = ctx.enter_context(nc.sbuf_tensor(f"sq_{tag}", [P, 4, w], F32))
        root = ctx.enter_context(nc.sbuf_tensor(f"root_{tag}", [P, 2, w], F32))
        rinv = ctx.enter_context(nc.sbuf_tensor(f"rinv_{tag}", [P, 2, w], F32))
        ps = [ctx.enter_context(nc.psum_tensor(f"ps_{tag}{b}", [P, BANK], F32)) for b in range(2)]
        with nc.Block() as block:
            @block.scalar
            def _(act):
                def root_of(c):
                    act.wait_ge(sq_used, (c + 1) * kt)
                    if c >= 2:
                        act.wait_ge(scaled, c - 1)
                    n = sizes[c]
                    nc.scalar.activation(root[:, c % 2, 0:n], ps[c % 2][:, 0:n], ACT.Sqrt, bias=S.vec[:, e0:e0 + 1],
                                         scale=1.0 / divisor).then_inc(rooted, 1)

                for c, n in enumerate(sizes):
                    for k in range(kt):
                        j = c * kt + k
                        if j >= 4:
                            act.wait_ge(sq_used, j - 3)
                        rows = src(c, k).shape[0]
                        nc.scalar.activation(sq[0:rows, j % 4, 0:n], src(c, k), ACT.Square).then_inc(squared, 1)
                    if c >= 1:
                        root_of(c - 1)
                root_of(n_c - 1)

            @block.tensor
            def _(pe):
                for c, n in enumerate(sizes):
                    if c >= 2:
                        pe.wait_ge(rooted, c - 1)
                    for k in range(kt):
                        j = c * kt + k
                        pe.wait_ge(squared, j + 1)
                        rows = src(c, k).shape[0]
                        last = nc.tensor.matmul(ps[c % 2][:, 0:n], S.ones[0:rows, :], sq[0:rows, j % 4, 0:n], start=(k == 0),
                                                stop=(k == kt - 1))
                        last.then_inc(sq_used, 1)

            @block.vector
            def _(dve):
                link = Chain(dve, chain)
                for c, n in enumerate(sizes):
                    dve.wait_ge(rooted, c + 1)
                    link(nc.vector.reciprocal(rinv[:, c % 2, 0:n], root[:, c % 2, 0:n]))
                    for k in range(kt):
                        last = nc.vector.scalar_tensor_tensor(dst(c, k), src(c, k), mul(c, k),
                                                              rinv[0:dst(c, k).shape[0], c % 2, 0:n], ALU.mult, ALU.mult)
                        if k == kt - 1 and add is not None:
                            link(last)
                    if add is not None:
                        for k in range(kt):
                            last = nc.vector.tensor_scalar(dst(c, k), dst(c, k), add(c, k), None,
                                                           ALU.add)
                    last.then_inc(scaled, 1)


def load_weights(nc, sp, iters, unroll, w, w_in, tile_done, view):
    sp.sem_inc(tile_done, len(w))
    with sp.Fori(0, iters) as i:
        for b in range(unroll):
            sp.wait_ge(tile_done, i * unroll + b + 1)
            sp.dma_start(w[b % len(w)][:, :, :], view(i, b)).then_inc(w_in[b % len(w)], 16)


def multiply_tiles(nc, pe, iters, unroll, w, w_in, tile_done, src, chunks, ps, ps_free):
    turns = unroll // len(w)
    pe.sem_inc(ps_free, len(ps))
    with pe.Fori(0, iters) as i:
        for b in range(unroll):
            pe.wait_ge(w_in[b % len(w)], (i * turns + b // len(w)) * 16 + 16)
            pe.wait_ge(ps_free, i * unroll + b + 1)
            kt = w[0].shape[1]
            for c, (at, n) in enumerate(chunks):
                for k in range(kt):
                    last = nc.tensor.matmul(ps[b % len(ps)][:, c, 0:n], w[b % len(w)][:, k, :], src(b)[:, k, at:at + n],
                                            start=(k == 0), stop=(k == kt - 1))
            last.then_inc(tile_done, 1)


def linear_stage_buffers(nc, ctx, tag, kt, n_buf, banks, sets=2):
    w = [ctx.enter_context(nc.sbuf_tensor(f"w_{tag}{b}", [P, kt, P], F32)) for b in range(n_buf)]
    ps = [ctx.enter_context(nc.psum_tensor(f"ps_{tag}{b}", [P, banks, BANK], F32)) for b in range(sets)]
    return w, ps


def feature_tiles(w_dram):
    return w_dram.rearrange("(k p) m -> p k m", p=P)


def conv_projection(nc, S, tag, w_dram, n_tiles, hT, convT, first, cw, cb):
    n_buf, iters = 4, n_tiles // 4
    chunks = chunks_of(T, CTX)
    pads = [1, 2, 2]
    W2 = T + 3
    with ExitStack() as ctx, stage(nc, *[f"w_in{b}" for b in range(4)],
                                   "ps_free", "tile_done", "convolved", "activated", "chain", "zeroed") as sems:
        w_in = sems[0:4]
        ps_free, tile_done, convolved, activated, chain, zeroed = sems[4:]
        w, ps = linear_stage_buffers(nc, ctx, tag, KT, n_buf, 3)
        raw = ctx.enter_context(nc.sbuf_tensor(f"raw_{tag}", [P, 2, W2], F32))
        con = ctx.enter_context(nc.sbuf_tensor(f"con_{tag}", [P, 2, W2], F32))
        with nc.Block() as block:
            @block.sync
            def _(sp):
                load_weights(nc, sp, iters, n_buf, w, w_in, tile_done,
                             lambda i, b: feature_tiles(w_dram)[:, :, bass.ds((i * n_buf + b) * P, P)])

            @block.tensor
            def _(pe):
                multiply_tiles(nc, pe, iters, n_buf, w, w_in, tile_done, lambda b: hT, chunks, ps, ps_free)

            @block.scalar
            def _(act):
                act.wait_ge(zeroed, 1)
                for m in range(n_tiles + 1):
                    if m < n_tiles:
                        act.wait_ge(tile_done, n_buf + m + 1)
                        if m >= 2:
                            act.wait_ge(convolved, m - 1)
                        for c, (at, n) in enumerate(chunks):
                            last = nc.scalar.activation(raw[:, m % 2, at + pads[c]:at + pads[c] + n],
                                                        ps[m % 2][:, c, 0:n], ACT.Copy)
                        last.then_inc(ps_free, 1)
                    if m >= 1:
                        j = m - 1
                        act.wait_ge(convolved, j + 1)
                        bias = 0.0 if cb is None else S.vec[:, cb + j:cb + j + 1]
                        nc.scalar.activation(convT[:, first + j, 0:CTX], con[:, j % 2, 1:1 + CTX], ACT.Silu, bias=bias)
                        nc.scalar.activation(convT[:, first + j, CTX:T], con[:, j % 2, CTX + 2:T + 2], ACT.Silu,
                                             bias=bias).then_inc(activated, 1)

            @block.vector
            def _(dve):
                link = Chain(dve, chain)
                link(nc.vector.memset(raw[:, :, :], 0.0))
                dve.sem_inc(zeroed, 1)
                for m in range(n_tiles):
                    dve.wait_ge(ps_free, m + 3)
                    if m >= 2:
                        dve.wait_ge(activated, m - 1)
                    row, out = raw[:, m % 2, :], con[:, m % 2, 1:W2 - 1]
                    tap = lambda j: S.vec[:, cw + j * n_tiles + m:cw + j * n_tiles + m + 1]
                    link(nc.vector.tensor_scalar(out, row[:, 1:W2 - 1], tap(1), None, ALU.mult))
                    link(nc.vector.scalar_tensor_tensor(out, row[:, 0:W2 - 2], tap(0), out, ALU.mult, ALU.add))
                    nc.vector.scalar_tensor_tensor(out, row[:, 2:W2], tap(2), out, ALU.mult, ALU.add).then_inc(convolved, 1)
C_G, C_DA, C_BETA, C_DT, NSMALL = 0, 4, 12, 16, 24
N_FEAT = 12
N_TOK = 14
TOK_W = N_TOK * P + 2 * NSMALL
SLOTS = NT + NC
STEPS = NT


def over(ap, shape):
    return ap.unsqueeze(2).to_broadcast(shape)


def under(ap, n, m):
    return ap.unsqueeze(1).to_broadcast([P, n, m])


def token_projections(nc, S, io, hT, small):
    with ExitStack() as ctx, stage(nc, "w_loaded", "z_full", "z_active", "z_stored0", "z_stored1", "small_full",
                                   "act_done", "chain") as (
            w_loaded, z_full, z_active, st0, st1, small_full, act_done, chain):
        stored = [st0, st1]
        wz = ctx.enter_context(nc.sbuf_tensor("w_z", [P, KT, 2 * GW], F32))
        ws = ctx.enter_context(nc.sbuf_tensor("w_small", [P, KT, 32], F32))
        zt = ctx.enter_context(nc.sbuf_tensor("z_rows", [P, 2, 2 * GW], F32))
        t = {n: ctx.enter_context(nc.sbuf_tensor(f"sp_{n}", [P, NT, 2, 12], F32)) for n in ("u", "m", "e", "q", "z", "z2", "p")}
        neg_a = ctx.enter_context(nc.sbuf_tensor("neg_a", [P, 2, 12], F32))
        ps = [ctx.enter_context(nc.psum_tensor(f"ps_z{b}", [P, 2, BANK], F32)) for b in range(2)]
        pss = ctx.enter_context(nc.psum_tensor("ps_small", [P, NT, 32], F32))
        flat = lambda n: t[n][:, :, :, :].rearrange("p t d h -> p (t d h)")
        with nc.Block() as block:
            @block.sync
            def _(sp):
                w_in = io["w_in"].rearrange("(k p) m -> p k m", p=P)
                sp.dma_start(ws[:, :, :], io["w_small"].rearrange("(k p) m -> p k m", p=P)).then_inc(w_loaded, 16)
                sp.dma_start(wz[:, :, 0:GW], w_in[:, :, IN_ZG:IN_ZG + GW]).then_inc(w_loaded, 16)
                sp.dma_start(wz[:, :, GW:2 * GW], w_in[:, :, IN_ZS:IN_ZS + GW]).then_inc(w_loaded, 16)
                for n in range(NX):
                    sp.wait_ge(z_active, n + 1)
                    sp.dma_start(S.z_dram[n], zt[:, n % 2, :]).then_inc(stored[n % 2], 16)
                sp.wait_ge(st0, 16 * NX // 2)
                sp.wait_ge(st1, 16 * NX // 2)

            @block.tensor
            def _(pe):
                pe.wait_ge(w_loaded, 48)
                for n in range(NT):
                    for k in range(KT):
                        last = nc.tensor.matmul(pss[:, n, :], hT[:, k, n * P:(n + 1) * P], ws[:, k, :],
                                                start=(k == 0), stop=(k == KT - 1))
                last.then_inc(small_full, 1)
                for n in range(NX):
                    if n >= 2:
                        pe.wait_ge(z_active, n - 1)
                    for g in range(2):
                        for k in range(KT):
                            last = nc.tensor.matmul(ps[n % 2][:, g, :], hT[:, k, (NC + n) * P:(NC + n + 1) * P],
                                                    wz[:, k, g * GW:(g + 1) * GW], start=(k == 0), stop=(k == KT - 1))
                    last.then_inc(z_full, 1)

            @block.scalar
            def _(act):
                act.wait_ge(chain, 4)
                nc.scalar.activation(flat("e"), flat("e"), ACT.Exp).then_inc(act_done, 1)
                r0, _w = ROW["gdn_A_log"]
                r1, _w = ROW["ssm_A_log"]
                nc.scalar.activation(neg_a[:, :, 0:GH], S.row[:, r0:r0 + 8].rearrange("p (d h) -> p d h", d=2), ACT.Exp)
                nc.scalar.activation(neg_a[:, :, GH:12], S.row[:, r1:r1 + 16].rearrange("p (d h) -> p d h", d=2),
                                     ACT.Exp).then_inc(act_done, 1)
                for d in range(2):
                    last = nc.scalar.activation(small[:, :, d, C_BETA:C_BETA + GH], pss[:, :, 8 + 4 * d:12 + 4 * d], ACT.Sigmoid)
                last.then_inc(act_done, 1)
                for n in range(NX):
                    act.wait_ge(z_full, n + 1)
                    if n >= 2:
                        act.wait_ge(stored[n % 2], 16 * (n // 2))
                    nc.scalar.activation(zt[:, n % 2, :].rearrange("p (g c) -> p g c", g=2), ps[n % 2][:, :, :],
                                         ACT.Silu).then_inc(z_active, 1)

            @block.vector
            def _(dve):
                link = Chain(dve, chain)
                dve.wait_ge(small_full, 1)
                r0, _w = ROW["gdn_dt_bias"]
                r1, _w = ROW["ssm_dt_bias"]
                for d in range(2):
                    nc.vector.tensor_tensor(t["u"][:, :, d, 0:GH], pss[:, :, 4 * d:4 * d + 4],
                                            under(S.row[:, r0 + 4 * d:r0 + 4 * d + 4], NT, GH), ALU.add)
                    last = nc.vector.tensor_tensor(t["u"][:, :, d, GH:12], pss[:, :, 16 + 8 * d:24 + 8 * d],
                                                   under(S.row[:, r1 + 8 * d:r1 + 8 * d + 8], NT, SH), ALU.add)
                    link(last)
                link(nc.vector.tensor_scalar(flat("m"), flat("u"), 0.0, None, ALU.max))
                link(nc.vector.scalar_tensor_tensor(flat("e"), flat("m"), -2.0, flat("u"), ALU.mult, ALU.add))
                dve.wait_ge(act_done, 3)
                log1p_series(nc, link, flat)
                link(nc.vector.scalar_tensor_tensor(flat("u"), flat("z2"), 2.0, flat("m"), ALU.mult, ALU.add))
                for d in range(2):
                    nc.vector.tensor_copy(small[:, :, d, C_DT:C_DT + SH], t["u"][:, :, d, GH:12])
                    link(nc.vector.scalar_tensor_tensor(small[:, :, d, 0:12], t["u"][:, :, d, :], -1.0,
                                                        under(neg_a[:, d, :], NT, 12), ALU.mult, ALU.mult))


def log1p_series(nc, link, flat):
    link(nc.vector.tensor_scalar(flat("q"), flat("e"), 2.0, None, ALU.add))
    link(nc.vector.reciprocal(flat("q"), flat("q")))
    link(nc.vector.tensor_tensor(flat("z"), flat("e"), flat("q"), ALU.mult))
    link(nc.vector.tensor_tensor(flat("z2"), flat("z"), flat("z"), ALU.mult))
    link(nc.vector.tensor_scalar(flat("p"), flat("z2"), 1.0 / 15, None, ALU.mult))
    for c in (13, 11, 9, 7, 5, 3):
        link(nc.vector.scalar_tensor_tensor(flat("p"), flat("p"), 1.0 / c, flat("z2"), ALU.add, ALU.mult))
    link(nc.vector.scalar_tensor_tensor(flat("z2"), flat("p"), 1.0, flat("z"), ALU.add, ALU.mult))


def pack_tiles(nc, S, convT, small):
    with ExitStack() as ctx, stage(nc, "transposed", "evacuated", "stored0", "stored1", "feat_stored") as (
            transposed, evacuated, st0, st1, feat_stored):
        stored = [st0, st1]
        ps = [ctx.enter_context(nc.psum_tensor(f"ps_pk{b}", [P, 16, P], F32)) for b in range(2)]
        tok = ctx.enter_context(nc.sbuf_tensor("tok", [P, 2, TOK_W], F32))
        copies = [[t] + ([NT + t] if t < NC else []) for t in range(NT)]
        count = [[16 * sum(len(copies[u]) for u in range(t % 2, t + 1, 2)) for t in range(NT)][t] for t in range(NT)]
        n_feat = 2 * sum(len(c) for c in copies)
        with nc.Block() as block:
            @block.sync
            def _(sp):
                for t in range(NT):
                    for slot in copies[t]:
                        cols = slice(t * P, (t + 1) * P)
                        feat = S.feat_dram[slot].rearrange("p (n c) -> p n c", c=P)
                        sp.dma_start(feat[:, 0:8, :], convT[:, 0:8, cols]).then_inc(feat_stored, 16)
                        sp.dma_start(feat[:, 8:12, :], convT[:, 16:20, cols]).then_inc(feat_stored, 16)
                for t in range(NT):
                    sp.wait_ge(evacuated, t + 1)
                    for slot in copies[t]:
                        sp.dma_start(S.tok_dram[slot], tok[:, t % 2, :]).then_inc(stored[t % 2], 16)
                sp.wait_ge(st0, count[NT - 2])
                sp.wait_ge(st1, count[NT - 1])
                sp.wait_ge(feat_stored, 16 * n_feat)

            @block.tensor
            def _(pe):
                for t in range(NT):
                    if t >= 2:
                        pe.wait_ge(evacuated, t - 1)
                    for n in range(N_TOK):
                        last = nc.tensor.transpose(ps[t % 2][:, n, :], convT[:, 4 + n, t * P:(t + 1) * P], S.ident)
                    last.then_inc(transposed, 1)

            @block.vector
            def _(dve):
                for t in range(NT):
                    dve.wait_ge(transposed, t + 1)
                    if t >= 2:
                        dve.wait_ge(stored[t % 2], count[t - 2])
                    nc.vector.tensor_copy(tok[:, t % 2, 0:N_TOK * P].rearrange("p (n c) -> p n c", c=P),
                                          ps[t % 2][:, 0:N_TOK, :])
                    nc.vector.tensor_copy(tok[:, t % 2, N_TOK * P:TOK_W],
                                          small[:, t, :, :].rearrange("p d c -> p (d c)")).then_inc(evacuated, 1)


DIRECTION_SEMS = ["rows_done", "cols_done", "decay_done", "ecols_done", "pool_done", "prods_done", "ant_done", "r_done",
                  "p_done", "pm_done", "xx_done", "x_done", "v_done", "vnew_done", "out_done", "state_done", "off_done",
                  "step_done", "loaded0", "loaded1"]


class DirectionSems:

    def __init__(self, sems):
        (self.rows_done, self.cols_done, self.decay_done, self.ecols_done, self.pool_done, self.prods_done, self.ant_done,
         self.r_done, self.p_done, self.pm_done, self.xx_done, self.x_done, self.v_done, self.vnew_done, self.out_done,
         self.state_done, self.off_done, self.step_done, self.loaded0, self.loaded1) = sems


class DirectionBuffers:

    def __init__(self, tile, d):
        self.cols = tile(f"cols{d}", 36)
        self.ecols = tile(f"ecols{d}", 36)
        self.ncol = tile(f"ncol{d}", 12)
        self.nbeta, self.edb = tile(f"nbeta{d}", 4), tile(f"edb{d}", 4)
        self.DT = tile(f"DT{d}", 12 * P)
        self.ANT = tile(f"ANT{d}", GW)
        self.QKT = tile(f"QKT{d}", GW)
        self.X, self.XT, self.Pm = tile(f"X{d}", GW), tile(f"XT{d}", GW), tile(f"Pm{d}", GW)
        self.WT = tile(f"WT{d}", 2 * GW)
        self.R, self.vnew, self.kd = tile(f"R{d}", GW), tile(f"vnew{d}", GW), tile(f"kd{d}", GW)
        self.xdt, self.xde = tile(f"xdt{d}", GW), tile(f"xde{d}", GW)
        self.S, self.H = tile(f"S{d}", GW), tile(f"H{d}", GW)
        self.tmp = tile(f"tmp{d}", GW)


def recurrences(nc, S, acc):
    names = DIRECTION_SEMS
    N_LINKS = 28
    with ExitStack() as ctx, stage(nc, *[f"{n}_{d}" for d in range(2) for n in names], "chain", "zeroed", "pchain") as sems:
        sem = [DirectionSems(sems[d * len(names):(d + 1) * len(names)]) for d in range(2)]
        chain, zeroed, pchain = sems[2 * len(names):]
        tile = lambda n, cols: ctx.enter_context(nc.sbuf_tensor(n, [P, cols], F32))
        feat = [[tile(f"feat{j}{d}", N_FEAT * P) for d in range(2)] for j in range(2)]
        tok = [[tile(f"tokp{j}{d}", TOK_W) for d in range(2)] for j in range(2)]
        buf = [DirectionBuffers(tile, d) for d in range(2)]
        bank = [[ctx.enter_context(nc.psum_tensor(f"bk{d}{b}", [P, BANK], F32)) for b in range(4)] for d in range(2)]
        tri = [S.mat[:, MAT[f"tri{d}"], :] for d in range(2)]
        neg = [S.mat[:, MAT[f"neg{d}"], :] for d in range(2)]
        lvl = [[S.mat[:, MAT[f"lvl{d}_{l}"], :] for l in range(7)] for d in range(2)]
        heads = lambda ap: ap.rearrange("p (h c) -> p h c", c=P)
        h64 = lambda ap: ap.rearrange("p (h c) -> p h c", c=SP)
        q = lambda j, d, h: feat[j][d][:, h * P:(h + 1) * P]
        k = lambda j, d, h: feat[j][d][:, (4 + h) * P:(5 + h) * P]
        bT = lambda j, d, g: feat[j][d][:, (8 + g) * P:(9 + g) * P]
        cT = lambda j, d, g: feat[j][d][:, (10 + g) * P:(11 + g) * P]
        k_tok = lambda j, d: tok[j][d][:, 0:GW]
        v_tok = lambda j, d: tok[j][d][:, GW:2 * GW]
        x_tok = lambda j, d: tok[j][d][:, 2 * GW:3 * GW]
        b_tok = lambda j, d, g: tok[j][d][:, 3 * GW + g * P:3 * GW + (g + 1) * P]
        num = lambda j, d, at, n: tok[j][d][:, N_TOK * P + d * NSMALL + at:N_TOK * P + d * NSMALL + at + n]
        hd = lambda ap, h: ap[:, h * P:(h + 1) * P]
        DIRS = range(2)
        with nc.Block() as block:
            @block.sync
            def _(sp):
                for d in DIRS:
                    sp.sem_inc(sem[d].step_done, 2)
                with sp.Fori(0, STEPS // 2) as i:
                    back = [sp.snap(i * -2 + (SLOTS - 1 - j)) for j in range(2)]
                    for j in range(2):
                        for d in DIRS:
                            sp.wait_ge(sem[d].step_done, 2 * i + j + 1)
                            slot = 2 * i + j if d == 0 else back[j]
                            loaded = sem[d].loaded0 if j == 0 else sem[d].loaded1
                            sp.dma_start(feat[j][d][:, :], S.feat_dram[bass.ds(slot, 1), :, :].rearrange(
                                "o p c -> (o p) c")).then_inc(loaded, 16)
                            sp.dma_start(tok[j][d][:, :], S.tok_dram[bass.ds(slot, 1), :, :].rearrange(
                                "o p c -> (o p) c")).then_inc(loaded, 16)

            @block.tensor
            def _(pe):
                mm = nc.tensor.matmul
                pe.wait_ge(zeroed, 1)
                with pe.Fori(0, STEPS // 2) as i:
                    for j in range(2):
                        s = 2 * i + j
                        for d in DIRS:
                            pe.wait_ge(sem[d].loaded0 if j == 0 else sem[d].loaded1, 32 * i + 32)
                            pe.wait_ge(sem[d].step_done, s + 2)
                            for b in range(3):
                                mm(heads(bank[d][b][:, :]), S.ident, under(neg[d], 4, P), start=True, stop=False)
                                for h in range(4):
                                    mm(hd(bank[d][b], h), num(j, d, 4 * b + h, 1).to_broadcast([P, P]), tri[d],
                                       start=False, stop=(h == 3))
                            mm(bank[d][3][:, 0:12], tri[d], num(j, d, 0, 12), start=True, stop=True)
                            mm(bank[d][3][:, 12:24], S.ones, num(j, d, 0, 12), start=True, stop=True).then_inc(sem[d].rows_done, 1)
                        for d in DIRS:
                            pe.wait_ge(sem[d].decay_done, s + 1)
                            for h in range(GH):
                                mm(hd(bank[d][0], h), k(j, d, h), k(j, d, h), start=True, stop=True)
                                mm(hd(bank[d][1], h), k(j, d, h), q(j, d, h), start=True, stop=True)
                            for g in range(SG):
                                mm(hd(bank[d][2], g), bT(j, d, g), cT(j, d, g), start=True, stop=True)
                            pe.wait_ge(sem[d].cols_done, s + 1)
                            for h in range(GH):
                                last = mm(hd(bank[d][3], h), k(j, d, h), hd(buf[d].S, h), start=True, stop=True)
                            last.then_inc(sem[d].prods_done, 1)
                        for level in range(7):
                            for d in DIRS:
                                if level == 0:
                                    pe.wait_ge(sem[d].ant_done, s + 1)
                                else:
                                    pe.wait_ge(sem[d].x_done, s * 7 + level)
                                for h in range(GH):
                                    last = mm(hd(bank[d][0], h), hd(buf[d].ANT, h),
                                              S.ident if level == 0 else hd(buf[d].X, h), start=True, stop=True)
                                last.then_inc(sem[d].p_done, 1)
                            for d in DIRS:
                                pe.wait_ge(sem[d].pm_done, s * 7 + level + 1)
                                for h in range(GH):
                                    if 0 < level < 6:
                                        mm(hd(bank[d][1], h), hd(buf[d].XT, h), hd(buf[d].Pm, h), start=True, stop=True)
                                    last = mm(hd(bank[d][2], h), hd(buf[d].Pm, h),
                                              S.ident if level == 0 else hd(buf[d].XT, h), start=True, stop=True)
                                last.then_inc(sem[d].xx_done, 1)
                        for d in DIRS:
                            pe.wait_ge(sem[d].x_done, s * 7 + 7)
                            pe.wait_ge(sem[d].r_done, s + 1)
                            for h in range(GH):
                                last = mm(hd(bank[d][0], h), hd(buf[d].XT, h), hd(buf[d].R, h), start=True, stop=True)
                            last.then_inc(sem[d].v_done, 1)
                        for d in DIRS:
                            pe.wait_ge(sem[d].vnew_done, s + 1)
                            pe.wait_ge(sem[d].pool_done, 5 * s + 5)
                            for h in range(GH):
                                mm(hd(bank[d][1], h), hd(buf[d].QKT, h), hd(buf[d].vnew, h), start=True, stop=True)
                                mm(hd(bank[d][2], h), hd(buf[d].kd, h), hd(buf[d].vnew, h), start=True, stop=True)
                                mm(hd(bank[d][3], h), q(j, d, h), hd(buf[d].S, h), start=True, stop=True)
                            for h in range(SH):
                                last = mm(bank[d][0][:, h * SP:(h + 1) * SP], hd(buf[d].WT, h),
                                          buf[d].xdt[:, h * SP:(h + 1) * SP], start=True, stop=True)
                            last.then_inc(sem[d].out_done, 1)
                        for d in DIRS:
                            pe.wait_ge(sem[d].state_done, s + 1)
                            for g in range(SG):
                                half = slice(g * 256, (g + 1) * 256)
                                mm(bank[d][1][:, half], cT(j, d, g), buf[d].H[:, half], start=True, stop=True)
                                last = mm(bank[d][2][:, half], b_tok(j, d, g), buf[d].xde[:, half], start=True, stop=True)
                            last.then_inc(sem[d].off_done, 1)

            @block.scalar
            def _(act):
                with act.Fori(0, STEPS // 2) as i:
                    for j in range(2):
                        s = 2 * i + j
                        for d in DIRS:
                            act.wait_ge(sem[d].cols_done, s + 1)
                            for h in range(12):
                                last = nc.scalar.activation(hd(buf[d].DT, h), hd(bank[d][h // 4], h % 4), ACT.Exp,
                                                            bias=buf[d].ncol[:, h:h + 1])
                            last.then_inc(sem[d].decay_done, 1)
                            nc.scalar.activation(buf[d].ecols[:, :], buf[d].cols[:, :], ACT.Exp).then_inc(sem[d].ecols_done, 1)
                        for d in DIRS:
                            act.wait_ge(sem[d].v_done, s + 1)
                            nc.scalar.activation(buf[d].vnew[:, :], bank[d][0][:, :], ACT.Copy).then_inc(sem[d].vnew_done, 1)

            @block.gpsimd
            def _(pool):
                with pool.Fori(0, STEPS // 2) as i:
                    for j in range(2):
                        s = 2 * i + j
                        for d in DIRS:
                            B = buf[d]
                            pool.wait_ge(sem[d].rows_done, s + 1)
                            mul = lambda out, a, b: nc.gpsimd.tensor_tensor(out, a, b, ALU.mult)
                            mul(h64(B.xdt[:, :]), h64(x_tok(j, d)), over(num(j, d, C_DT, 8), [P, 8, SP])).then_inc(sem[d].pool_done, 1)
                            nc.gpsimd.tensor_scalar(B.nbeta[:, :], num(j, d, C_BETA, 4), -1.0, None, ALU.mult).then_inc(sem[d].pool_done, 1)
                            pool.wait_ge(sem[d].ecols_done, s + 1)
                            mul(B.edb[:, :], num(j, d, C_BETA, 4), B.ecols[:, 24:28]).then_inc(sem[d].pool_done, 1)
                            pool.wait_ge(sem[d].pool_done, 5 * s + 3)
                            mul(heads(B.kd[:, :]), heads(k_tok(j, d)), over(B.edb[:, :], [P, 4, P])).then_inc(sem[d].pool_done, 1)
                            mul(h64(B.xde[:, :]), h64(B.xdt[:, :]), over(B.ecols[:, 28:36], [P, 8, SP])).then_inc(sem[d].pool_done, 1)

            @block.vector
            def _(dve):
                tt, stt = nc.vector.tensor_tensor, nc.vector.scalar_tensor_tensor
                for d in DIRS:
                    nc.vector.memset(buf[d].S[:, :], 0.0)
                    nc.vector.memset(buf[d].H[:, :], 0.0)
                nc.vector.memset(acc[:, :, :], 0.0).then_inc(zeroed, 1)
                dve.wait_ge(zeroed, 1)
                with dve.Fori(0, STEPS // 2) as i:
                    link = Chain(dve, chain, i * N_LINKS)
                    back = [dve.snap(i * -2 + (SLOTS - 1 - j)) for j in range(2)]
                    for j in range(2):
                        s = 2 * i + j
                        for d in DIRS:
                            B = buf[d]
                            dve.wait_ge(sem[d].rows_done, s + 1)
                            link(nc.vector.tensor_copy(B.cols[:, 0:24], bank[d][3][:, 0:24]))
                            link(nc.vector.tensor_scalar(B.ncol[:, :], B.cols[:, 0:12], -1.0, None, ALU.mult))
                            tt(B.cols[:, 24:36], B.cols[:, 12:24], B.ncol[:, :], ALU.add).then_inc(sem[d].cols_done, 1)
                        for d in DIRS:
                            B = buf[d]
                            dve.wait_ge(sem[d].prods_done, s + 1)
                            dve.wait_ge(sem[d].pool_done, 5 * s + 2)
                            for h in range(GH):
                                last = stt(hd(B.ANT, h), hd(bank[d][0], h), B.nbeta[:, h:h + 1], hd(B.DT, h), ALU.mult, ALU.mult)
                            last.then_inc(sem[d].ant_done, 1)
                            for h in range(GH):
                                stt(hd(B.QKT, h), hd(bank[d][1], h), num(j, d, C_BETA + h, 1), hd(B.DT, h), ALU.mult, ALU.mult)
                            for g in range(SG):
                                tt(heads(B.WT[:, g * GW:(g + 1) * GW]), under(hd(bank[d][2], g), 4, P),
                                   heads(B.DT[:, (1 + g) * GW:(2 + g) * GW]), ALU.mult)
                            dve.wait_ge(sem[d].ecols_done, s + 1)
                            link(tt(heads(B.tmp[:, :]), heads(bank[d][3][:, :]), over(B.ecols[:, 0:4], [P, 4, P]), ALU.mult))
                            tt(B.R[:, :], v_tok(j, d), B.tmp[:, :], ALU.subtract).then_inc(sem[d].r_done, 1)
                        for level in range(7):
                            for d in DIRS:
                                B = buf[d]
                                dve.wait_ge(sem[d].p_done, s * 7 + level + 1)
                                tt(heads(B.Pm[:, :]), heads(bank[d][0][:, :]), under(lvl[d][level], 4, P),
                                   ALU.mult).then_inc(sem[d].pm_done, 1)
                            for d in DIRS:
                                B = buf[d]
                                if level == 0:
                                    dve.wait_ge(sem[d].pm_done, s * 7 + level + 1)
                                    tt(heads(B.X[:, :]), heads(B.Pm[:, :]), under(S.ident, 4, P), ALU.add)
                                dve.wait_ge(sem[d].xx_done, s * 7 + level + 1)
                                if level == 0:
                                    tt(heads(B.XT[:, :]), heads(bank[d][2][:, :]), under(S.ident, 4, P),
                                       ALU.add).then_inc(sem[d].x_done, 1)
                                else:
                                    if level < 6:
                                        tt(B.X[:, :], B.X[:, :], bank[d][1][:, :], ALU.add)
                                    tt(B.XT[:, :], B.XT[:, :], bank[d][2][:, :], ALU.add).then_inc(sem[d].x_done, 1)
                        slots = [s, back[j]]
                        out_o = [acc[:, bass.ds(at, 1), 0:GW].rearrange("p o c -> p (o c)") for at in slots]
                        out_y = [acc[:, bass.ds(at, 1), GW:2 * GW].rearrange("p o c -> p (o c)") for at in slots]
                        for d in DIRS:
                            B = buf[d]
                            dve.wait_ge(sem[d].out_done, s + 1)
                            link(tt(out_o[d], out_o[d], bank[d][1][:, :], ALU.add))
                            tt(heads(B.tmp[:, :]), heads(bank[d][3][:, :]), over(B.ecols[:, 0:4], [P, 4, P]), ALU.mult)
                            link(tt(heads(B.S[:, :]), heads(B.S[:, :]), over(B.ecols[:, 12:16], [P, 4, P]), ALU.mult))
                            tt(B.S[:, :], B.S[:, :], bank[d][2][:, :], ALU.add).then_inc(sem[d].state_done, 1)
                            tt(out_o[d], out_o[d], B.tmp[:, :], ALU.add)
                            link(tt(out_y[d], out_y[d], bank[d][0][:, :], ALU.add))
                        for d in DIRS:
                            B = buf[d]
                            dve.wait_ge(sem[d].off_done, s + 1)
                            tt(h64(B.tmp[:, :]), h64(bank[d][1][:, :]), over(B.ecols[:, 4:12], [P, 8, SP]), ALU.mult)
                            link(tt(h64(B.H[:, :]), h64(B.H[:, :]), over(B.ecols[:, 16:24], [P, 8, SP]), ALU.mult))
                            tt(out_y[d], out_y[d], B.tmp[:, :], ALU.add)
                            tt(B.H[:, :], B.H[:, :], bank[d][2][:, :], ALU.add).then_inc(sem[d].step_done, 1)
                    assert link.n == N_LINKS, link.n


def gate_mix(nc, S, acc, mixT):
    with ExitStack() as ctx, stage(nc, "in0", "in1", "rooted", "gated", "transposed", "evacuated", "chain") as (
            in0, in1, rooted, gated, transposed, evacuated, chain):
        loaded = [in0, in1]
        z = ctx.enter_context(nc.sbuf_tensor("z_in", [P, 2, 2 * GW], F32))
        xs = ctx.enter_context(nc.sbuf_tensor("xs_in", [P, 2, GW], F32))
        sq = ctx.enter_context(nc.sbuf_tensor("sq_mix", [P, 2 * GW], F32))
        out = ctx.enter_context(nc.sbuf_tensor("mix_rows", [P, 2, 2 * GW], F32))
        ss = ctx.enter_context(nc.sbuf_tensor("ss_mix", [P, 2, 8], F32))
        ps = [ctx.enter_context(nc.psum_tensor(f"ps_mix{b}", [P, KT, P], F32)) for b in range(2)]
        e0, d0 = VEC["eps"][0], ROW["ssm_D"][0]
        heads = lambda ap: ap.rearrange("p (h c) -> p h c", c=P)
        h64 = lambda ap: ap.rearrange("p (h c) -> p h c", c=SP)
        with nc.Block() as block:
            @block.sync
            def _(sp):
                for t in range(NX):
                    if t >= 2:
                        sp.wait_ge(gated, t - 1)
                    sp.dma_start(z[:, t % 2, :], S.z_dram[t]).then_inc(loaded[t % 2], 16)
                    sp.dma_start(xs[:, t % 2, :], S.tok_dram[NC + t][:, 2 * GW:3 * GW]).then_inc(loaded[t % 2], 16)

            @block.scalar
            def _(act):
                for t in range(NX):
                    act.wait_ge(chain, 11 * t + 8)
                    nc.scalar.activation(ss[:, t % 2, 0:4], ss[:, t % 2, 0:4], ACT.Sqrt, bias=S.vec[:, e0:e0 + 1], scale=1.0 / P)
                    nc.scalar.activation(ss[:, t % 2, 4:5], ss[:, t % 2, 4:5], ACT.Sqrt, bias=S.vec[:, e0:e0 + 1],
                                         scale=1.0 / GW).then_inc(rooted, 1)

            @block.vector
            def _(dve):
                tt = nc.vector.tensor_tensor
                link = Chain(dve, chain)

                def evacuate(t):
                    dve.wait_ge(transposed, t + 1)
                    for m in range(KT):
                        g = VEC["gdn_norm_g"][0] if m < 4 else VEC["ssm_norm_g"][0] + m - 4
                        last = nc.vector.tensor_scalar(mixT[:, m, t * P:(t + 1) * P], ps[t % 2][:, m, :],
                                                       S.vec[:, g:g + 1], None, ALU.mult)
                    last.then_inc(evacuated, 1)

                for t in range(NX):
                    dve.wait_ge(loaded[t % 2], 32 * (t // 2 + 1))
                    if t >= 2:
                        dve.wait_ge(transposed, t - 1)
                    o, y = acc[:, NC + t, 0:GW], acc[:, NC + t, GW:2 * GW]
                    link(tt(h64(out[:, t % 2, GW:2 * GW]), h64(xs[:, t % 2, :]), over(S.row[:, d0:d0 + 8], [P, 8, SP]), ALU.mult))
                    link(tt(out[:, t % 2, GW:2 * GW], out[:, t % 2, GW:2 * GW], y, ALU.add))
                    link(tt(out[:, t % 2, GW:2 * GW], out[:, t % 2, GW:2 * GW], z[:, t % 2, GW:2 * GW], ALU.mult))
                    link(tt(sq[:, 0:GW], o, o, ALU.mult))
                    link(tt(sq[:, GW:2 * GW], out[:, t % 2, GW:2 * GW], out[:, t % 2, GW:2 * GW], ALU.mult))
                    link(nc.vector.reduce_sum(ss[:, t % 2, 0:4], heads(sq[:, 0:GW]), AX.X))
                    link(nc.vector.reduce_sum(ss[:, t % 2, 4:5], sq[:, GW:2 * GW], AX.X))
                    link(tt(out[:, t % 2, 0:GW], o, z[:, t % 2, 0:GW], ALU.mult))
                    dve.wait_ge(rooted, t + 1)
                    link(nc.vector.reciprocal(ss[:, t % 2, 0:5], ss[:, t % 2, 0:5]))
                    link(tt(heads(out[:, t % 2, 0:GW]), heads(out[:, t % 2, 0:GW]), over(ss[:, t % 2, 0:4], [P, 4, P]), ALU.mult))
                    link(nc.vector.tensor_scalar(out[:, t % 2, GW:2 * GW], out[:, t % 2, GW:2 * GW], ss[:, t % 2, 4:5],
                                                 None, ALU.mult))
                    dve.sem_inc(gated, 1)
                    if t >= 1:
                        evacuate(t - 1)
                evacuate(NX - 1)

            @block.tensor
            def _(pe):
                for t in range(NX):
                    pe.wait_ge(gated, t + 1)
                    if t >= 2:
                        pe.wait_ge(evacuated, t - 1)
                    for m in range(KT):
                        last = nc.tensor.transpose(ps[t % 2][:, m, :], out[:, t % 2, m * P:(m + 1) * P], S.ident)
                    last.then_inc(transposed, 1)
def residual_linear(nc, S, tag, w_dram, src, xT, factor):
    n_buf = 2
    kt = w_dram.shape[0] // P
    with ExitStack() as ctx, stage(nc, "w_in0", "w_in1", "tile_done", "ps_free") as (w_in0, w_in1, tile_done, ps_free):
        w_in = [w_in0, w_in1]
        w, ps = linear_stage_buffers(nc, ctx, tag, kt, n_buf, 2)
        with nc.Block() as block:
            @block.sync
            def _(sp):
                load_weights(nc, sp, KT // n_buf, n_buf, w, w_in, tile_done,
                             lambda i, b: feature_tiles(w_dram)[:, :, bass.ds((i * n_buf + b) * P, P)])

            @block.tensor
            def _(pe):
                multiply_tiles(nc, pe, KT // n_buf, n_buf, w, w_in, tile_done, lambda b: src, chunks_of(SEQ), ps, ps_free)

            @block.vector
            def _(dve):
                for m in range(KT):
                    dve.wait_ge(tile_done, n_buf + m + 1)
                    row = xT[:, m, :].rearrange("p (a c) -> p a c", c=BANK)
                    nc.vector.scalar_tensor_tensor(row, ps[m % 2][:, :, :], factor(m) if factor else 1.0, row,
                                                   ALU.mult, ALU.add).then_inc(ps_free, 1)


def gated_unit(nc, S, io, hT, guT, spare):
    UN, n_buf, sets = 4, 2, 4
    rows = SEQ // GRID
    with ExitStack() as ctx, stage(nc, "w_in0", "w_in1", "tile_done", "ps_free", "padded", "convolved", "activated",
                                   "multiplied", "zeroed", "chain") as (
            w_in0, w_in1, tile_done, ps_free, padded, convolved, activated, multiplied, zeroed, chain):
        w_in = [w_in0, w_in1]
        w = [spare[:, 2 + b, :].rearrange("p (k c) -> p k c", c=P) for b in range(n_buf)]
        ps = [ctx.enter_context(nc.psum_tensor(f"ps_ffn{b}", [P, 2, BANK], F32)) for b in range(sets)]
        grid = ctx.enter_context(nc.sbuf_tensor("grid", [P, 2, rows + 2, GRID + 2], F32))
        con = spare[:, 0:2, :].rearrange("p b (r c) -> p b r c", c=GRID)
        cw, cb = VEC["ffn_conv_w"][0], VEC["ffn_conv_b"][0]
        with nc.Block() as block:
            @block.sync
            def _(sp):
                gate, up = feature_tiles(io["ffn_w_gate"]), feature_tiles(io["ffn_w_up"])
                load_weights(nc, sp, 2 * FT // UN, UN, w, w_in, tile_done,
                             lambda i, b: (gate, up)[b % 2][:, :, bass.ds(i * (UN // 2 * P) + b // 2 * P, P)])

            @block.tensor
            def _(pe):
                multiply_tiles(nc, pe, 2 * FT // UN, UN, w, w_in, tile_done, lambda b: hT, chunks_of(SEQ), ps, ps_free)

            @block.scalar
            def _(act):
                act.wait_ge(zeroed, 1)
                for f in range(FT + 1):
                    if f < FT:
                        act.wait_ge(tile_done, n_buf + 2 * f + 1)
                        if f >= 2:
                            act.wait_ge(convolved, f - 1)
                        for a in range(2):
                            last = nc.scalar.activation(grid[:, f % 2, 1 + 8 * a:9 + 8 * a, 1:1 + GRID],
                                                        ps[2 * f % sets][:, a, :].rearrange("p (r c) -> p r c", c=GRID),
                                                        ACT.Copy)
                        last.then_inc(padded, 1)
                    if f >= 1:
                        act.wait_ge(convolved, f)
                        row = con[:, (f - 1) % 2, :, :]
                        nc.scalar.activation(row, row, ACT.Silu, bias=S.vec[:, cb + f - 1:cb + f]).then_inc(activated, 1)

            @block.vector
            def _(dve):
                link = Chain(dve, chain)
                nc.vector.memset(grid[:, :, :, :], 0.0).then_inc(zeroed, 1)

                def multiply(f):
                    dve.wait_ge(activated, f + 1)
                    dve.wait_ge(tile_done, n_buf + 2 * f + 2)
                    nc.vector.tensor_tensor(guT[:, f, :].rearrange("p (a c) -> p a c", c=BANK),
                                            con[:, f % 2, :, :].rearrange("p (a r) c -> p a (r c)", a=2),
                                            ps[(2 * f + 1) % sets][:, :, :], ALU.mult).then_inc(ps_free, 2)

                for f in range(FT):
                    dve.wait_ge(padded, f + 1)
                    out = con[:, f % 2, :, :]
                    for tap in range(9):
                        shifted = grid[:, f % 2, tap // 3:tap // 3 + rows, tap % 3:tap % 3 + GRID]
                        weight = S.vec[:, cw + tap * FT + f:cw + tap * FT + f + 1]
                        if tap == 0:
                            link(nc.vector.tensor_scalar(out, shifted, weight, None, ALU.mult))
                        elif tap < 8:
                            link(nc.vector.scalar_tensor_tensor(out, shifted, weight, out, ALU.mult, ALU.add))
                        else:
                            nc.vector.scalar_tensor_tensor(out, shifted, weight, out, ALU.mult, ALU.add).then_inc(convolved, 1)
                    if f >= 1:
                        multiply(f - 1)
                multiply(FT - 1)
IN2_X, IN2_Y, IN2_CQ, IN2_PE, IN2_GA, IN2_GB = 0, 1024, 2048, 2560, 2624, 3648
TWO_PI = 2 * np.pi
PI_A = 6.28125
PI_B = 0.0019350051879882812
PI_C = TWO_PI - PI_A - PI_B
CONV_W = 4


def rotary_tables(nc, S, io, cos, sin):
    R = ROPE
    with ExitStack() as ctx, stage(nc, "pos_in", "reduced", "done", "chain") as (pos_in, reduced, done, chain):
        ints = ctx.enter_context(nc.sbuf_tensor("pos_i", [R, SEQ], I32))
        turns = ctx.enter_context(nc.sbuf_tensor("turns_i", [R, SEQ], I32))
        ang = ctx.enter_context(nc.sbuf_tensor("ang", [R, SEQ], F32))
        k = ctx.enter_context(nc.sbuf_tensor("turns_f", [R, SEQ], F32))
        f0 = VEC["inv_freq"][0]
        with nc.Block() as block:
            @block.sync
            def _(sp):
                sp.dma_start(ints[:, :], io["positions"][0, :].partition_broadcast(R)).then_inc(pos_in, 16)

            @block.vector
            def _(dve):
                link = Chain(dve, chain)
                ts, stt = nc.vector.tensor_scalar, nc.vector.scalar_tensor_tensor

                def into_half_turn(a):
                    link(ts(k[:, :], a, float(np.pi), -TWO_PI, ALU.is_gt, ALU.mult))
                    link(nc.vector.tensor_tensor(a, a, k[:, :], ALU.add))
                    link(ts(k[:, :], a, -float(np.pi), TWO_PI, ALU.is_lt, ALU.mult))
                    link(nc.vector.tensor_tensor(a, a, k[:, :], ALU.add))
                    link(ts(a, a, 3.1415925, -3.1415925, ALU.min, ALU.max))

                dve.wait_ge(pos_in, 16)
                link(nc.vector.tensor_copy(ang[:, :], ints[:, :]))
                link(ts(ang[:, :], ang[:, :], S.vec[0:R, f0:f0 + 1], None, ALU.mult))
                link(ts(k[:, :], ang[:, :], float(1 / TWO_PI), None, ALU.mult))
                link(nc.vector.tensor_copy(turns[:, :], k[:, :]))
                link(nc.vector.tensor_copy(k[:, :], turns[:, :]))
                for part in (PI_A, PI_B, PI_C):
                    link(stt(ang[:, :], k[:, :], -part, ang[:, :], ALU.mult, ALU.add))
                into_half_turn(ang[:, :])
                link(ts(cos[0:R, :], ang[:, :], float(np.pi / 2), None, ALU.add))
                into_half_turn(cos[0:R, :])
                dve.sem_inc(reduced, 1)

            @block.scalar
            def _(act):
                act.wait_ge(reduced, 1)
                nc.scalar.activation(sin[0:R, :], ang[:, :], ACT.Sin)
                nc.scalar.activation(cos[0:R, :], cos[0:R, :], ACT.Sin).then_inc(done, 1)


def latent_projections(nc, S, io, uT, lat, k_pe):
    with ExitStack() as ctx, stage(nc, "w_loaded", "tile_done", "evacuated") as (w_loaded, tile_done, evacuated):
        n_out = 2 * LORA + ROPE
        w = ctx.enter_context(nc.sbuf_tensor("w_lat", [P, KT, n_out], F32))
        ps = [ctx.enter_context(nc.psum_tensor(f"ps_lat{b}", [P, 2, BANK], F32)) for b in range(4)]
        with nc.Block() as block:
            @block.sync
            def _(sp):
                sp.dma_start(w[:, :, :], feature_tiles(io["w_in_2"])[:, :, IN2_CQ:IN2_CQ + n_out]).then_inc(w_loaded, 16)

            @block.tensor
            def _(pe):
                pe.wait_ge(w_loaded, 16)
                for m in range(5):
                    rows = min(P, n_out - m * P)
                    if m >= 4:
                        pe.wait_ge(evacuated, m - 3)
                    for c in range(2):
                        for k in range(KT):
                            last = nc.tensor.matmul(ps[m % 4][0:rows, c, :], w[:, k, m * P:m * P + rows],
                                                    uT[:, k, c * BANK:(c + 1) * BANK], start=(k == 0), stop=(k == KT - 1))
                    last.then_inc(tile_done, 1)

            @block.vector
            def _(dve):
                for m in range(5):
                    dve.wait_ge(tile_done, m + 1)
                    out = lat[:, m, :] if m < 4 else k_pe[0:ROPE, :]
                    nc.vector.tensor_copy(out.rearrange("p (a c) -> p a c", a=2),
                                          ps[m % 4][0:out.shape[0], :, :]).then_inc(evacuated, 1)


def head_projections(nc, S, io, h0, lat, qk, v):
    with ExitStack() as ctx, stage(nc, "w_loaded", "unit_done", "evacuated") as (w_loaded, unit_done, evacuated):
        wq = ctx.enter_context(nc.sbuf_tensor(f"w_q{h0}", [P, LT, 2 * QK], F32))
        wkv = ctx.enter_context(nc.sbuf_tensor(f"w_kv{h0}", [P, LT, 2, NOPE + DV], F32))
        ps = [ctx.enter_context(nc.psum_tensor(f"ps_hp{h0}{b}", [P, 2, BANK], F32)) for b in range(4)]
        units = []
        for h in range(2):
            units += [(lambda k, h=h: wq[:, k, h * QK:h * QK + NOPE], 0, NOPE, qk[:, h, 0, :]),
                      (lambda k, h=h: wq[:, k, h * QK + NOPE:(h + 1) * QK], 0, ROPE, qk[0:ROPE, h, 1, :]),
                      (lambda k, h=h: wkv[:, k, h, 0:NOPE], LT, NOPE, qk[:, h, 2, :])]
        with nc.Block() as block:
            @block.sync
            def _(sp):
                sp.dma_start(wq[:, :, :], feature_tiles(io["w_uq_2"])[:, :, h0 * QK:(h0 + 2) * QK]).then_inc(w_loaded, 16)
                sp.dma_start(wkv[:, :, :, :].rearrange("p k h c -> p k (h c)"), feature_tiles(io["w_ukv_2"])[
                    :, :, h0 * (NOPE + DV):(h0 + 2) * (NOPE + DV)]).then_inc(w_loaded, 16)

            @block.tensor
            def _(pe):
                pe.wait_ge(w_loaded, 32)
                for u, (weights, first, rows, _out) in enumerate(units):
                    if u >= 4:
                        pe.wait_ge(evacuated, u - 3)
                    for c in range(2):
                        for k in range(LT):
                            last = nc.tensor.matmul(ps[u % 4][0:rows, c, :], weights(k),
                                                    lat[:, first + k, c * BANK:(c + 1) * BANK], start=(k == 0), stop=(k == LT - 1))
                    last.then_inc(unit_done, 1)
                for g in range(2):
                    u = len(units) + g
                    pe.wait_ge(evacuated, u - 3)
                    for t in range(4):
                        for k in range(LT):
                            at = (g * 4 + t) * P
                            last = nc.tensor.matmul(ps[u % 4][:, t // 2, t % 2 * 256:t % 2 * 256 + 256].rearrange(
                                "p (h c) -> p h c", h=2), lat[:, LT + k, at:at + P], wkv[:, k, :, NOPE:NOPE + DV],
                                start=(k == 0), stop=(k == LT - 1))
                    last.then_inc(unit_done, 1)

            @block.vector
            def _(dve):
                for u in range(len(units) + 2):
                    dve.wait_ge(unit_done, u + 1)
                    if u < len(units):
                        out = units[u][3].rearrange("p (a c) -> p a c", a=2)
                    else:
                        g = u - len(units)
                        out = v[:, g * 4:g * 4 + 4, :].rearrange("p (a t) c -> p a (t c)", a=2)
                    nc.vector.tensor_copy(out, ps[u % 4][0:out.shape[0], :, :]).then_inc(evacuated, 1)


def rotate(nc, S, tag, tiles, cos, sin):
    parts = [t[:, c * BANK:(c + 1) * BANK] for t in tiles for c in range(2)]
    with ExitStack() as ctx, stage(nc, "turned", "rotated", "chain") as (turned, rotated, chain):
        ps = [ctx.enter_context(nc.psum_tensor(f"ps_rot{tag}{b}", [P, BANK], F32)) for b in range(4)]
        tmp = ctx.enter_context(nc.sbuf_tensor(f"rot_tmp{tag}", [P, BANK], F32))
        with nc.Block() as block:
            @block.tensor
            def _(pe):
                for u, x in enumerate(parts):
                    if u >= 4:
                        pe.wait_ge(rotated, u - 3)
                    nc.tensor.matmul(ps[u % 4][0:ROPE, :], S.mat[0:ROPE, MAT["rope"], 0:ROPE], x,
                                     start=True, stop=True).then_inc(turned, 1)

            @block.vector
            def _(dve):
                link = Chain(dve, chain)
                for u, x in enumerate(parts):
                    cols = slice(u % 2 * BANK, (u % 2 + 1) * BANK)
                    dve.wait_ge(turned, u + 1)
                    if u >= 1:
                        dve.wait_ge(rotated, u)
                    nc.vector.tensor_tensor(tmp[0:ROPE, :], ps[u % 4][0:ROPE, :], sin[0:ROPE, cols], ALU.mult)
                    link(nc.vector.tensor_tensor(x, x, cos[0:ROPE, cols], ALU.mult))
                    nc.vector.tensor_tensor(x, x, tmp[0:ROPE, :], ALU.add).then_inc(rotated, 1)


def attention(nc, S, h0, qk, v, oT):
    scale = float(QK) ** -0.5
    units = [(h, b) for h in range(2) for b in range(NX)]
    U = len(units)
    with ExitStack() as ctx, stage(nc, "scores_done", "max_done", "exp_done", "probs_done", "turned", "turned_out",
                                   "pv_done", "o_copied", "chain") as (
            scores_done, max_done, exp_done, probs_done, turned, turned_out, pv_done, o_copied, chain):
        p = ctx.enter_context(nc.sbuf_tensor(f"probs{h0}", [P, 2, SEQ], F32))
        pT = ctx.enter_context(nc.sbuf_tensor(f"probsT{h0}", [P, 2, SEQ], F32))
        st = ctx.enter_context(nc.sbuf_tensor(f"stat{h0}", [P, 2, 4], F32))
        sc = [ctx.enter_context(nc.psum_tensor(f"ps_sc{h0}{b}", [P, 2 * BANK], F32)) for b in range(2)]
        tr = ctx.enter_context(nc.psum_tensor(f"ps_tr{h0}", [P, 2 * BANK], F32))
        po = [ctx.enter_context(nc.psum_tensor(f"ps_o{h0}{b}", [P, P], F32)) for b in range(2)]
        with nc.Block() as block:
            @block.tensor
            def _(pe):
                def scores(u):
                    h, b = units[u]
                    q_cols = slice(b * P, (b + 1) * P)
                    if u >= 2:
                        pe.wait_ge(exp_done, u - 1)
                    for at, n in chunks_of((b + 1) * P):
                        out, final = sc[u % 2][:, at:at + n], at + n == (b + 1) * P
                        nc.tensor.matmul(out, qk[:, h, 0, q_cols], qk[:, h, 2, at:at + n], start=True, stop=False)
                        last = nc.tensor.matmul(out, qk[0:ROPE, h, 1, q_cols], qk[0:ROPE, h, 3, at:at + n], start=False, stop=not final)
                    last = nc.tensor.matmul(sc[u % 2][:, b * P:(b + 1) * P], S.ident, S.mat[:, MAT["neg1"], :], start=False, stop=True)
                    last.then_inc(scores_done, 1)

                def turn(u):
                    pe.wait_ge(probs_done, u + 1)
                    if u >= 1:
                        pe.wait_ge(turned_out, u)
                    for t in range(units[u][1] + 1):
                        last = nc.tensor.transpose(tr[:, t * P:(t + 1) * P], p[:, u % 2, t * P:(t + 1) * P], S.ident)
                    last.then_inc(turned, 1)

                def values(u):
                    h, b = units[u]
                    pe.wait_ge(turned_out, u + 1)
                    if u >= 2:
                        pe.wait_ge(o_copied, u - 1)
                    for t in range(b + 1):
                        last = nc.tensor.matmul(po[u % 2][:, :], v[:, t, h * DV:(h + 1) * DV], pT[:, u % 2, t * P:(t + 1) * P],
                                                start=(t == 0), stop=(t == b))
                    last.then_inc(pv_done, 1)

                scores(0)
                for u in range(U + 1):
                    if u + 1 < U:
                        scores(u + 1)
                    if u < U:
                        turn(u)
                    if u >= 1:
                        values(u - 1)

            @block.vector
            def _(dve):
                link = Chain(dve, chain)
                for u in range(U + 2):
                    if u < U:
                        n = (units[u][1] + 1) * P
                        dve.wait_ge(scores_done, u + 1)
                        link(nc.vector.reduce_max(st[:, u % 2, 0:1], sc[u % 2][:, 0:n], AX.X))
                        nc.vector.tensor_scalar(st[:, u % 2, 1:2], st[:, u % 2, 0:1], -scale, None, ALU.mult).then_inc(max_done, 1)
                    if 1 <= u <= U:
                        w = u - 1
                        n = (units[w][1] + 1) * P
                        dve.wait_ge(exp_done, w + 1)
                        link(nc.vector.reciprocal(st[:, w % 2, 3:4], st[:, w % 2, 2:3]))
                        nc.vector.tensor_scalar(p[:, w % 2, 0:n], p[:, w % 2, 0:n], st[:, w % 2, 3:4], None,
                                                ALU.mult).then_inc(probs_done, 1)
                    if u >= 2:
                        w = u - 2
                        h, b = units[w]
                        dve.wait_ge(pv_done, w + 1)
                        nc.vector.tensor_copy(oT[:, h0 + h, b * P:(b + 1) * P], po[w % 2][:, :]).then_inc(o_copied, 1)

            @block.scalar
            def _(act):
                for u in range(U + 1):
                    if u < U:
                        n = (units[u][1] + 1) * P
                        act.wait_ge(max_done, u + 1)
                        if u >= 2:
                            act.wait_ge(turned, u - 1)
                        nc.scalar.activation(p[:, u % 2, 0:n], sc[u % 2][:, 0:n], ACT.Exp, bias=st[:, u % 2, 1:2],
                                             scale=scale, accum_out=st[:, u % 2, 2:3]).then_inc(exp_done, 1)
                    if u >= 1:
                        w = u - 1
                        n = (units[w][1] + 1) * P
                        act.wait_ge(turned, w + 1)
                        if w >= 2:
                            act.wait_ge(pv_done, w - 1)
                        nc.scalar.activation(pT[:, w % 2, 0:n], tr[:, 0:n], ACT.Copy).then_inc(turned_out, 1)


def gated_linear(nc, S, tag, w_gate, gate_src, w_value, value_src, out, add):
    UN, n_buf, sets = 4, 4, 4
    with ExitStack() as ctx, stage(nc, *[f"w_in{b}" for b in range(n_buf)], "tile_done", "ps_free", "gate_done",
                                   "chain") as sems:
        w_in, (tile_done, ps_free, gate_done, chain) = sems[:n_buf], sems[n_buf:]
        w, ps = linear_stage_buffers(nc, ctx, tag, KT, n_buf, 2, sets)
        gate = ctx.enter_context(nc.sbuf_tensor(f"gate_{tag}", [P, 2, 2, BANK], F32))
        halves = lambda ap: ap.rearrange("p (a c) -> p a c", a=2)
        with nc.Block() as block:
            @block.sync
            def _(sp):
                sp.sem_inc(tile_done, n_buf)
                for m in range(2 * KT):
                    sp.wait_ge(tile_done, m + 1)
                    sp.dma_start(w[m % n_buf][:, :, :], feature_tiles((w_gate, w_value)[m % 2])[
                        :, :, m // 2 * P:(m // 2 + 1) * P]).then_inc(w_in[m % n_buf], 16)

            @block.tensor
            def _(pe):
                multiply_tiles(nc, pe, 2 * KT // UN, UN, w, w_in, tile_done, lambda b: (gate_src, value_src)[b % 2],
                               chunks_of(SEQ), ps, ps_free)

            @block.scalar
            def _(act):
                for m in range(KT):
                    act.wait_ge(tile_done, n_buf + 2 * m + 1)
                    if m >= 2:
                        act.wait_ge(ps_free, sets + 2 * (m - 1))
                    nc.scalar.activation(gate[:, m % 2, :, :], ps[2 * m % sets][:, :, :], ACT.Sigmoid).then_inc(gate_done, 1)

            @block.vector
            def _(dve):
                link = Chain(dve, chain)
                for m in range(KT):
                    dve.wait_ge(gate_done, m + 1)
                    dve.wait_ge(tile_done, n_buf + 2 * m + 2)
                    g = gate[:, m % 2, :, :]
                    if add:
                        link(nc.vector.tensor_tensor(g, g, ps[(2 * m + 1) % sets][:, :, :], ALU.mult))
                        last = nc.vector.tensor_tensor(halves(out[:, m, :]), halves(out[:, m, :]), g, ALU.add)
                    else:
                        last = nc.vector.tensor_tensor(halves(out[:, m, :]), g, ps[(2 * m + 1) % sets][:, :, :], ALU.mult)
                    last.then_inc(ps_free, 2)


def causal_projection(nc, S, io, uT, xr):
    n_buf, pad = 4, CONV_W - 1
    cw, cb = VEC["conv_w_2"][0], VEC["conv_b_2"][0]
    with ExitStack() as ctx, stage(nc, *[f"w_in{b}" for b in range(n_buf)], "tile_done", "ps_free", "convolved",
                                   "zeroed", "chain") as sems:
        w_in, (tile_done, ps_free, convolved, zeroed, chain) = sems[:n_buf], sems[n_buf:]
        w, ps = linear_stage_buffers(nc, ctx, "xr", KT, n_buf, 2)
        row = ctx.enter_context(nc.sbuf_tensor("row_xr", [P, 2, SEQ + pad], F32))
        with nc.Block() as block:
            @block.sync
            def _(sp):
                load_weights(nc, sp, KT // n_buf, n_buf, w, w_in, tile_done, lambda i, b: feature_tiles(
                    io["w_in_2"])[:, :, bass.ds((i * n_buf + b) * P, P)])

            @block.tensor
            def _(pe):
                multiply_tiles(nc, pe, KT // n_buf, n_buf, w, w_in, tile_done, lambda b: uT, chunks_of(SEQ), ps, ps_free)

            @block.scalar
            def _(act):
                act.wait_ge(zeroed, 1)
                for m in range(KT):
                    act.wait_ge(tile_done, n_buf + m + 1)
                    if m >= 2:
                        act.wait_ge(convolved, m - 1)
                    nc.scalar.activation(row[:, m % 2, pad:pad + SEQ].rearrange("p (a c) -> p a c", a=2),
                                         ps[m % 2][:, :, :], ACT.Copy).then_inc(ps_free, 1)

            @block.vector
            def _(dve):
                link = Chain(dve, chain)
                nc.vector.memset(row[:, :, 0:pad], 0.0).then_inc(zeroed, 1)
                for m in range(KT):
                    dve.wait_ge(ps_free, 2 + m + 1)
                    tap = lambda j: S.vec[:, cw + j * KT + m:cw + j * KT + m + 1]
                    out = xr[:, m, :]
                    link(nc.vector.tensor_scalar(out, row[:, m % 2, 0:SEQ], tap(0), S.vec[:, cb + m:cb + m + 1], ALU.mult, ALU.add))
                    for j in range(1, CONV_W):
                        last = nc.vector.scalar_tensor_tensor(out, row[:, m % 2, j:j + SEQ], tap(j), out, ALU.mult, ALU.add)
                        if j < CONV_W - 1:
                            link(last)
                    last.then_inc(convolved, 1)


def recurrent_unit(nc, S, io, xr):
    with ExitStack() as ctx, stage(nc, "w_loaded", "rates", "lam_exp", "lam_done", "gates_full", "sig_done", "exps_done",
                                   "mult_ready", "rooted", "scanned", "chain", "doubled") as (
            w_loaded, rates, lam_exp, lam_done, gates_full, sig_done, exps_done, mult_ready, rooted, scanned, chain, doubled):
        w = ctx.enter_context(nc.sbuf_tensor("w_lru", [P, 2, KT, P], F32))
        t = {n: ctx.enter_context(nc.sbuf_tensor(f"lam_{n}", [P, KT], F32)) for n in ("e", "m", "q", "z", "z2", "p")}
        fac = ctx.enter_context(nc.sbuf_tensor("lam_fac", [P, 3, KT], F32))
        r = ctx.enter_context(nc.sbuf_tensor("lru_r", [P, 2, SEQ], F32))
        g = ctx.enter_context(nc.sbuf_tensor("lru_i", [P, 2, SEQ], F32))
        a = ctx.enter_context(nc.sbuf_tensor("lru_a", [P, 2, SEQ], F32))
        e2 = ctx.enter_context(nc.sbuf_tensor("lru_e2", [P, 2, SEQ], F32))
        ps = [ctx.enter_context(nc.psum_tensor(f"ps_lru{b}", [P, 2, 2 * BANK], F32)) for b in range(2)]
        lam0, ba, bx = VEC["lru_lambda_2"][0], VEC["lru_ba_2"][0], VEC["lru_bx_2"][0]
        lam = S.vec[:, lam0:lam0 + KT]
        flat = lambda n: t[n][:, :]
        with nc.Block() as block:
            @block.sync
            def _(sp):
                for j, n in enumerate(("lru_wa_2", "lru_wx_2")):
                    sp.dma_start(w[:, j, :, :], io[n].rearrange("n k j -> k n j")).then_inc(w_loaded, 16)

            @block.tensor
            def _(pe):
                pe.wait_ge(w_loaded, 32)
                for n in range(KT):
                    if n >= 2:
                        pe.wait_ge(sig_done, n - 1)
                    for j in range(2):
                        for c in range(2):
                            last = nc.tensor.matmul(ps[n % 2][:, j, c * BANK:(c + 1) * BANK], w[:, j, n, :],
                                                    xr[:, n, c * BANK:(c + 1) * BANK], start=True, stop=True)
                    last.then_inc(gates_full, 1)

            @block.scalar
            def _(act):
                act.wait_ge(chain, 2)
                nc.scalar.activation(flat("e"), flat("e"), ACT.Exp).then_inc(lam_exp, 1)
                for n in range(KT):
                    act.wait_ge(gates_full, n + 1)
                    if n >= 2:
                        act.wait_ge(scanned, n - 1)
                    nc.scalar.activation(r[:, n % 2, :], ps[n % 2][:, 0, :], ACT.Sigmoid, bias=S.vec[:, ba + n:ba + n + 1])
                    nc.scalar.activation(g[:, n % 2, :], ps[n % 2][:, 1, :], ACT.Sigmoid,
                                         bias=S.vec[:, bx + n:bx + n + 1]).then_inc(sig_done, 1)
                    if n == 0:
                        act.wait_ge(lam_done, 1)
                    act.wait_ge(sig_done, n + 1)
                    nc.scalar.activation(a[:, n % 2, :], r[:, n % 2, :], ACT.Exp, scale=fac[:, 0, n:n + 1])
                    nc.scalar.activation(e2[:, n % 2, :], r[:, n % 2, :], ACT.Exp, scale=fac[:, 1, n:n + 1])
                    nc.scalar.activation(r[:, n % 2, :], r[:, n % 2, :], ACT.Tanh, scale=fac[:, 2, n:n + 1]).then_inc(exps_done, 1)
                    act.wait_ge(mult_ready, n + 1)
                    nc.scalar.activation(e2[:, n % 2, :], e2[:, n % 2, :], ACT.Sqrt).then_inc(rooted, 1)

            @block.vector
            def _(dve):
                tt, stt, ts = nc.vector.tensor_tensor, nc.vector.scalar_tensor_tensor, nc.vector.tensor_scalar
                link = Chain(dve, chain)
                link(ts(flat("m"), lam, -1.0, 0.0, ALU.mult, ALU.max))
                link(stt(flat("e"), flat("m"), -2.0, lam, ALU.mult, ALU.subtract))
                dve.wait_ge(lam_exp, 1)
                log1p_series(nc, link, flat)
                link(stt(flat("m"), flat("z2"), 2.0, flat("m"), ALU.mult, ALU.add))
                for j, c in enumerate((-8.0, -16.0, 8.0)):
                    last = ts(fac[:, j, :], flat("m"), c, None, ALU.mult)
                last.then_inc(lam_done, 1)
                for n in range(KT):
                    b = n % 2
                    dve.wait_ge(exps_done, n + 1)
                    stt(e2[:, b, :], e2[:, b, :], 1.0, r[:, b, :], ALU.add, ALU.mult).then_inc(mult_ready, 1)
                    link(tt(g[:, b, :], g[:, b, :], xr[:, n, :], ALU.mult))
                    dve.wait_ge(rooted, n + 1)
                    link(tt(g[:, b, :], g[:, b, :], e2[:, b, :], ALU.mult))
                    nc.vector.tensor_tensor_scan(xr[:, n, :], a[:, b, :], g[:, b, :], 0.0, ALU.mult, ALU.add).then_inc(scanned, 1)


def gelu_projection(nc, S, io, uT, xr):
    n_buf = 4
    with ExitStack() as ctx, stage(nc, *[f"w_in{b}" for b in range(n_buf)], "tile_done", "ps_free", "multiplied") as sems:
        w_in, (tile_done, ps_free, multiplied) = sems[:n_buf], sems[n_buf:]
        w, ps = linear_stage_buffers(nc, ctx, "yr", KT, n_buf, 2)
        act_row = ctx.enter_context(nc.sbuf_tensor("gelu_row", [P, 2, 2, BANK], F32))
        with nc.Block() as block:
            @block.sync
            def _(sp):
                load_weights(nc, sp, KT // n_buf, n_buf, w, w_in, tile_done, lambda i, b: feature_tiles(
                    io["w_in_2"])[:, :, bass.ds((i * n_buf + b) * P + IN2_Y, P)])

            @block.tensor
            def _(pe):
                multiply_tiles(nc, pe, KT // n_buf, n_buf, w, w_in, tile_done, lambda b: uT, chunks_of(SEQ), ps, ps_free)

            @block.scalar
            def _(act):
                for m in range(KT):
                    act.wait_ge(tile_done, n_buf + m + 1)
                    if m >= 2:
                        act.wait_ge(multiplied, m - 1)
                    nc.scalar.activation(act_row[:, m % 2, :, :], ps[m % 2][:, :, :], ACT.Gelu_apprx_tanh).then_inc(ps_free, 1)

            @block.vector
            def _(dve):
                for m in range(KT):
                    dve.wait_ge(ps_free, 2 + m + 1)
                    out = xr[:, m, :].rearrange("p (a c) -> p a c", a=2)
                    nc.vector.tensor_tensor(out, out, act_row[:, m % 2, :, :], ALU.mult).then_inc(multiplied, 1)
def store_rows(nc, S, tag, src, out_dram):
    with ExitStack() as ctx, stage(nc, "transposed", "copied", "stored0", "stored1") as (transposed, copied, st0, st1):
        stored = [st0, st1]
        rows = ctx.enter_context(nc.sbuf_tensor(f"rows_{tag}", [P, 2, D], F32))
        ps = [ctx.enter_context(nc.psum_tensor(f"ps_{tag}{b}", [P, D], F32)) for b in range(2)]
        with nc.Block() as block:
            @block.tensor
            def _(pe):
                for t in range(NX):
                    if t >= 2:
                        pe.wait_ge(copied, t - 1)
                    for k in range(KT):
                        last = nc.tensor.transpose(ps[t % 2][:, k * P:(k + 1) * P], src[:, k, t * P:(t + 1) * P], S.ident)
                    last.then_inc(transposed, 1)

            @block.vector
            def _(dve):
                for t in range(NX):
                    dve.wait_ge(transposed, t + 1)
                    if t >= 2:
                        dve.wait_ge(stored[t % 2], 16 * (t // 2))
                    nc.vector.tensor_copy(rows[:, t % 2, :], ps[t % 2][:, :]).then_inc(copied, 1)

            @block.sync
            def _(sp):
                for t in range(NX):
                    sp.wait_ge(copied, t + 1)
                    sp.dma_start(out_dram[t * P:(t + 1) * P, :], rows[:, t % 2, :]).then_inc(stored[t % 2], 16)
                sp.wait_ge(st0, 16 * NX // 2)
                sp.wait_ge(st1, 16 * NX // 2)


def route(nc, S, io, xnT, gates, dest, block_expert):
    E, J = NE, EPG
    with ExitStack() as ctx, stage(nc, "w_loaded", "logits_done", "diff_ready", "exp_done", "choice_ready", "counted",
                                   "chain", "ids_ready", "zero_ready", "zero_stored", "dest_ready", "scattered") as (
            w_loaded, logits_done, diff_ready, exp_done, choice_ready, counted, chain, ids_ready, zero_ready, zero_stored,
            dest_ready, scattered):
        tile = lambda n, shape, dt=F32: ctx.enter_context(nc.sbuf_tensor(f"rt_{n}", shape, dt))
        w = tile("w", [P, KT, NG + NE])
        L = tile("logits", [P, NX, NG + NE])
        desc = tile("desc", [P, J])
        top = tile("top", [P, 4, NX])
        eq, diff, eg = tile("eq", [P, NX, J]), tile("diff", [P, NX, J]), tile("eg", [P, NX, J])
        hot = [tile(f"hot{n}", [P, NX, J]) for n in range(3)]
        spread = tile("spread", [P, NX, NG, J])
        pick = [tile(f"pick{n}", [P, NX, E]) for n in range(2)]
        both = tile("both", [P, NX, E])
        prob = tile("prob", [P, 4, NX])
        cnt, blocks, ends, starts = [tile(n, [P, E]) for n in ("cnt", "blocks", "ends", "starts")]
        dest_f = tile("dest_f", [P, 2 * NX])
        cmp = tile("cmp", [1, MOE_BLOCKS, E])
        be_f = tile("be_f", [1, MOE_BLOCKS])
        ids = tile("ids", [P, NX], I32)
        zeros = tile("zeros", [P, MOE_BLOCKS], I32)
        ps = ctx.enter_context(nc.psum_tensor("ps_logits", [P, NX, P], F32))
        ps_rank = ctx.enter_context(nc.psum_tensor("ps_rank", [P, NX, E], F32))
        ps_cnt = ctx.enter_context(nc.psum_tensor("ps_cnt", [P, E], F32))
        with nc.Block() as block:
            @block.sync
            def _(sp):
                sp.dma_start(w[:, :, :], io["router_w"].rearrange("(k p) m -> p k m", p=P)).then_inc(w_loaded, 16)
                sp.wait_ge(zero_ready, 1)
                sp.dma_start(S.slot_dram.rearrange("(p b) o -> p (b o)", p=P), zeros[:, :]).then_inc(zero_stored, 16)
                sp.wait_ge(zero_stored, 16)

            @block.gpsimd
            def _(pool):
                nc.gpsimd.memset(zeros[:, :], 0).then_inc(zero_ready, 1)
                nc.gpsimd.iota(ids[:, :], pattern=[[P, NX]], base=0, channel_multiplier=1).then_inc(ids_ready, 1)
                pool.wait_ge(ids_ready, 1)
                pool.wait_ge(zero_stored, 16)
                pool.wait_ge(dest_ready, 1)
                for c in range(2 * NX):
                    nc.gpsimd.indirect_dma_start(out=S.slot_dram, out_offset=bass.IndirectOffsetOnAxis(
                        ap=dest[:, c:c + 1], axis=0), in_=ids[:, c % NX:c % NX + 1], in_offset=None).then_inc(scattered, 16)
                pool.wait_ge(scattered, 16 * 2 * NX)

            @block.tensor
            def _(pe):
                pe.wait_ge(w_loaded, 16)
                for t in range(NX):
                    for k in range(KT):
                        last = nc.tensor.matmul(ps[:, t, 0:NG + NE], xnT[:, k, t * P:(t + 1) * P], w[:, k, :],
                                                start=(k == 0), stop=(k == KT - 1))
                last.then_inc(logits_done, 1)
                pe.wait_ge(choice_ready, 1)
                for t in range(NX):
                    for u in range(t + 1):
                        nc.tensor.matmul(ps_rank[:, t, :], S.ones if u < t else S.mat[:, MAT["before"], :], both[:, u, :],
                                         start=(u == 0), stop=(u == t))
                for t in range(NX):
                    last = nc.tensor.matmul(ps_cnt[:, :], S.ones, both[:, t, :], start=(t == 0), stop=(t == NX - 1))
                last.then_inc(counted, 1)

            @block.scalar
            def _(act):
                act.wait_ge(diff_ready, 1)
                nc.scalar.activation(diff[:, :, :], diff[:, :, :], ACT.Exp)
                nc.scalar.activation(prob[:, 1, :], prob[:, 1, :], ACT.Exp).then_inc(exp_done, 1)

            @block.vector
            def _(dve):
                tt, ts, stt = nc.vector.tensor_tensor, nc.vector.tensor_scalar, nc.vector.scalar_tensor_tensor
                link = Chain(dve, chain)
                r0, i0, s0 = ROW["router_b"][0], ROW["expert_iota"][0], ROW["block_start"][0]
                wide = [P, NX, J]

                def first_of_max(x, m, out):
                    link(nc.vector.reduce_max(m, x, AX.X))
                    link(tt(eq[:, :, :], x, over(m, wide), ALU.is_equal))
                    link(tt(eq[:, :, :], eq[:, :, :], under(desc[:, :], NX, J), ALU.mult))
                    link(nc.vector.reduce_max(top[:, 3, :], eq[:, :, :], AX.X))
                    link(tt(out, eq[:, :, :], over(top[:, 3, :], wide), ALU.is_equal))

                link(ts(desc[:, :], S.row[:, i0:i0 + J], -1.0, float(J), ALU.mult, ALU.add))
                dve.wait_ge(logits_done, 1)
                link(tt(L[:, :, :], ps[:, :, 0:NG + NE], under(S.row[:, r0:r0 + NG + NE], NX, NG + NE), ALU.add))
                g, e = L[:, :, 0:NG], L[:, :, NG:NG + NE].rearrange("p t (g j) -> p t g j", g=NG)
                first_of_max(g, top[:, 0, :], hot[0][:, :, :])
                link(tt(diff[:, :, :], g, over(top[:, 0, :], wide), ALU.subtract))
                link(tt(spread[:, :, :, :], e, hot[0][:, :, :].unsqueeze(3).to_broadcast([P, NX, NG, J]), ALU.mult))
                link(nc.vector.reduce_sum(eg[:, :, :], spread[:, :, :, :].rearrange("p t g j -> p t j g"), AX.X))
                first_of_max(eg[:, :, :], top[:, 1, :], hot[1][:, :, :])
                link(stt(eg[:, :, :], hot[1][:, :, :], -1e30, eg[:, :, :], ALU.mult, ALU.add))
                first_of_max(eg[:, :, :], top[:, 2, :], hot[2][:, :, :])
                link(tt(prob[:, 1, :], top[:, 2, :], top[:, 1, :], ALU.subtract))
                for n in range(2):
                    link(tt(pick[n][:, :, :].rearrange("p t (g j) -> p t g j", g=NG),
                            hot[0][:, :, :].unsqueeze(3).to_broadcast([P, NX, NG, J]),
                            hot[1 + n][:, :, :].unsqueeze(2).to_broadcast([P, NX, NG, J]), ALU.mult))
                dve.sem_inc(diff_ready, 1)
                tt(both[:, :, :], pick[0][:, :, :], pick[1][:, :, :], ALU.add).then_inc(choice_ready, 1)
                dve.wait_ge(exp_done, 1)
                link(nc.vector.reduce_sum(prob[:, 0, :], diff[:, :, :], AX.X))
                link(ts(prob[:, 2, :], prob[:, 1, :], 1.0, None, ALU.add))
                link(tt(prob[:, 0, :], prob[:, 0, :], prob[:, 2, :], ALU.mult))
                link(nc.vector.reciprocal(gates[:, 0:NX], prob[:, 0, :]))
                link(tt(gates[:, NX:2 * NX], gates[:, 0:NX], prob[:, 1, :], ALU.mult))
                dve.wait_ge(counted, 1)
                link(nc.vector.tensor_copy(cnt[:, :], ps_cnt[:, :]))
                link(ts(blocks[:, :], cnt[:, :], 0.0, None, ALU.is_gt))
                for n in range(1, NX):
                    link(stt(blocks[:, :], cnt[:, :], float(n * P), blocks[:, :], ALU.is_gt, ALU.add))
                link(nc.vector.tensor_tensor_scan(ends[:, :], S.ones[:, 0:E], blocks[:, :], 0.0, ALU.mult, ALU.add))
                link(tt(starts[:, :], ends[:, :], blocks[:, :], ALU.subtract))
                link(ts(starts[:, :], starts[:, :], float(P), None, ALU.mult))
                link(tt(both[:, :, :], ps_rank[:, :, :], under(starts[:, :], NX, E), ALU.add))
                for n in range(2):
                    link(tt(pick[n][:, :, :], pick[n][:, :, :], both[:, :, :], ALU.mult))
                    link(nc.vector.reduce_sum(dest_f[:, n * NX:(n + 1) * NX], pick[n][:, :, :], AX.X))
                link(nc.vector.tensor_copy(dest[:, :], dest_f[:, :]))
                dve.sem_inc(dest_ready, 1)
                link(tt(cmp[:, :, :], ends[0:1, :].unsqueeze(1).to_broadcast([1, MOE_BLOCKS, E]),
                        S.row[0:1, s0:s0 + MOE_BLOCKS].unsqueeze(2).to_broadcast([1, MOE_BLOCKS, E]), ALU.is_le))
                link(nc.vector.reduce_sum(be_f[:, :], cmp[:, :, :], AX.X))
                link(ts(be_f[:, :], be_f[:, :], float(NE - 1), None, ALU.min))
                link(nc.vector.tensor_copy(block_expert[:, :], be_f[:, :]))


def expert_blocks(nc, S, io, block_expert):
    N = MOE_BLOCKS
    with ExitStack() as ctx, stage(nc, "ids_in0", "ids_in1", "x_in0", "x_in1", "w_in0", "w_in1", "x_turned", "xT_ready",
                                   "h_done", "s_ready", "g_ready", "g_turned", "gT_ready", "y_done", "y_ready", "st0", "st1", "gathers") as (
            ids_in0, ids_in1, x_in0, x_in1, w_in0, w_in1, x_turned, xT_ready, h_done, s_ready, g_ready, g_turned, gT_ready,
            y_done, y_ready, st0, st1, gathers):
        ids_in, x_in, w_in, stored = [ids_in0, ids_in1], [x_in0, x_in1], [w_in0, w_in1], [st0, st1]
        tile = lambda n, shape, dt=F32: [ctx.enter_context(nc.sbuf_tensor(f"{n}{b}", shape, dt)) for b in range(2)]
        ids, x, xT = tile("mo_ids", [P, 1], I32), tile("mo_x", [P, D]), tile("mo_xT", [P, KT, P])
        w13, w2 = tile("mo_w13", [P, KT, 2 * DE]), tile("mo_w2", [P, 2, D])
        s, g, gT, y = tile("mo_s", [P, DE]), tile("mo_g", [P, DE]), tile("mo_gT", [P, 2, P]), tile("mo_y", [P, D])
        ps_x = ctx.enter_context(nc.psum_tensor("ps_mx", [P, KT, P], F32))
        ps_h = [ctx.enter_context(nc.psum_tensor(f"ps_mh{b}", [P, BANK], F32)) for b in range(2)]
        ps_g = ctx.enter_context(nc.psum_tensor("ps_mg", [P, 2, P], F32))
        ps_y = ctx.enter_context(nc.psum_tensor("ps_my", [P, 2, BANK], F32))
        with nc.Block() as block:
            @block.sync
            def _(sp):
                sp.sem_inc(y_done, 2)
                with sp.Fori(0, N // 2) as i:
                    for q in range(2):
                        sp.wait_ge(y_done, 2 * i + q + 1)
                        sp.dma_start(ids[q][:, :], S.slot_dram[bass.ds(i * (2 * P) + q * P, P), :]).then_inc(ids_in[q], 16)
                        e = sp.value_load(block_expert[0:1, bass.ds(2 * i + q, 1)], min_val=0, max_val=NE - 1)
                        for j, n in enumerate(("exp_w1_2", "exp_w3_2")):
                            sp.dma_start(w13[q][:, :, j * DE:(j + 1) * DE], io[n][bass.ds(e, 1), :, :].rearrange(
                                "o (k p) m -> p (o k) m", p=P)).then_inc(w_in[q], 16)
                        sp.dma_start(w2[q][:, :, :], io["exp_w2_2"][bass.ds(e, 1), :, :].rearrange(
                            "o (k p) m -> p (o k) m", p=P)).then_inc(w_in[q], 16)

            @block.gpsimd
            def _(pool):
                with pool.Fori(0, N // 2) as i:
                    for q in range(2):
                        pool.wait_ge(ids_in[q], i * 16 + 16)
                        pool.sem_inc(gathers, 1)
                        nc.gpsimd.indirect_dma_start(out=x[q][:, :], out_offset=None, in_=S.xn_dram, in_offset=
                                                     bass.IndirectOffsetOnAxis(ap=ids[q][:, 0:1], axis=0)).then_inc(x_in[q], 16)

            @block.tensor
            def _(pe):
                def turn_x(b, turn, q):
                    pe.wait_ge(x_in[q], turn * 16 + 16)
                    for k in range(KT):
                        last = nc.tensor.transpose(ps_x[:, k, :], x[q][:, k * P:(k + 1) * P], S.ident)
                    last.then_inc(x_turned, 1)

                def first_product(b, turn, q):
                    pe.wait_ge(w_in[q], turn * 48 + 48)
                    pe.wait_ge(xT_ready, b + 1)
                    for k in range(KT):
                        last = nc.tensor.matmul(ps_h[q][:, :], xT[q][:, k, :], w13[q][:, k, :], start=(k == 0), stop=(k == KT - 1))
                    last.then_inc(h_done, 1)

                def second_product(b, q):
                    pe.wait_ge(g_ready, b + 1)
                    for k in range(2):
                        last = nc.tensor.transpose(ps_g[:, k, :], g[q][:, k * P:(k + 1) * P], S.ident)
                    last.then_inc(g_turned, 1)
                    pe.wait_ge(gT_ready, b + 1)
                    pe.wait_ge(y_ready, b + 1)
                    for c in range(2):
                        for k in range(2):
                            last = nc.tensor.matmul(ps_y[:, c, :], gT[q][:, k, :], w2[q][:, k, c * BANK:(c + 1) * BANK],
                                                    start=(k == 0), stop=(k == 1))
                    last.then_inc(y_done, 1)

                pe.sem_inc(y_ready, 1)
                turn_x(0, 0, 0)
                first_product(0, 0, 0)
                with pe.Fori(0, N // 2 - 1) as i:
                    for j in range(2):
                        b, turn, q = 2 * i + 1 + j, i + j, 1 - j
                        turn_x(b, turn, q)
                        second_product(2 * i + j, j)
                        first_product(b, turn, q)
                turn_x(N - 1, N // 2 - 1, 1)
                second_product(N - 2, 0)
                first_product(N - 1, N // 2 - 1, 1)
                second_product(N - 1, 1)

            @block.scalar
            def _(act):
                def gate(b, q):
                    act.wait_ge(h_done, b + 1)
                    nc.scalar.activation(s[q][:, :], ps_h[q][:, 0:DE], ACT.Silu).then_inc(s_ready, 1)

                def outputs(b, turn, q):
                    act.wait_ge(g_turned, b + 1)
                    nc.scalar.activation(gT[q][:, :, :], ps_g[:, :, :], ACT.Copy).then_inc(gT_ready, 1)
                    act.wait_ge(y_done, b + 3)
                    act.wait_ge(stored[q], turn * 16 + 16)
                    nc.scalar.activation(y[q][:, :], ps_y[:, :, :].rearrange("p a c -> p (a c)"), ACT.Copy).then_inc(y_ready, 1)
                    act.wait_ge(y_ready, b + 2)
                    act.dma_start(S.y_dram[bass.ds(b * P, P), :] if not isinstance(b, int) else
                                  S.y_dram[b * P:(b + 1) * P, :], y[q][:, :]).then_inc(stored[q], 16)

                act.sem_inc(st0, 16)
                act.sem_inc(st1, 16)
                gate(0, 0)
                with act.Fori(0, N // 2 - 1) as i:
                    for j in range(2):
                        outputs(2 * i + j, i, j)
                        gate(2 * i + 1 + j, 1 - j)
                outputs(N - 2, N // 2 - 1, 0)
                gate(N - 1, 1)
                outputs(N - 1, N // 2 - 1, 1)
                act.wait_ge(st0, 16 * (N // 2 + 1))
                act.wait_ge(st1, 16 * (N // 2 + 1))

            @block.vector
            def _(dve):
                with dve.Fori(0, N // 2) as i:
                    for q in range(2):
                        b = 2 * i + q
                        dve.wait_ge(x_turned, b + 1)
                        nc.vector.tensor_copy(xT[q][:, :, :], ps_x[:, :, :]).then_inc(xT_ready, 1)
                        dve.wait_ge(s_ready, b + 1)
                        nc.vector.tensor_tensor(g[q][:, :], s[q][:, :], ps_h[q][:, DE:2 * DE], ALU.mult).then_inc(g_ready, 1)


def combine(nc, S, io, xT, gates, dest):
    with ExitStack() as ctx, stage(nc, "y_in0", "y_in1", "turned", "added", "stored0", "stored1", "chain") as (
            y_in0, y_in1, turned, added, st0, st1, chain):
        y_in, stored = [y_in0, y_in1], [st0, st1]
        ys = [[ctx.enter_context(nc.sbuf_tensor(f"cy{b}{n}", [P, D], F32)) for n in range(2)] for b in range(2)]
        rows = ctx.enter_context(nc.sbuf_tensor("c_rows", [P, 2, D], F32))
        ps = [ctx.enter_context(nc.psum_tensor(f"ps_c{b}", [P, D], F32)) for b in range(2)]
        with nc.Block() as block:
            @block.gpsimd
            def _(pool):
                for t in range(NX):
                    if t >= 2:
                        pool.wait_ge(added, t - 1)
                    for n in range(2):
                        nc.gpsimd.indirect_dma_start(out=ys[t % 2][n][:, :], out_offset=None, in_=S.y_dram, in_offset=
                                                     bass.IndirectOffsetOnAxis(ap=dest[:, n * NX + t:n * NX + t + 1], axis=0)
                                                     ).then_inc(y_in[t % 2], 16)

            @block.tensor
            def _(pe):
                for t in range(NX):
                    if t >= 2:
                        pe.wait_ge(added, t - 1)
                    for k in range(KT):
                        last = nc.tensor.transpose(ps[t % 2][:, k * P:(k + 1) * P], xT[:, k, t * P:(t + 1) * P], S.ident)
                    last.then_inc(turned, 1)

            @block.vector
            def _(dve):
                stt = nc.vector.scalar_tensor_tensor
                link = Chain(dve, chain)
                for t in range(NX):
                    dve.wait_ge(turned, t + 1)
                    dve.wait_ge(y_in[t % 2], 32 * (t // 2 + 1))
                    if t >= 2:
                        dve.wait_ge(stored[t % 2], 16 * (t // 2))
                    row = rows[:, t % 2, :]
                    link(stt(row, ys[t % 2][0][:, :], gates[:, t:t + 1], ps[t % 2][:, :], ALU.mult, ALU.add))
                    stt(row, ys[t % 2][1][:, :], gates[:, NX + t:NX + t + 1], row, ALU.mult, ALU.add).then_inc(added, 1)

            @block.sync
            def _(sp):
                for t in range(NX):
                    sp.wait_ge(added, t + 1)
                    sp.dma_start(io["out"][t * P:(t + 1) * P, :], rows[:, t % 2, :]).then_inc(stored[t % 2], 16)
                sp.wait_ge(st0, 16 * NX // 2)
                sp.wait_ge(st1, 16 * NX // 2)
def build_program(nc, io):
    with ExitStack() as ctx:
        dram = lambda n, shape: nc.dram_tensor(n, shape, F32, kind="Internal").ap()
        tile = lambda n, shape, dt=F32: ctx.enter_context(nc.sbuf_tensor(n, shape, dt))
        S = Shared()
        S.mat, S.vec, S.row = tile("mat", [P, NMAT, P]), tile("vec", [P, NVEC]), tile("row", [P, NROW])
        S.mod, S.fac = tile("mod", [P, 2, 48]), tile("fac", [P, 3, KT])
        S.xT_dram = dram("xT_scratch", (P, KT, T))
        S.z_dram = dram("z_scratch", (NX, P, 2 * GW))
        S.feat_dram = dram("feat_scratch", (SLOTS, P, N_FEAT * P))
        S.tok_dram = dram("tok_scratch", (SLOTS, P, TOK_W))
        S.xn_dram = dram("xn_scratch", (SEQ, D))
        S.y_dram = dram("y_scratch", (MOE_BLOCKS * P, D))
        S.slot_dram = nc.dram_tensor("slot_scratch", (MOE_BLOCKS * P, 1), I32, kind="Internal").ap()
        S.ident, S.ones = S.mat[:, MAT["ident"], :], S.mat[:, MAT["ones"], :]
        vec = lambda n, k=0: S.vec[:, VEC[n][0] + k:VEC[n][0] + k + 1]
        load_constants(nc, S, io)
        modulation(nc, S, io)
        with ExitStack() as mixer:
            convT = mixer.enter_context(nc.sbuf_tensor("convT", [P, NCONV, T], F32))
            small = mixer.enter_context(nc.sbuf_tensor("small", [P, NT, 2, NSMALL], F32))
            chunks = chunks_of(T, CTX)
            with nc.sbuf_tensor("hT", [P, KT, T], F32) as hT:
                xT = convT[:, 0:KT, :]
                load_transposed(nc, S, io, xT)
                piece = lambda a: lambda c, k: a[:, k, chunks[c][0]:chunks[c][0] + chunks[c][1]]
                rms_features(nc, S, "n1", piece(xT), piece(hT), KT, [n for _, n in chunks],
                             lambda c, k: S.fac[:, 1 if c == 0 else 0, k:k + 1],
                             lambda c, k: S.mod[:, 1 if c == 0 else 0, k:k + 1])
                store_dram(nc, [(S.xT_dram, xT)])
                token_projections(nc, S, io, hT, small)
                conv_projection(nc, S, "qkv", io["w_in"][:, IN_QKV:IN_QKV + NQKV * P], NQKV, hT, convT, 0,
                                VEC["gdn_conv_w"][0], None)
                conv_projection(nc, S, "xbc", io["w_in"][:, IN_XBC:IN_XBC + NXBC * P], NXBC, hT, convT, NQKV,
                                VEC["ssm_conv_w"][0], VEC["ssm_conv_b"][0])
            parts = [(m, at, n) for m in range(2 * GH) for at, n in chunks]
            part = lambda c, k: convT[:, parts[c][0], parts[c][1]:parts[c][1] + parts[c][2]]
            rms_features(nc, S, "l2", part, part, 1, [n for _, _, n in parts],
                         lambda c, k: P ** -0.5 if parts[c][0] < GH else 1.0, divisor=1)
            pack_tiles(nc, S, convT, small)
        chunks = chunks_of(SEQ)
        piece = lambda a: lambda c, k: a[:, k, c * BANK:(c + 1) * BANK]
        pieces = [BANK] * (SEQ // BANK)
        acc = tile("acc", [P, SLOTS, 2 * GW])
        recurrences(nc, S, acc)
        xT, spare = acc[:, 0:KT, :], acc[:, KT:SLOTS, :]
        with nc.sbuf_tensor("mixT", [P, KT, SEQ], F32) as mixT:
            gate_mix(nc, S, acc, mixT)
            load_dram(nc, [(xT, S.xT_dram[:, :, CTX:T])])
            residual_linear(nc, S, "wout", io["w_out"], mixT, xT, lambda m: S.mod[:, 0, 16 + m:17 + m])
        with ExitStack() as ffn:
            guT = ffn.enter_context(nc.sbuf_tensor("guT", [P, FT, SEQ], F32))
            with nc.sbuf_tensor("hT_ffn", [P, KT, SEQ], F32) as hT:
                rms_features(nc, S, "n2", piece(xT), piece(hT), KT, pieces, lambda c, k: S.fac[:, 2, k:k + 1],
                             lambda c, k: S.mod[:, 0, 24 + k:25 + k])
                gated_unit(nc, S, io, hT, guT, spare)
            residual_linear(nc, S, "wdown", io["ffn_w_down"], guT, xT, lambda m: S.mod[:, 0, 40 + m:41 + m])
        rms_features(nc, S, "nf", piece(xT), piece(xT), KT, pieces, lambda c, k: vec("final_norm_g", k))
        with ExitStack() as second:
            big = lambda n: second.enter_context(nc.sbuf_tensor(n, [P, KT, SEQ], F32))
            uT, oT = big("uT"), big("oT")
            rms_features(nc, S, "n1b", piece(xT), piece(uT), KT, pieces, lambda c, k: vec("norm1_g_2", k))
            with ExitStack() as mla:
                lat = spare
                k_pe, cos, sin = [mla.enter_context(nc.sbuf_tensor(n, [P, SEQ], F32)) for n in ("k_pe", "cos", "sin")]
                rotary_tables(nc, S, io, cos, sin)
                latent_projections(nc, S, io, uT, lat, k_pe)
                for first, g in ((0, "q_norm_g_2"), (LT, "kv_norm_g_2")):
                    part = piece(lat[:, first:first + LT, :])
                    rms_features(nc, S, g, part, part, LT, pieces, lambda c, k: vec(g, k))
                qk = mla.enter_context(nc.sbuf_tensor("qk", [P, 2, 4, SEQ], F32))
                v = mla.enter_context(nc.sbuf_tensor("v", [P, NX, 2 * DV], F32))
                for h0 in range(0, NH, 2):
                    head_projections(nc, S, io, h0, lat, qk, v)
                    units = [(h, w, c) for h in range(2) for w in range(2) for c in range(2)]
                    rows = (P, ROPE)
                    place = lambda u, k: qk[0:rows[k], units[u][0], 2 * units[u][1] + k,
                                            units[u][2] * BANK:(units[u][2] + 1) * BANK]
                    before = lambda u, k: (k_pe[0:ROPE, units[u][2] * BANK:(units[u][2] + 1) * BANK]
                                           if k == 1 and units[u][1] == 1 else place(u, k))
                    gain = lambda u, k: vec(("q_g_", "k_g_")[units[u][1]] + ("nope", "rope")[k])[0:rows[k], :]
                    rms_features(nc, S, f"qk{h0}", before, place, 2, [BANK] * len(units), gain, divisor=QK)
                    rotate(nc, S, h0, [qk[0:ROPE, h, w, :] for h in range(2) for w in (1, 3)], cos, sin)
                    attention(nc, S, h0, qk, v, oT)
            merged = big("merged")
            gate_b = io["w_in_2"][:, IN2_GB:IN2_GB + D]
            gated_linear(nc, S, "mla", gate_b, uT, io["w_mla_o_2"], oT, merged, add=False)
            xr = oT
            causal_projection(nc, S, io, uT, xr)
            recurrent_unit(nc, S, io, xr)
            gelu_projection(nc, S, io, uT, xr)
            gate_a = io["w_in_2"][:, IN2_GA:IN2_GA + D]
            gated_linear(nc, S, "rnn", gate_a, uT, io["w_rnn_o_2"], xr, merged, add=True)
            residual_linear(nc, S, "wout2", io["w_out_2"], merged, xT, None)
        gates, dest = tile("gates", [P, 2 * NX]), tile("dest", [P, 2 * NX], U32)
        block_expert = tile("block_expert", [1, MOE_BLOCKS], I32)
        with nc.sbuf_tensor("xnT", [P, KT, SEQ], F32) as xnT:
            rms_features(nc, S, "n2b", piece(xT), piece(xnT), KT, pieces, lambda c, k: vec("norm2_g_2", k))
            store_rows(nc, S, "xn", xnT, S.xn_dram)
            route(nc, S, io, xnT, gates, dest, block_expert)
        expert_blocks(nc, S, io, block_expert)
        combine(nc, S, io, xT, gates, dest)


def load_dram(nc, pairs):
    with stage(nc, "brought") as (brought,):
        with nc.Block() as block:
            @block.sync
            def _(sp):
                for out, src in pairs:
                    sp.dma_start(out, src).then_inc(brought, 16)
                sp.wait_ge(brought, 16 * len(pairs))


def store_dram(nc, pairs):
    with stage(nc, "kept") as (kept,):
        with nc.Block() as block:
            @block.sync
            def _(sp):
                for out, src in pairs:
                    sp.dma_start(out, src).then_inc(kept, 16)
                sp.wait_ge(kept, 16 * len(pairs))


def _columns(a):
    return a.reshape(-1, P).T


def _constants():
    i, j = np.arange(P)[:, None], np.arange(P)[None, :]
    m = np.zeros((NMAT, P, P), np.float32)
    m[MAT["ident"]] = i == j
    m[MAT["ones"]] = 1
    m[MAT["tri0"]] = i <= j
    m[MAT["tri1"]] = i >= j
    m[MAT["neg0"]] = np.where(i <= j, 0, -1e30)
    m[MAT["neg1"]] = np.where(i >= j, 0, -1e30)
    m[MAT["before"]] = i < j
    half = ROPE // 2
    m[MAT["rope"]] = np.where((j < half) & (i == j + half), -1, 0) + np.where((j >= half) & (j < ROPE) & (i == j - half), 1, 0)
    for level in range(7):
        n = 1 << level
        low = (i // (2 * n) == j // (2 * n)) & (i // n % 2 == 1) & (j // n % 2 == 0)
        m[MAT[f"lvl0_{level}"]] = low
        m[MAT[f"lvl1_{level}"]] = low.T
    return np.ascontiguousarray(m.transpose(1, 0, 2))


def _layout(a):
    f = lambda n: np.asarray(a[n])[0]
    vec = {n: _columns(f(n)) for n in ("b_ada", "norm1_g", "norm2_g", "gdn_norm_g", "ssm_norm_g", "ffn_conv_b",
                                       "norm1_g_2", "conv_b_2", "lru_ba_2", "lru_bx_2", "lru_lambda_2", "q_norm_g_2",
                                       "kv_norm_g_2", "norm2_g_2", "ssm_conv_b")}
    vec["c"] = _columns(np.asarray(a["c"])[0])
    vec["c_ctx"] = _columns(np.asarray(a["c_ctx"]))
    vec["final_norm_g"] = _columns(np.asarray(a["final_norm_g"]))
    for n in ("gdn_conv_w", "ssm_conv_w", "ffn_conv_w", "conv_w_2"):
        vec[n] = _columns(f(n).reshape(-1))
    for n, to in (("qk_norm_q_g_2", "q_g"), ("qk_norm_k_g_2", "k_g")):
        vec[to + "_nope"] = f(n)[:NOPE, None]
        vec[to + "_rope"] = np.concatenate([f(n)[NOPE:], np.zeros(P - ROPE, np.float32)])[:, None]
    vec["eps"] = np.full((P, 1), EPS, np.float32)
    freq = (10000.0 ** (-np.arange(0, ROPE, 2, dtype=np.float32) / ROPE)).astype(np.float32)
    vec["inv_freq"] = np.tile(freq, P // len(freq))[:, None]
    vecs = np.zeros((P, NVEC), np.float32)
    for n, (at, w) in VEC.items():
        vecs[:, at:at + w] = vec[n]
    row = {n: f(n).reshape(-1) for n in ("gdn_dt_bias", "ssm_dt_bias", "gdn_A_log", "ssm_A_log", "ssm_D")}
    row["router_b"] = np.concatenate([f("router_bg_2"), f("router_be_2")])
    row["expert_iota"] = np.arange(NE, dtype=np.float32)
    row["block_start"] = np.arange(MOE_BLOCKS, dtype=np.float32)
    rows = np.zeros((1, NROW), np.float32)
    for n, (at, w) in ROW.items():
        rows[0, at:at + w] = row[n]
    w_in = f("w_in")
    out = dict(mats=_constants(), vecs=vecs, rows=rows, x=f("x"), ctx=f("ctx"), w_ada=f("w_ada"), w_in=w_in,
               w_small=np.concatenate([w_in[:, IN_AB:IN_AB + 16], w_in[:, IN_DT:IN_DT + 16]], axis=1),
               positions=np.asarray(a["positions_2"]).astype(np.int32),
               router_w=np.concatenate([f("router_wg_2"), f("router_we_2")], axis=1))
    for n in ("w_out", "ffn_w_gate", "ffn_w_up", "ffn_w_down", "w_in_2", "lru_wa_2", "lru_wx_2", "w_rnn_o_2", "w_uq_2",
              "w_ukv_2", "w_mla_o_2", "w_out_2", "exp_w1_2", "exp_w3_2", "exp_w2_2"):
        out[n] = f(n)
    return {n: np.ascontiguousarray(v) for n, v in out.items()}


def kernel(**inputs):
    import concourse.bacc as bacc
    from concourse.bass_utils import run_bass_kernel_spmd

    nc = bacc.Bacc("TRN2", target_bir_lowering=False, num_devices=1)
    arrays = {f"in_{n}_dram": v for n, v in _layout(inputs).items()}
    io = {n[3:-5]: nc.dram_tensor(n, v.shape, mybir.dt.from_np(v.dtype), kind="ExternalInput").ap()
          for n, v in arrays.items()}
    io["out"] = nc.dram_tensor("out_0_dram", (SEQ, D), F32, kind="ExternalOutput").ap()
    build_program(nc, io)
    result = run_bass_kernel_spmd(nc, [arrays], core_ids=[0])
    return result.results[0]["out_0_dram"].reshape(1, SEQ, D)
```

```python
import numpy as np
from contextlib import ExitStack, contextmanager

import concourse.bass as bass
from concourse import mybir
from concourse.alu_op_type import AluOpType as ALU

F32 = mybir.dt.float32
I32 = mybir.dt.int32
U32 = mybir.dt.uint32
ACT = mybir.ActivationFunctionType
AX = mybir.AxisListType

P = 128
BANK = 512
D = 1024
KT = D // P
SEQ, CTX = 1024, 256
NX, NC = SEQ // P, CTX // P
NT = NX + NC
T = SEQ + CTX
EPS = 1e-6

GH, SH, SG = 4, 8, 2
SP = 64
GW = GH * P
IN_QKV, IN_ZG, IN_AB, IN_ZS, IN_XBC, IN_DT = 0, 1536, 2048, 2064, 2576, 3600
NQKV, NXBC = 12, 8
NCONV = NQKV + NXBC
DFF = 2816
FT = DFF // P
GRID = 64

NH, NOPE, ROPE, DV = 8, 128, 64, 128
QK = NOPE + ROPE
LORA = 256
LT = LORA // P
NG, EPG = 8, 8
NE = NG * EPG
DE = 256
MOE_BLOCKS = 2 * SEQ // P + NE

VEC = {}
_n = 0
for _name, _w in [("c", 8), ("c_ctx", 8), ("b_ada", 48), ("norm1_g", 8), ("norm2_g", 8), ("final_norm_g", 8),
                  ("gdn_conv_w", 36), ("ssm_conv_w", 24), ("ssm_conv_b", 8), ("gdn_norm_g", 1), ("ssm_norm_g", 4),
                  ("ffn_conv_w", 9 * FT), ("ffn_conv_b", FT), ("norm1_g_2", 8), ("conv_w_2", 32), ("conv_b_2", 8),
                  ("lru_ba_2", 8), ("lru_bx_2", 8), ("lru_lambda_2", 8), ("q_norm_g_2", 2), ("kv_norm_g_2", 2),
                  ("q_g_nope", 1), ("q_g_rope", 1), ("k_g_nope", 1), ("k_g_rope", 1), ("norm2_g_2", 8),
                  ("eps", 1), ("inv_freq", 1)]:
    VEC[_name] = (_n, _w)
    _n += _w
NVEC = _n

ROW = {}
_n = 0
for _name, _w in [("gdn_dt_bias", 8), ("ssm_dt_bias", 16), ("gdn_A_log", 8), ("ssm_A_log", 16), ("ssm_D", 8),
                  ("router_b", NG + NE), ("expert_iota", NE), ("block_start", MOE_BLOCKS)]:
    ROW[_name] = (_n, _w)
    _n += _w
NROW = _n

MAT = {n: i for i, n in enumerate(
    ["ident", "ones", "tri0", "tri1", "neg0", "neg1", "before", "rope"] + [f"lvl{d}_{l}" for d in range(2) for l in range(7)])}
NMAT = len(MAT)


class Shared:
    pass


class Chain:

    def __init__(self, eng, sem, base=0):
        self.eng, self.sem, self.base, self.n = eng, sem, base, 0

    def __call__(self, instruction):
        instruction.then_inc(self.sem, 1)
        self.n += 1
        self.eng.wait_ge(self.sem, self.base + self.n)


STAGE_NUMBERS = iter(range(1 << 30))


@contextmanager
def stage(nc, *names):
    number = next(STAGE_NUMBERS)
    sems = [nc.alloc_semaphore(f"{n}_s{number}") for n in names]
    yield sems
    nc.clear_and_free_semaphores(sems)
    nc.all_engine_barrier(sem_only=True)


def chunks_of(total, first=0):
    out = [(0, first)] if first else []
    at = first
    while at < total:
        out.append((at, min(BANK, total - at)))
        at += out[-1][1]
    return out


def load_constants(nc, S, io):
    with stage(nc, "consts_in") as (consts_in,):
        with nc.Block() as block:
            @block.sync
            def _(sp):
                sp.dma_start(S.mat[:, :, :], io["mats"]).then_inc(consts_in, 16)
                sp.dma_start(S.vec[:, :], io["vecs"]).then_inc(consts_in, 16)
                sp.dma_start(S.row[:, :], io["rows"].partition_broadcast(P)).then_inc(consts_in, 16)
                sp.wait_ge(consts_in, 48)


def modulation(nc, S, io):
    GROUP = BANK
    PAIRS = 6 * D // GROUP // 2
    with ExitStack() as ctx, stage(nc, "w_in0", "w_in1", "w_used0", "w_used1", "copied", "silu_done", "turned", "chain") as (
            w_in0, w_in1, w_used0, w_used1, copied, silu_done, turned, chain):
        w_in, w_used = [w_in0, w_in1], [w_used0, w_used1]
        w = [ctx.enter_context(nc.sbuf_tensor(f"ada{b}", [P, KT, GROUP], F32)) for b in range(2)]
        sc = ctx.enter_context(nc.sbuf_tensor("silu_c", [P, KT, 2], F32))
        rows = ctx.enter_context(nc.sbuf_tensor("mod_rows", [2, 6 * D], F32))
        ps_row = [ctx.enter_context(nc.psum_tensor(f"ps_row{b}", [2, GROUP], F32)) for b in range(2)]
        ps = ctx.enter_context(nc.psum_tensor("ps_mod", [P, 48, 2], F32))
        view = io["w_ada"].rearrange("(k p) m -> p k m", p=P)
        with nc.Block() as block:
            @block.sync
            def _(sp):
                sp.sem_inc(w_used0, 1)
                sp.sem_inc(w_used1, 1)
                with sp.Fori(0, PAIRS) as i:
                    for b in range(2):
                        sp.wait_ge(w_used[b], i + 1)
                        sp.dma_start(w[b][:, :, :], view[:, :, bass.ds((i * 2 + b) * GROUP, GROUP)]).then_inc(w_in[b], 16)

            @block.scalar
            def _(act):
                c0, _w = VEC["c"]
                nc.scalar.activation(sc[:, :, 0], S.vec[:, c0:c0 + KT], ACT.Silu).then_inc(silu_done, 1)
                nc.scalar.activation(sc[:, :, 1], S.vec[:, c0 + KT:c0 + 2 * KT], ACT.Silu).then_inc(silu_done, 1)

            @block.tensor
            def _(pe):
                pe.wait_ge(silu_done, 2)
                pe.sem_inc(copied, 2)
                with pe.Fori(0, PAIRS) as i:
                    for b in range(2):
                        pe.wait_ge(w_in[b], i * 16 + 16)
                        pe.wait_ge(copied, i * 2 + b + 1)
                        for k in range(KT):
                            last = nc.tensor.matmul(ps_row[b][:, :], sc[:, k, :], w[b][:, k, :],
                                                    start=(k == 0), stop=(k == KT - 1))
                        last.then_inc(w_used[b], 1)
                pe.wait_ge(copied, 2 * PAIRS + 2)
                for m in range(48):
                    last = nc.tensor.transpose(ps[:, m, :], rows[:, m * P:(m + 1) * P], S.ident[0:2, 0:2])
                last.then_inc(turned, 1)

            @block.vector
            def _(dve):
                link = Chain(dve, chain)
                for g in range(2 * PAIRS):
                    dve.wait_ge(w_used[g % 2], g // 2 + 2)
                    nc.vector.tensor_copy(rows[:, g * GROUP:(g + 1) * GROUP], ps_row[g % 2][:, :]).then_inc(copied, 1)
                b0, _w = VEC["b_ada"]
                dve.wait_ge(turned, 1)
                for t in range(2):
                    link(nc.vector.tensor_tensor(S.mod[:, t, :], ps[:, :, t], S.vec[:, b0:b0 + 48], ALU.add))
                for t, at, g, to in ((0, 8, "norm1_g", 0), (1, 8, "norm1_g", 1), (0, 32, "norm2_g", 2)):
                    g0, _w = VEC[g]
                    link(nc.vector.scalar_tensor_tensor(S.fac[:, to, :], S.mod[:, t, at:at + KT], 1.0,
                                                        S.vec[:, g0:g0 + KT], ALU.add, ALU.mult))


def load_transposed(nc, S, io, xT):
    with ExitStack() as ctx, stage(nc, "rows_in0", "rows_in1", "transposed", "evacuated") as (in0, in1, transposed, evacuated):
        rows_in = [in0, in1]
        rows = [ctx.enter_context(nc.sbuf_tensor(f"rows{b}", [P, D], F32)) for b in range(2)]
        ps = [ctx.enter_context(nc.psum_tensor(f"ps_t{b}", [P, KT, P], F32)) for b in range(2)]
        with nc.Block() as block:
            @block.sync
            def _(sp):
                for t in range(NT):
                    if t >= 2:
                        sp.wait_ge(transposed, t - 1)
                    src = io["ctx"][t * P:(t + 1) * P, :] if t < NC else io["x"][(t - NC) * P:(t - NC + 1) * P, :]
                    sp.dma_start(rows[t % 2][:, :], src).then_inc(rows_in[t % 2], 16)

            @block.tensor
            def _(pe):
                for t in range(NT):
                    pe.wait_ge(rows_in[t % 2], 16 * (t // 2 + 1))
                    if t >= 2:
                        pe.wait_ge(evacuated, t - 1)
                    for k in range(KT):
                        last = nc.tensor.transpose(ps[t % 2][:, k, :], rows[t % 2][:, k * P:(k + 1) * P], S.ident)
                    last.then_inc(transposed, 1)

            @block.vector
            def _(dve):
                for t in range(NT):
                    dve.wait_ge(transposed, t + 1)
                    nc.vector.tensor_copy(xT[:, :, t * P:(t + 1) * P], ps[t % 2][:, :, :]).then_inc(evacuated, 1)


def rms_features(nc, S, tag, src, dst, kt, sizes, mul, add=None, divisor=None, moves=(), on_pool=None):
    n_c, w = len(sizes), max(sizes)
    divisor = divisor or kt * P
    e0, _w = VEC["eps"]
    with ExitStack() as ctx, stage(nc, "squared", "sq_used", "rooted", "scaled", "chain", "moved", "inverted") as (
            squared, sq_used, rooted, scaled, chain, moved, inverted):
        sq = ctx.enter_context(nc.sbuf_tensor(f"sq_{tag}", [P, 4, w], F32))
        root = ctx.enter_context(nc.sbuf_tensor(f"root_{tag}", [P, 2, w], F32))
        rinv = ctx.enter_context(nc.sbuf_tensor(f"rinv_{tag}", [P, 2, w], F32))
        ps = [ctx.enter_context(nc.psum_tensor(f"ps_{tag}{b}", [P, BANK], F32)) for b in range(2)]
        with nc.Block() as block:
            @block.gpsimd
            def _(pool):
                for c in range(n_c if on_pool is None else on_pool, n_c):
                    pool.wait_ge(inverted, c - on_pool + 1)
                    nc.gpsimd.tensor_tensor(dst(c, 0), src(c, 0), rinv[:, c % 2, 0:sizes[c]], ALU.mult).then_inc(scaled, 1)

            @block.sync
            def _(sp):
                for to, source in moves:
                    sp.dma_start(to, source).then_inc(moved, 16)
                if moves:
                    sp.wait_ge(moved, 16 * len(moves))

            @block.scalar
            def _(act):
                def root_of(c):
                    act.wait_ge(sq_used, (c + 1) * kt)
                    if c >= 2:
                        act.wait_ge(scaled, c - 1)
                    n = sizes[c]
                    nc.scalar.activation(root[:, c % 2, 0:n], ps[c % 2][:, 0:n], ACT.Sqrt, bias=S.vec[:, e0:e0 + 1],
                                         scale=1.0 / divisor).then_inc(rooted, 1)

                for c, n in enumerate(sizes):
                    for k in range(kt):
                        j = c * kt + k
                        if j >= 4:
                            act.wait_ge(sq_used, j - 3)
                        rows = src(c, k).shape[0]
                        nc.scalar.activation(sq[0:rows, j % 4, 0:n], src(c, k), ACT.Square).then_inc(squared, 1)
                    if c >= 1:
                        root_of(c - 1)
                root_of(n_c - 1)

            @block.tensor
            def _(pe):
                for c, n in enumerate(sizes):
                    if c >= 2:
                        pe.wait_ge(rooted, c - 1)
                    for k in range(kt):
                        j = c * kt + k
                        pe.wait_ge(squared, j + 1)
                        rows = src(c, k).shape[0]
                        last = nc.tensor.matmul(ps[c % 2][:, 0:n], S.ones[0:rows, :], sq[0:rows, j % 4, 0:n], start=(k == 0),
                                                stop=(k == kt - 1))
                        last.then_inc(sq_used, 1)

            @block.vector
            def _(dve):
                link = Chain(dve, chain)
                for c, n in enumerate(sizes):
                    dve.wait_ge(rooted, c + 1)
                    if on_pool is not None and c >= on_pool:
                        dve.wait_ge(scaled, c - 1)
                        nc.vector.reciprocal(rinv[:, c % 2, 0:n], root[:, c % 2, 0:n]).then_inc(inverted, 1)
                        continue
                    link(nc.vector.reciprocal(rinv[:, c % 2, 0:n], root[:, c % 2, 0:n]))
                    for k in range(kt):
                        last = nc.vector.scalar_tensor_tensor(dst(c, k), src(c, k), mul(c, k),
                                                              rinv[0:dst(c, k).shape[0], c % 2, 0:n], ALU.mult, ALU.mult)
                        if k == kt - 1 and add is not None:
                            link(last)
                    if add is not None:
                        for k in range(kt):
                            last = nc.vector.tensor_scalar(dst(c, k), dst(c, k), add(c, k), None,
                                                           ALU.add)
                    last.then_inc(scaled, 1)


def load_weights(nc, sp, iters, unroll, w, w_in, tile_done, view):
    sp.sem_inc(tile_done, len(w))
    with sp.Fori(0, iters) as i:
        for b in range(unroll):
            sp.wait_ge(tile_done, i * unroll + b + 1)
            sp.dma_start(w[b % len(w)][:, :, :], view(i, b)).then_inc(w_in[b % len(w)], 16)


def multiply_tiles(nc, pe, iters, unroll, w, w_in, tile_done, src, chunks, ps, ps_free):
    turns = unroll // len(w)
    pe.sem_inc(ps_free, len(ps))
    with pe.Fori(0, iters) as i:
        for b in range(unroll):
            pe.wait_ge(w_in[b % len(w)], (i * turns + b // len(w)) * 16 + 16)
            pe.wait_ge(ps_free, i * unroll + b + 1)
            kt = w[0].shape[1]
            for c, (at, n) in enumerate(chunks):
                for k in range(kt):
                    last = nc.tensor.matmul(ps[b % len(ps)][:, c, 0:n], w[b % len(w)][:, k, :], src(b)[:, k, at:at + n],
                                            start=(k == 0), stop=(k == kt - 1))
            last.then_inc(tile_done, 1)


def linear_stage_buffers(nc, ctx, tag, kt, n_buf, banks, sets=2):
    w = [ctx.enter_context(nc.sbuf_tensor(f"w_{tag}{b}", [P, kt, P], F32)) for b in range(n_buf)]
    ps = [ctx.enter_context(nc.psum_tensor(f"ps_{tag}{b}", [P, banks, BANK], F32)) for b in range(sets)]
    return w, ps


def feature_tiles(w_dram):
    return w_dram.rearrange("(k p) m -> p k m", p=P)


def conv_projection(nc, S, tag, w_dram, n_tiles, hT, convT, first, cw, cb):
    n_buf, iters = 4, n_tiles // 4
    chunks = chunks_of(T, CTX)
    pads = [1, 2, 2]
    W2 = T + 3
    with ExitStack() as ctx, stage(nc, *[f"w_in{b}" for b in range(4)],
                                   "ps_free", "tile_done", "convolved", "activated", "chain", "zeroed") as sems:
        w_in = sems[0:4]
        ps_free, tile_done, convolved, activated, chain, zeroed = sems[4:]
        w, ps = linear_stage_buffers(nc, ctx, tag, KT, n_buf, 3)
        raw = ctx.enter_context(nc.sbuf_tensor(f"raw_{tag}", [P, 2, W2], F32))
        con = ctx.enter_context(nc.sbuf_tensor(f"con_{tag}", [P, 2, W2], F32))
        with nc.Block() as block:
            @block.sync
            def _(sp):
                load_weights(nc, sp, iters, n_buf, w, w_in, tile_done,
                             lambda i, b: feature_tiles(w_dram)[:, :, bass.ds((i * n_buf + b) * P, P)])

            @block.tensor
            def _(pe):
                multiply_tiles(nc, pe, iters, n_buf, w, w_in, tile_done, lambda b: hT, chunks, ps, ps_free)

            @block.scalar
            def _(act):
                act.wait_ge(zeroed, 1)
                for m in range(n_tiles + 1):
                    if m < n_tiles:
                        act.wait_ge(tile_done, n_buf + m + 1)
                        if m >= 2:
                            act.wait_ge(convolved, m - 1)
                        for c, (at, n) in enumerate(chunks):
                            last = nc.scalar.activation(raw[:, m % 2, at + pads[c]:at + pads[c] + n],
                                                        ps[m % 2][:, c, 0:n], ACT.Copy)
                        last.then_inc(ps_free, 1)
                    if m >= 1:
                        j = m - 1
                        act.wait_ge(convolved, j + 1)
                        bias = 0.0 if cb is None else S.vec[:, cb + j:cb + j + 1]
                        nc.scalar.activation(convT[:, first + j, 0:CTX], con[:, j % 2, 1:1 + CTX], ACT.Silu, bias=bias)
                        nc.scalar.activation(convT[:, first + j, CTX:T], con[:, j % 2, CTX + 2:T + 2], ACT.Silu,
                                             bias=bias).then_inc(activated, 1)

            @block.vector
            def _(dve):
                link = Chain(dve, chain)
                link(nc.vector.memset(raw[:, :, :], 0.0))
                dve.sem_inc(zeroed, 1)
                for m in range(n_tiles):
                    dve.wait_ge(ps_free, m + 3)
                    if m >= 2:
                        dve.wait_ge(activated, m - 1)
                    row, out = raw[:, m % 2, :], con[:, m % 2, 1:W2 - 1]
                    tap = lambda j: S.vec[:, cw + j * n_tiles + m:cw + j * n_tiles + m + 1]
                    link(nc.vector.tensor_scalar(out, row[:, 1:W2 - 1], tap(1), None, ALU.mult))
                    link(nc.vector.scalar_tensor_tensor(out, row[:, 0:W2 - 2], tap(0), out, ALU.mult, ALU.add))
                    nc.vector.scalar_tensor_tensor(out, row[:, 2:W2], tap(2), out, ALU.mult, ALU.add).then_inc(convolved, 1)
C_G, C_DA, C_BETA, C_DT, NSMALL = 0, 4, 12, 16, 24
N_FEAT = 12
N_TOK = 14
TOK_W = N_TOK * P + 2 * NSMALL
SLOTS = NT + NC
STEPS = NT


def over(ap, shape):
    return ap.unsqueeze(2).to_broadcast(shape)


def under(ap, n, m):
    return ap.unsqueeze(1).to_broadcast([P, n, m])


def token_projections(nc, S, hT, small, wz, ws):
    with ExitStack() as ctx, stage(nc, "z_full", "z_active", "z_stored0", "z_stored1", "small_full",
                                   "act_done", "chain") as (
            z_full, z_active, st0, st1, small_full, act_done, chain):
        stored = [st0, st1]
        zt = ctx.enter_context(nc.sbuf_tensor("z_rows", [P, 2, 2 * GW], F32))
        t = {n: ctx.enter_context(nc.sbuf_tensor(f"sp_{n}", [P, NT, 2, 12], F32)) for n in ("u", "m", "e", "q", "z", "z2", "p")}
        neg_a = ctx.enter_context(nc.sbuf_tensor("neg_a", [P, 2, 12], F32))
        ps = [ctx.enter_context(nc.psum_tensor(f"ps_z{b}", [P, 2, BANK], F32)) for b in range(2)]
        pss = ctx.enter_context(nc.psum_tensor("ps_small", [P, NT, 32], F32))
        flat = lambda n: t[n][:, :, :, :].rearrange("p t d h -> p (t d h)")
        with nc.Block() as block:
            @block.sync
            def _(sp):
                for n in range(NX):
                    sp.wait_ge(z_active, n + 1)
                    sp.dma_start(S.z_dram[n], zt[:, n % 2, :]).then_inc(stored[n % 2], 16)
                sp.wait_ge(st0, 16 * NX // 2)
                sp.wait_ge(st1, 16 * NX // 2)

            @block.tensor
            def _(pe):
                for n in range(NT):
                    for k in range(KT):
                        last = nc.tensor.matmul(pss[:, n, :], hT[:, k, n * P:(n + 1) * P], ws[:, k, :],
                                                start=(k == 0), stop=(k == KT - 1))
                last.then_inc(small_full, 1)
                for n in range(NX):
                    if n >= 2:
                        pe.wait_ge(z_active, n - 1)
                    for g in range(2):
                        for k in range(KT):
                            last = nc.tensor.matmul(ps[n % 2][:, g, :], hT[:, k, (NC + n) * P:(NC + n + 1) * P],
                                                    wz[:, k, g * GW:(g + 1) * GW], start=(k == 0), stop=(k == KT - 1))
                    last.then_inc(z_full, 1)

            @block.scalar
            def _(act):
                act.wait_ge(chain, 4)
                nc.scalar.activation(flat("e"), flat("e"), ACT.Exp).then_inc(act_done, 1)
                r0, _w = ROW["gdn_A_log"]
                r1, _w = ROW["ssm_A_log"]
                nc.scalar.activation(neg_a[:, :, 0:GH], S.row[:, r0:r0 + 8].rearrange("p (d h) -> p d h", d=2), ACT.Exp)
                nc.scalar.activation(neg_a[:, :, GH:12], S.row[:, r1:r1 + 16].rearrange("p (d h) -> p d h", d=2),
                                     ACT.Exp).then_inc(act_done, 1)
                for d in range(2):
                    last = nc.scalar.activation(small[:, :, d, C_BETA:C_BETA + GH], pss[:, :, 8 + 4 * d:12 + 4 * d], ACT.Sigmoid)
                last.then_inc(act_done, 1)
                for n in range(NX):
                    act.wait_ge(z_full, n + 1)
                    if n >= 2:
                        act.wait_ge(stored[n % 2], 16 * (n // 2))
                    nc.scalar.activation(zt[:, n % 2, :].rearrange("p (g c) -> p g c", g=2), ps[n % 2][:, :, :],
                                         ACT.Silu).then_inc(z_active, 1)

            @block.vector
            def _(dve):
                link = Chain(dve, chain)
                dve.wait_ge(small_full, 1)
                r0, _w = ROW["gdn_dt_bias"]
                r1, _w = ROW["ssm_dt_bias"]
                for d in range(2):
                    nc.vector.tensor_tensor(t["u"][:, :, d, 0:GH], pss[:, :, 4 * d:4 * d + 4],
                                            under(S.row[:, r0 + 4 * d:r0 + 4 * d + 4], NT, GH), ALU.add)
                    last = nc.vector.tensor_tensor(t["u"][:, :, d, GH:12], pss[:, :, 16 + 8 * d:24 + 8 * d],
                                                   under(S.row[:, r1 + 8 * d:r1 + 8 * d + 8], NT, SH), ALU.add)
                    link(last)
                link(nc.vector.tensor_scalar(flat("m"), flat("u"), 0.0, None, ALU.max))
                link(nc.vector.scalar_tensor_tensor(flat("e"), flat("m"), -2.0, flat("u"), ALU.mult, ALU.add))
                dve.wait_ge(act_done, 3)
                log1p_series(nc, link, flat)
                link(nc.vector.scalar_tensor_tensor(flat("u"), flat("z2"), 2.0, flat("m"), ALU.mult, ALU.add))
                for d in range(2):
                    nc.vector.tensor_copy(small[:, :, d, C_DT:C_DT + SH], t["u"][:, :, d, GH:12])
                    link(nc.vector.scalar_tensor_tensor(small[:, :, d, 0:12], t["u"][:, :, d, :], -1.0,
                                                        under(neg_a[:, d, :], NT, 12), ALU.mult, ALU.mult))


def log1p_series(nc, link, flat):
    link(nc.vector.tensor_scalar(flat("q"), flat("e"), 2.0, None, ALU.add))
    link(nc.vector.reciprocal(flat("q"), flat("q")))
    link(nc.vector.tensor_tensor(flat("z"), flat("e"), flat("q"), ALU.mult))
    link(nc.vector.tensor_tensor(flat("z2"), flat("z"), flat("z"), ALU.mult))
    link(nc.vector.tensor_scalar(flat("p"), flat("z2"), 1.0 / 15, None, ALU.mult))
    for c in (13, 11, 9, 7, 5, 3):
        link(nc.vector.scalar_tensor_tensor(flat("p"), flat("p"), 1.0 / c, flat("z2"), ALU.add, ALU.mult))
    link(nc.vector.scalar_tensor_tensor(flat("z2"), flat("p"), 1.0, flat("z"), ALU.add, ALU.mult))


def pack_tiles(nc, S, convT, small):
    with ExitStack() as ctx, stage(nc, "transposed", "evacuated", "stored0", "stored1", "feat_stored") as (
            transposed, evacuated, st0, st1, feat_stored):
        stored = [st0, st1]
        ps = [ctx.enter_context(nc.psum_tensor(f"ps_pk{b}", [P, 16, P], F32)) for b in range(2)]
        tok = ctx.enter_context(nc.sbuf_tensor("tok", [P, 2, TOK_W], F32))
        copies = [[t] + ([NT + t] if t < NC else []) for t in range(NT)]
        count = [[16 * sum(len(copies[u]) for u in range(t % 2, t + 1, 2)) for t in range(NT)][t] for t in range(NT)]
        n_feat = 2 * sum(len(c) for c in copies)
        with nc.Block() as block:
            @block.sync
            def _(sp):
                for t in range(NT):
                    for slot in copies[t]:
                        cols = slice(t * P, (t + 1) * P)
                        feat = S.feat_dram[slot].rearrange("p (n c) -> p n c", c=P)
                        sp.dma_start(feat[:, 0:8, :], convT[:, 0:8, cols]).then_inc(feat_stored, 16)
                        sp.dma_start(feat[:, 8:12, :], convT[:, 16:20, cols]).then_inc(feat_stored, 16)
                for t in range(NT):
                    sp.wait_ge(evacuated, t + 1)
                    for slot in copies[t]:
                        sp.dma_start(S.tok_dram[slot], tok[:, t % 2, :]).then_inc(stored[t % 2], 16)
                sp.wait_ge(st0, count[NT - 2])
                sp.wait_ge(st1, count[NT - 1])
                sp.wait_ge(feat_stored, 16 * n_feat)

            @block.tensor
            def _(pe):
                for t in range(NT):
                    if t >= 2:
                        pe.wait_ge(evacuated, t - 1)
                    for n in range(N_TOK):
                        last = nc.tensor.transpose(ps[t % 2][:, n, :], convT[:, 4 + n, t * P:(t + 1) * P], S.ident)
                    last.then_inc(transposed, 1)

            @block.vector
            def _(dve):
                for t in range(NT):
                    dve.wait_ge(transposed, t + 1)
                    if t >= 2:
                        dve.wait_ge(stored[t % 2], count[t - 2])
                    nc.vector.tensor_copy(tok[:, t % 2, 0:N_TOK * P].rearrange("p (n c) -> p n c", c=P),
                                          ps[t % 2][:, 0:N_TOK, :])
                    nc.vector.tensor_copy(tok[:, t % 2, N_TOK * P:TOK_W],
                                          small[:, t, :, :].rearrange("p d c -> p (d c)")).then_inc(evacuated, 1)


DIRECTION_SEMS = ["rows_full", "cols_full", "cols_done", "decay_done", "ecols_done", "pool_done", "prods_done", "ant_done", "r_done",
                  "p_done", "pm_done", "xx_done", "x_done", "v_done", "vnew_done", "out_done", "state_done", "off_done",
                  "xt0_done", "kept_done", "raw_done", "mixed_done", "step_done", "loaded0", "loaded1"]


class DirectionSems:

    def __init__(self, sems):
        (self.rows_full, self.cols_full, self.cols_done, self.decay_done, self.ecols_done, self.pool_done, self.prods_done, self.ant_done,
         self.r_done, self.p_done, self.pm_done, self.xx_done, self.x_done, self.v_done, self.vnew_done, self.out_done,
         self.state_done, self.off_done, self.xt0_done, self.kept_done, self.raw_done, self.mixed_done, self.step_done, self.loaded0, self.loaded1) = sems


class DirectionBuffers:

    def __init__(self, tile, d):
        two = lambda n, cols: [tile(f"{n}{d}{j}", cols) for j in range(2)]
        self.cols = two("cols", 36)
        self.ecols = two("ecols", 36)
        self.ncol = two("ncol", 12)
        self.nbeta, self.edb = tile(f"nbeta{d}", 4), tile(f"edb{d}", 4)
        self.DT = two("DT", 12 * P)
        self.ANT = tile(f"ANT{d}", GW)
        self.QKT = tile(f"QKT{d}", GW)
        self.X, self.XT, self.Pm = tile(f"X{d}", GW), tile(f"XT{d}", GW), tile(f"Pm{d}", GW)
        self.WT = tile(f"WT{d}", 2 * GW)
        self.R, self.vnew, self.kd = tile(f"R{d}", GW), tile(f"vnew{d}", GW), tile(f"kd{d}", GW)
        self.BC = self.vnew[:, 0:SG * P]
        self.xdt, self.xde = tile(f"xdt{d}", GW), tile(f"xde{d}", GW)
        self.S, self.H = tile(f"S{d}", GW), tile(f"H{d}", GW)
        self.keptS, self.keptH = tile(f"keptS{d}", GW), self.Pm
        self.tmp = tile(f"tmp{d}", GW)


def recurrences(nc, S, acc):
    names = DIRECTION_SEMS
    N_LINKS = 28
    with ExitStack() as ctx, stage(nc, *[f"{n}_{d}" for d in range(2) for n in names], "chain", "zeroed", "pchain") as sems:
        sem = [DirectionSems(sems[d * len(names):(d + 1) * len(names)]) for d in range(2)]
        chain, zeroed, pchain = sems[2 * len(names):]
        tile = lambda n, cols: ctx.enter_context(nc.sbuf_tensor(n, [P, cols], F32))
        feat = [[tile(f"feat{j}{d}", N_FEAT * P) for d in range(2)] for j in range(2)]
        tok = [[tile(f"tokp{j}{d}", TOK_W) for d in range(2)] for j in range(2)]
        buf = [DirectionBuffers(tile, d) for d in range(2)]
        bank = [[ctx.enter_context(nc.psum_tensor(f"bk{d}{b}", [P, BANK], F32)) for b in range(4)] for d in range(2)]
        tri = [S.mat[:, MAT[f"tri{d}"], :] for d in range(2)]
        r_ident, r_neg = tile("r_ident", P), [tile(f"r_neg{d}", P) for d in range(2)]
        lvl = [[S.mat[:, MAT[f"lvl{d}_{l}"], :] for l in range(7)] for d in range(2)]
        heads = lambda ap: ap.rearrange("p (h c) -> p h c", c=P)
        h64 = lambda ap: ap.rearrange("p (h c) -> p h c", c=SP)
        q = lambda j, d, h: feat[j][d][:, h * P:(h + 1) * P]
        k = lambda j, d, h: feat[j][d][:, (4 + h) * P:(5 + h) * P]
        bT = lambda j, d, g: feat[j][d][:, (8 + g) * P:(9 + g) * P]
        cT = lambda j, d, g: feat[j][d][:, (10 + g) * P:(11 + g) * P]
        k_tok = lambda j, d: tok[j][d][:, 0:GW]
        v_tok = lambda j, d: tok[j][d][:, GW:2 * GW]
        x_tok = lambda j, d: tok[j][d][:, 2 * GW:3 * GW]
        b_tok = lambda j, d, g: tok[j][d][:, 3 * GW + g * P:3 * GW + (g + 1) * P]
        num = lambda j, d, at, n: tok[j][d][:, N_TOK * P + d * NSMALL + at:N_TOK * P + d * NSMALL + at + n]
        hd = lambda ap, h: ap[:, h * P:(h + 1) * P]
        DIRS = range(2)
        with nc.Block() as block:
            @block.sync
            def _(sp):
                for d in DIRS:
                    sp.sem_inc(sem[d].step_done, 2)
                with sp.Fori(0, STEPS // 2) as i:
                    back = [sp.snap(i * -2 + (SLOTS - 1 - j)) for j in range(2)]
                    for j in range(2):
                        for d in DIRS:
                            sp.wait_ge(sem[d].step_done, 2 * i + j + 1)
                            slot = 2 * i + j if d == 0 else back[j]
                            loaded = sem[d].loaded0 if j == 0 else sem[d].loaded1
                            sp.dma_start(feat[j][d][:, :], S.feat_dram[bass.ds(slot, 1), :, :].rearrange(
                                "o p c -> (o p) c")).then_inc(loaded, 16)
                            sp.dma_start(tok[j][d][:, :], S.tok_dram[bass.ds(slot, 1), :, :].rearrange(
                                "o p c -> (o p) c")).then_inc(loaded, 16)
                for d in DIRS:
                    sp.wait_ge(sem[d].step_done, STEPS + 1)
                    sp.dma_start(tok[0][d][:, :], S.tok_dram[(STEPS, SLOTS - 1 - STEPS)[d]]).then_inc(sem[d].loaded0, 32)

            @block.tensor
            def _(pe):
                mm = nc.tensor.matmul

                def decay_columns(n, j, loads):
                    for d in DIRS:
                        pe.wait_ge(sem[d].loaded0 if j == 0 else sem[d].loaded1, loads)
                        mm(bank[d][3][:, 0:12], tri[d], num(j, d, 0, 12), start=True, stop=True)
                        mm(bank[d][3][:, 12:24], S.ones, num(j, d, 0, 12), start=True, stop=True).then_inc(sem[d].cols_full, 1)

                def decay_rows(n, j, b):
                    for d in DIRS:
                        if b == 0:
                            pe.wait_ge(sem[d].cols_done, n + 1)
                        else:
                            pe.wait_ge(sem[d].decay_done, 3 * n + b)
                        mm(heads(bank[d][3][:, :]), rounded(r_ident[:, :]), rounded(r_neg[d][:, :]).unsqueeze(1).to_broadcast(
                            [P, 4, P]), start=True, stop=False)
                        for h in range(4):
                            last = mm(hd(bank[d][3], h), num(j, d, 4 * b + h, 1).to_broadcast([P, P]), tri[d],
                                      start=False, stop=(h == 3))
                        last.then_inc(sem[d].rows_full, 1)

                pe.wait_ge(zeroed, 1)
                decay_columns(0, 0, 32)
                for b in range(3):
                    decay_rows(0, 0, b)
                with pe.Fori(0, STEPS // 2) as i:
                    for j in range(2):
                        s = 2 * i + j
                        for d in DIRS:
                            pe.wait_ge(sem[d].step_done, s + 2)
                            pe.wait_ge(sem[d].decay_done, 3 * s + 3)
                            for h in range(GH):
                                mm(hd(bank[d][0], h), k(j, d, h), k(j, d, h), start=True, stop=True)
                                mm(hd(bank[d][1], h), k(j, d, h), q(j, d, h), start=True, stop=True)
                            for g in range(SG):
                                mm(hd(bank[d][2], g), bT(j, d, g), cT(j, d, g), start=True, stop=True)
                            for h in range(GH):
                                last = mm(hd(bank[d][3], h), k(j, d, h), hd(buf[d].S, h), start=True, stop=True)
                            last.then_inc(sem[d].prods_done, 1)
                        for level in range(7):
                            for d in DIRS:
                                if level == 0:
                                    pe.wait_ge(sem[d].ant_done, s + 1)
                                else:
                                    pe.wait_ge(sem[d].x_done, s * 7 + level)
                                for h in range(GH):
                                    if level == 0:
                                        last = nc.tensor.transpose(hd(bank[d][0], h), hd(buf[d].ANT, h), S.ident)
                                    else:
                                        last = mm(hd(bank[d][0], h), hd(buf[d].ANT, h), hd(buf[d].X, h), start=True, stop=True)
                                last.then_inc(sem[d].p_done, 1)
                            for d in DIRS if level else ():
                                if level == 1:
                                    pe.wait_ge(sem[d].xt0_done, 2 * s + 2)
                                    pe.wait_ge(sem[d].raw_done, s + 1)
                                pe.wait_ge(sem[d].pm_done, s * 6 + level)
                                for h in range(GH):
                                    if level < 6:
                                        mm(hd(bank[d][1], h), hd(buf[d].XT, h), hd(buf[d].Pm, h), start=True, stop=True)
                                    last = mm(hd(bank[d][2], h), hd(buf[d].Pm, h), hd(buf[d].XT, h), start=True, stop=True)
                                last.then_inc(sem[d].xx_done, 1)
                            if level == 2:
                                for d in DIRS:
                                    pe.wait_ge(sem[d].r_done, s + 1)
                                decay_columns(s + 1, 1 - j, 32 * i + 32 * j + 32)
                            elif 3 <= level < 6:
                                decay_rows(s + 1, 1 - j, level - 3)
                        for d in DIRS:
                            pe.wait_ge(sem[d].x_done, s * 7 + 7)
                            pe.wait_ge(sem[d].r_done, s + 1)
                            for h in range(GH):
                                last = mm(hd(bank[d][0], h), hd(buf[d].XT, h), hd(buf[d].R, h), start=True, stop=True)
                            last.then_inc(sem[d].v_done, 1)
                        for d in DIRS:
                            pe.wait_ge(sem[d].vnew_done, s + 1)
                            pe.wait_ge(sem[d].decay_done, 3 * s + 6)
                            pe.wait_ge(sem[d].pool_done, 5 * s + 5)
                            pe.wait_ge(sem[d].mixed_done, 2 * s + 2)
                            for h in range(GH):
                                mm(hd(bank[d][1], h), hd(buf[d].QKT, h), hd(buf[d].vnew, h), start=True, stop=True)
                                mm(hd(bank[d][2], h), hd(buf[d].kd, h), hd(buf[d].vnew, h), start=True, stop=True)
                                mm(hd(bank[d][3], h), q(j, d, h), hd(buf[d].S, h), start=True, stop=True)
                            for h in range(SH):
                                last = mm(bank[d][0][:, h * SP:(h + 1) * SP], hd(buf[d].WT, h),
                                          buf[d].xdt[:, h * SP:(h + 1) * SP], start=True, stop=True)
                            last.then_inc(sem[d].out_done, 1)
                        for d in DIRS:
                            pe.wait_ge(sem[d].state_done, s + 1)
                            for g in range(SG):
                                half = slice(g * 256, (g + 1) * 256)
                                mm(bank[d][1][:, half], cT(j, d, g), buf[d].H[:, half], start=True, stop=True)
                                last = mm(bank[d][2][:, half], b_tok(j, d, g), buf[d].xde[:, half], start=True, stop=True)
                            last.then_inc(sem[d].off_done, 1)

            @block.scalar
            def _(act):
                def decays(n, j):
                    for d in DIRS:
                        act.wait_ge(sem[d].cols_done, n + 1)
                        nc.scalar.activation(buf[d].ecols[j][:, :], buf[d].cols[j][:, :], ACT.Exp).then_inc(sem[d].ecols_done, 1)
                    for b in range(3):
                        for d in DIRS:
                            act.wait_ge(sem[d].rows_full, 3 * n + b + 1)
                            for h in range(4):
                                last = nc.scalar.activation(hd(buf[d].DT[j], 4 * b + h), hd(bank[d][3], h), ACT.Exp,
                                                            bias=buf[d].ncol[j][:, 4 * b + h:4 * b + h + 1])
                            last.then_inc(sem[d].decay_done, 1)

                decays(0, 0)
                with act.Fori(0, STEPS // 2) as i:
                    for j in range(2):
                        s = 2 * i + j
                        for d in DIRS:
                            act.wait_ge(sem[d].prods_done, s + 1)
                            nc.scalar.activation(buf[d].QKT[:, :], bank[d][1][:, :], ACT.Copy)
                            nc.scalar.activation(buf[d].BC[:, :], bank[d][2][:, 0:SG * P], ACT.Copy).then_inc(sem[d].raw_done, 1)
                        decays(s + 1, 1 - j)
                        for d in DIRS:
                            act.wait_ge(sem[d].v_done, s + 1)
                            act.wait_ge(sem[d].mixed_done, 2 * s + 2)
                            nc.scalar.activation(buf[d].vnew[:, :], bank[d][0][:, :], ACT.Copy).then_inc(sem[d].vnew_done, 1)

            @block.gpsimd
            def _(pool):
                with pool.Fori(0, STEPS // 2) as i:
                    for j in range(2):
                        s = 2 * i + j
                        for d in DIRS:
                            B = buf[d]
                            pool.wait_ge(sem[d].cols_done, s + 1)
                            pool.wait_ge(sem[d].step_done, s + 2)
                            mul = lambda out, a, b: nc.gpsimd.tensor_tensor(out, a, b, ALU.mult)
                            mul(h64(B.xdt[:, :]), h64(x_tok(j, d)), over(num(j, d, C_DT, 8), [P, 8, SP])).then_inc(sem[d].pool_done, 1)
                            nc.gpsimd.tensor_scalar(B.nbeta[:, :], num(j, d, C_BETA, 4), -1.0, None, ALU.mult).then_inc(sem[d].pool_done, 1)
                            pool.wait_ge(sem[d].ecols_done, s + 1)
                            mul(B.edb[:, :], num(j, d, C_BETA, 4), B.ecols[j][:, 24:28]).then_inc(sem[d].pool_done, 1)
                            pool.wait_ge(sem[d].pool_done, 5 * s + 3)
                            mul(heads(B.kd[:, :]), heads(k_tok(j, d)), over(B.edb[:, :], [P, 4, P])).then_inc(sem[d].pool_done, 1)
                            mul(h64(B.xde[:, :]), h64(B.xdt[:, :]), over(B.ecols[j][:, 28:36], [P, 8, SP])).then_inc(sem[d].pool_done, 1)
                        for d in DIRS:
                            B = buf[d]
                            pool.wait_ge(sem[d].ant_done, s + 1)
                            mul(heads(B.XT[:, :]), heads(B.ANT[:, :]), under(lvl[1 - d][0], 4, P)).then_inc(sem[d].xt0_done, 1)
                            pool.wait_ge(sem[d].xt0_done, 2 * s + 1)
                            nc.gpsimd.tensor_tensor(heads(B.XT[:, :]), heads(B.XT[:, :]), under(S.ident, 4, P),
                                                    ALU.add).then_inc(sem[d].xt0_done, 1)
                        for d in DIRS:
                            B = buf[d]
                            mul(heads(B.keptS[:, :]), heads(B.S[:, :]), over(B.ecols[j][:, 12:16], [P, 4, P]))
                        for d in DIRS:
                            B = buf[d]
                            pool.wait_ge(sem[d].raw_done, s + 1)
                            mul(B.QKT[:, :], B.QKT[:, :], B.DT[j][:, 0:GW]).then_inc(sem[d].mixed_done, 1)
                            for g in range(SG):
                                mul(heads(B.WT[:, g * GW:(g + 1) * GW]), under(hd(B.BC, g), 4, P),
                                    heads(B.DT[j][:, (1 + g) * GW:(2 + g) * GW]))
                            pool.wait_ge(sem[d].mixed_done, 2 * s + 1)
                            mul(heads(B.QKT[:, :]), heads(B.QKT[:, :]), over(num(j, d, C_BETA, 4), [P, 4, P])).then_inc(
                                sem[d].mixed_done, 1)
                        for d in DIRS:
                            B = buf[d]
                            pool.wait_ge(sem[d].xx_done, 6 * s + 6)
                            mul(h64(B.keptH[:, :]), h64(B.H[:, :]), over(B.ecols[j][:, 16:24], [P, 8, SP])).then_inc(sem[d].kept_done, 1)

            @block.vector
            def _(dve):
                tt, stt = nc.vector.tensor_tensor, nc.vector.scalar_tensor_tensor
                for d in DIRS:
                    nc.vector.memset(buf[d].S[:, :], 0.0)
                    nc.vector.memset(buf[d].H[:, :], 0.0)
                nc.vector.tensor_copy(rounded(r_ident[:, :]), S.ident)
                for d in DIRS:
                    nc.vector.tensor_copy(rounded(r_neg[d][:, :]), S.mat[:, MAT[f"neg{d}"], :])
                nc.vector.memset(acc[:, :, :], 0.0).then_inc(zeroed, 1)
                dve.wait_ge(zeroed, 1)

                def decay_columns(link, n, j):
                    for d in DIRS:
                        B = buf[d]
                        dve.wait_ge(sem[d].cols_full, n + 1)
                        link(nc.vector.tensor_copy(B.cols[j][:, 0:24], bank[d][3][:, 0:24]))
                        link(nc.vector.tensor_scalar(B.ncol[j][:, :], B.cols[j][:, 0:12], -1.0, None, ALU.mult))
                        tt(B.cols[j][:, 24:36], B.cols[j][:, 12:24], B.ncol[j][:, :], ALU.add).then_inc(sem[d].cols_done, 1)

                decay_columns(Chain(dve, pchain), 0, 0)
                with dve.Fori(0, STEPS // 2) as i:
                    link = Chain(dve, chain, i * N_LINKS)
                    back = [dve.snap(i * -2 + (SLOTS - 1 - j)) for j in range(2)]
                    for j in range(2):
                        s = 2 * i + j
                        for d in DIRS:
                            B = buf[d]
                            dve.wait_ge(sem[d].prods_done, s + 1)
                            dve.wait_ge(sem[d].pool_done, 5 * s + 2)
                            for h in range(GH):
                                last = stt(hd(B.ANT, h), hd(bank[d][0], h), B.nbeta[:, h:h + 1], hd(B.DT[j], h), ALU.mult, ALU.mult)
                            last.then_inc(sem[d].ant_done, 1)
                        for d in DIRS:
                            B = buf[d]
                            dve.wait_ge(sem[d].p_done, s * 7 + 1)
                            link(tt(heads(B.X[:, :]), heads(bank[d][0][:, :]), under(lvl[d][0], 4, P), ALU.mult))
                            tt(heads(B.X[:, :]), heads(B.X[:, :]), under(S.ident, 4, P), ALU.add).then_inc(sem[d].x_done, 1)
                        for level in range(1, 7):
                            for d in DIRS:
                                B = buf[d]
                                dve.wait_ge(sem[d].p_done, s * 7 + level + 1)
                                tt(heads(B.Pm[:, :]), heads(bank[d][0][:, :]), under(lvl[d][level], 4, P),
                                   ALU.mult).then_inc(sem[d].pm_done, 1)
                            if level <= 2:
                                d = level - 1
                                B = buf[d]
                                dve.wait_ge(sem[d].ecols_done, s + 1)
                                link(tt(heads(B.tmp[:, :]), heads(bank[d][3][:, :]), over(B.ecols[j][:, 0:4], [P, 4, P]), ALU.mult))
                                tt(B.R[:, :], v_tok(j, d), B.tmp[:, :], ALU.subtract).then_inc(sem[d].r_done, 1)
                            if level == 1:
                                for d in DIRS:
                                    dve.wait_ge(sem[d].xt0_done, 2 * s + 2)
                            if level == 3:
                                decay_columns(link, s + 1, 1 - j)
                            for d in DIRS:
                                B = buf[d]
                                dve.wait_ge(sem[d].xx_done, s * 6 + level)
                                if level < 6:
                                    tt(B.X[:, :], B.X[:, :], bank[d][1][:, :], ALU.add)
                                tt(B.XT[:, :], B.XT[:, :], bank[d][2][:, :], ALU.add).then_inc(sem[d].x_done, 1)
                        slots = [s, back[j]]
                        out_o = [acc[:, bass.ds(at, 1), 0:GW].rearrange("p o c -> p (o c)") for at in slots]
                        out_y = [acc[:, bass.ds(at, 1), GW:2 * GW].rearrange("p o c -> p (o c)") for at in slots]
                        for d in DIRS:
                            B = buf[d]
                            dve.wait_ge(sem[d].out_done, s + 1)
                            tt(out_o[d], out_o[d], bank[d][1][:, :], ALU.add)
                            dve.wait_ge(sem[d].kept_done, s + 1)
                            tt(B.S[:, :], B.keptS[:, :], bank[d][2][:, :], ALU.add).then_inc(sem[d].state_done, 1)
                            link(tt(heads(B.tmp[:, :]), heads(bank[d][3][:, :]), over(B.ecols[j][:, 0:4], [P, 4, P]), ALU.mult))
                            tt(out_o[d], out_o[d], B.tmp[:, :], ALU.add)
                            link(tt(out_y[d], out_y[d], bank[d][0][:, :], ALU.add))
                        for d in DIRS:
                            B = buf[d]
                            dve.wait_ge(sem[d].off_done, s + 1)
                            link(tt(h64(B.tmp[:, :]), h64(bank[d][1][:, :]), over(B.ecols[j][:, 4:12], [P, 8, SP]), ALU.mult))
                            tt(out_y[d], out_y[d], B.tmp[:, :], ALU.add)
                            tt(B.H[:, :], B.keptH[:, :], bank[d][2][:, :], ALU.add).then_inc(sem[d].step_done, 1)
                    assert link.n == N_LINKS, link.n


def gate_mix(nc, S, acc, mixT):
    with ExitStack() as ctx, stage(nc, "in0", "in1", "y_gated", "summed", "rooted", "gated", "transposed", "evacuated", "chain") as (
            in0, in1, y_gated, summed, rooted, gated, transposed, evacuated, chain):
        loaded = [in0, in1]
        z = ctx.enter_context(nc.sbuf_tensor("z_in", [P, 2, 2 * GW], F32))
        xs = ctx.enter_context(nc.sbuf_tensor("xs_in", [P, 2, GW], F32))
        sq = ctx.enter_context(nc.sbuf_tensor("sq_mix", [P, 2 * GW], F32))
        out = ctx.enter_context(nc.sbuf_tensor("mix_rows", [P, 2, 2 * GW], F32))
        ss = ctx.enter_context(nc.sbuf_tensor("ss_mix", [P, 2, 8], F32))
        ps = [ctx.enter_context(nc.psum_tensor(f"ps_mix{b}", [P, KT, P], F32)) for b in range(2)]
        e0, d0 = VEC["eps"][0], ROW["ssm_D"][0]
        heads = lambda ap: ap.rearrange("p (h c) -> p h c", c=P)
        h64 = lambda ap: ap.rearrange("p (h c) -> p h c", c=SP)
        with nc.Block() as block:
            @block.sync
            def _(sp):
                for t in range(NX):
                    if t >= 2:
                        sp.wait_ge(gated, t - 1)
                    sp.dma_start(z[:, t % 2, :], S.z_dram[t]).then_inc(loaded[t % 2], 16)
                    sp.dma_start(xs[:, t % 2, :], S.tok_dram[NC + t][:, 2 * GW:3 * GW]).then_inc(loaded[t % 2], 16)

            @block.scalar
            def _(act):
                def evacuate(t):
                    act.wait_ge(transposed, t + 1)
                    for m in range(KT):
                        g = VEC["gdn_norm_g"][0] if m < 4 else VEC["ssm_norm_g"][0] + m - 4
                        last = nc.scalar.activation(mixT[:, m, t * P:(t + 1) * P], ps[t % 2][:, m, :], ACT.Copy,
                                                    scale=S.vec[:, g:g + 1])
                    last.then_inc(evacuated, 1)

                for t in range(NX):
                    if t >= 1:
                        act.wait_ge(rooted, t)
                    if t >= 2:
                        act.wait_ge(gated, t - 1)
                    for h in range(4):
                        nc.scalar.activation(sq[:, h * P:(h + 1) * P], acc[:, NC + t, h * P:(h + 1) * P], ACT.Square,
                                             accum_out=ss[:, t % 2, h:h + 1])
                    act.wait_ge(y_gated, t + 1)
                    nc.scalar.activation(sq[:, GW:2 * GW], out[:, t % 2, GW:2 * GW], ACT.Square,
                                         accum_out=ss[:, t % 2, 4:5]).then_inc(summed, 1)
                    act.wait_ge(summed, t + 1)
                    nc.scalar.activation(ss[:, t % 2, 0:4], ss[:, t % 2, 0:4], ACT.Sqrt, bias=S.vec[:, e0:e0 + 1], scale=1.0 / P)
                    nc.scalar.activation(ss[:, t % 2, 4:5], ss[:, t % 2, 4:5], ACT.Sqrt, bias=S.vec[:, e0:e0 + 1],
                                         scale=1.0 / GW).then_inc(rooted, 1)
                    if t >= 1:
                        evacuate(t - 1)
                evacuate(NX - 1)

            @block.vector
            def _(dve):
                tt = nc.vector.tensor_tensor
                link = Chain(dve, chain)
                for t in range(NX):
                    dve.wait_ge(loaded[t % 2], 32 * (t // 2 + 1))
                    if t >= 2:
                        dve.wait_ge(transposed, t - 1)
                    o, y = acc[:, NC + t, 0:GW], acc[:, NC + t, GW:2 * GW]
                    link(tt(h64(out[:, t % 2, GW:2 * GW]), h64(xs[:, t % 2, :]), over(S.row[:, d0:d0 + 8], [P, 8, SP]), ALU.mult))
                    link(tt(out[:, t % 2, GW:2 * GW], out[:, t % 2, GW:2 * GW], y, ALU.add))
                    tt(out[:, t % 2, GW:2 * GW], out[:, t % 2, GW:2 * GW], z[:, t % 2, GW:2 * GW], ALU.mult).then_inc(y_gated, 1)
                    link(tt(out[:, t % 2, 0:GW], o, z[:, t % 2, 0:GW], ALU.mult))
                    dve.wait_ge(rooted, t + 1)
                    link(nc.vector.reciprocal(ss[:, t % 2, 0:5], ss[:, t % 2, 0:5]))
                    link(tt(heads(out[:, t % 2, 0:GW]), heads(out[:, t % 2, 0:GW]), over(ss[:, t % 2, 0:4], [P, 4, P]), ALU.mult))
                    nc.vector.tensor_scalar(out[:, t % 2, GW:2 * GW], out[:, t % 2, GW:2 * GW], ss[:, t % 2, 4:5],
                                            None, ALU.mult).then_inc(gated, 1)

            @block.tensor
            def _(pe):
                for t in range(NX):
                    pe.wait_ge(gated, t + 1)
                    if t >= 2:
                        pe.wait_ge(evacuated, t - 1)
                    for m in range(KT):
                        last = nc.tensor.transpose(ps[t % 2][:, m, :], out[:, t % 2, m * P:(m + 1) * P], S.ident)
                    last.then_inc(transposed, 1)


def rounded(ap):
    return ap.bitcast(mybir.dt.float32r)


class Source:

    def __init__(self, high, x, low):
        self.high, self.x, self.low = high, x, low

    def part(self, first, n):
        return Source(self.high[:, 0:n, :], self.x[:, first:first + n, :], self.low[:, first:first + n, :])


def high_parts(nc, act, src, high_done):
    for k in range(src.x.shape[1]):
        nc.scalar.activation(rounded(src.high[:, k, :]), src.x[:, k, :], ACT.Copy).then_inc(high_done, 1)


def low_parts(nc, dve, src, high_done, low_done):
    for k in range(src.x.shape[1]):
        dve.wait_ge(high_done, k + 1)
        nc.vector.tensor_tensor(rounded(src.low[:, k, :]), src.x[:, k, :], src.high[:, k, :], ALU.subtract).then_inc(low_done, 1)


N_RAW = 2
LINEAR_SEMS = [f"w_in{b}" for b in range(N_RAW)] + ["parts_free", "high_taken", "w_split", "tile_done", "ps_free"]
N_LINEAR = len(LINEAR_SEMS)


class Linear:

    def __init__(self, nc, ctx, tag, sems, kt, banks, sets, places=None):
        self.nc, self.kt = nc, kt
        self.w_in = sems[:N_RAW]
        self.parts_free, self.high_taken, self.w_split, self.tile_done, self.ps_free = sems[N_RAW:N_LINEAR]
        tile = lambda n: ctx.enter_context(nc.sbuf_tensor(f"w_{tag}_{n}", [P, kt, P], F32))
        self.raw = ([place.rearrange("p (k c) -> p k c", c=P) for place in places] if places else
                    [tile(f"raw{b}") for b in range(N_RAW)])
        self.parts = [(tile(f"high{b}"), tile(f"low{b}")) for b in range(2)]
        self.ps = [ctx.enter_context(nc.psum_tensor(f"ps_{tag}{b}", [P, banks, BANK], F32)) for b in range(sets)]

    def load(self, sp, iters, unroll, view):
        n = len(self.raw)
        sp.sem_inc(self.w_split, n)
        with sp.Fori(0, iters) as i:
            for b in range(unroll):
                sp.wait_ge(self.w_split, i * unroll + b + 1)
                sp.dma_start(self.raw[b % n][:, :, :], view(i, b)).then_inc(self.w_in[b % n], 16)

    def split(self, pool, iters, unroll):
        nc, n = self.nc, len(self.raw)
        pool.sem_inc(self.tile_done, 2)
        with pool.Fori(0, iters) as i:
            for b in range(unroll):
                raw, (high, low) = self.raw[b % n], self.parts[b % 2]
                pool.wait_ge(self.w_in[b % n], (i * (unroll // n) + b // n) * 16 + 16)
                pool.wait_ge(self.tile_done, i * unroll + b + 1)
                pool.sem_inc(self.parts_free, 1)
                nc.gpsimd.tensor_copy(rounded(high[:, :, :]), raw[:, :, :]).then_inc(self.high_taken, 1)
                pool.wait_ge(self.high_taken, i * unroll + b + 1)
                nc.gpsimd.tensor_tensor(rounded(low[:, :, :]), raw[:, :, :], high[:, :, :], ALU.subtract).then_inc(self.w_split, 1)

    def multiply(self, pe, iters, unroll, src, chunks, low_done=None):
        nc, n, sets = self.nc, len(self.raw), len(self.ps)
        pe.sem_inc(self.ps_free, sets)
        with pe.Fori(0, iters) as i:
            for b in range(unroll):
                pe.wait_ge(self.w_split, i * unroll + b + n + 1)
                pe.wait_ge(self.ps_free, i * unroll + b + 1)
                (w_high, w_low), x_high, x_low = self.parts[b % 2], src(b).high, src(b).low
                for c, (at, width) in enumerate(chunks):
                    for k in range(self.kt):
                        if low_done is not None and c == 0:
                            pe.wait_ge(low_done, k + 1)
                        for j, (w, x) in enumerate(((w_high, x_high), (w_high, x_low), (w_low, x_high))):
                            last = nc.tensor.matmul(self.ps[b % sets][:, c, 0:width], rounded(w[:, k, :]),
                                                    rounded(x[:, k, at:at + width]), start=(k == 0 and j == 0),
                                                    stop=(k == self.kt - 1 and j == 2))
                last.then_inc(self.tile_done, 1)

    def wait_tile(self, eng, m):
        eng.wait_ge(self.tile_done, 2 + m + 1)


def residual_linear(nc, S, tag, w_dram, src, xT, factor, bring=None, keep=None):
    UN = 4
    kt = w_dram.shape[0] // P
    with ExitStack() as ctx, stage(nc, *LINEAR_SEMS, "high_done", "low_done", "x_in", "added", "kept") as sems:
        L, (high_done, low_done, x_in, added, kept) = Linear(nc, ctx, tag, sems, kt, 2, 2), sems[N_LINEAR:]
        with nc.Block() as block:
            @block.sync
            def _(sp):
                L.load(sp, KT // UN, UN, lambda i, b: feature_tiles(w_dram)[:, :, bass.ds((i * UN + b) * P, P)])
                if keep is not None:
                    sp.wait_ge(added, KT)
                    sp.dma_start(keep, xT[:, :, :]).then_inc(kept, 16)
                    sp.wait_ge(kept, 16)

            @block.gpsimd
            def _(pool):
                L.split(pool, KT // UN, UN)

            @block.tensor
            def _(pe):
                L.multiply(pe, KT // UN, UN, lambda b: src, chunks_of(SEQ), low_done)

            @block.scalar
            def _(act):
                if bring is not None:
                    act.dma_start(xT[:, :, :], bring).then_inc(x_in, 16)
                high_parts(nc, act, src, high_done)

            @block.vector
            def _(dve):
                low_parts(nc, dve, src, high_done, low_done)
                if bring is not None:
                    dve.wait_ge(x_in, 16)
                for m in range(KT):
                    L.wait_tile(dve, m)
                    row = xT[:, m, :].rearrange("p (a c) -> p a c", c=BANK)
                    nc.vector.scalar_tensor_tensor(row, L.ps[m % 2][:, :, :], factor(m) if factor else 1.0, row,
                                                   ALU.mult, ALU.add).then_inc(L.ps_free, 1)
                if keep is not None:
                    dve.wait_ge(L.ps_free, 2 + KT)
                    dve.sem_inc(added, KT)


def split_stage(nc, src):
    with stage(nc, "high_done", "low_done") as (high_done, low_done):
        with nc.Block() as block:
            @block.scalar
            def _(act):
                high_parts(nc, act, src, high_done)

            @block.vector
            def _(dve):
                low_parts(nc, dve, src, high_done, low_done)


def gated_unit(nc, S, io, hT, guT, spare):
    UN, sets = 4, 4
    rows = SEQ // GRID
    with ExitStack() as ctx, stage(nc, *LINEAR_SEMS, "high_done", "low_done", "padded", "convolved", "activated",
                                   "zeroed", "chain") as sems:
        L = Linear(nc, ctx, "ffn", sems, KT, 2, sets, places=[spare[:, 1, :], spare[:, 2, :]])
        high_done, low_done, padded, convolved, activated, zeroed, chain = sems[N_LINEAR:]
        grid = ctx.enter_context(nc.sbuf_tensor("grid", [P, rows + 2, GRID + 2], F32))
        con = spare[:, 0, :].rearrange("p (r c) -> p r c", c=GRID)
        cw, cb = VEC["ffn_conv_w"][0], VEC["ffn_conv_b"][0]
        with nc.Block() as block:
            @block.sync
            def _(sp):
                gate, up = feature_tiles(io["ffn_w_gate"]), feature_tiles(io["ffn_w_up"])
                L.load(sp, 2 * FT // UN, UN, lambda i, b: (gate, up)[b % 2][:, :, bass.ds(i * (UN // 2 * P) + b // 2 * P, P)])

            @block.gpsimd
            def _(pool):
                L.split(pool, 2 * FT // UN, UN)

            @block.tensor
            def _(pe):
                L.multiply(pe, 2 * FT // UN, UN, lambda b: hT, chunks_of(SEQ), low_done)

            @block.scalar
            def _(act):
                high_parts(nc, act, hT, high_done)
                act.wait_ge(zeroed, 1)
                for f in range(FT + 1):
                    if f >= 1:
                        act.wait_ge(convolved, f)
                        nc.scalar.activation(con[:, :, :], con[:, :, :], ACT.Silu,
                                             bias=S.vec[:, cb + f - 1:cb + f]).then_inc(activated, 1)
                    if f < FT:
                        L.wait_tile(act, 2 * f)
                        for a in range(2):
                            last = nc.scalar.activation(grid[:, 1 + 8 * a:9 + 8 * a, 1:1 + GRID],
                                                        L.ps[2 * f % sets][:, a, :].rearrange("p (r c) -> p r c", c=GRID),
                                                        ACT.Copy)
                        last.then_inc(padded, 1)

            @block.vector
            def _(dve):
                link = Chain(dve, chain)
                nc.vector.memset(grid[:, :, :], 0.0).then_inc(zeroed, 1)
                low_parts(nc, dve, hT, high_done, low_done)
                for f in range(FT):
                    dve.wait_ge(padded, f + 1)
                    if f >= 1:
                        dve.wait_ge(L.ps_free, sets + 2 * f)
                    out = con[:, :, :]
                    for tap in range(9):
                        shifted = grid[:, tap // 3:tap // 3 + rows, tap % 3:tap % 3 + GRID]
                        weight = S.vec[:, cw + tap * FT + f:cw + tap * FT + f + 1]
                        if tap == 0:
                            link(nc.vector.tensor_scalar(out, shifted, weight, None, ALU.mult))
                        elif tap < 8:
                            link(nc.vector.scalar_tensor_tensor(out, shifted, weight, out, ALU.mult, ALU.add))
                        else:
                            nc.vector.scalar_tensor_tensor(out, shifted, weight, out, ALU.mult, ALU.add).then_inc(convolved, 1)
                    dve.wait_ge(activated, f + 1)
                    L.wait_tile(dve, 2 * f + 1)
                    nc.vector.tensor_tensor(guT[:, f, :].rearrange("p (a c) -> p a c", c=BANK),
                                            con[:, :, :].rearrange("p (a r) c -> p a (r c)", a=2),
                                            L.ps[(2 * f + 1) % sets][:, :, :], ALU.mult).then_inc(L.ps_free, 2)
IN2_X, IN2_Y, IN2_CQ, IN2_PE, IN2_GA, IN2_GB = 0, 1024, 2048, 2560, 2624, 3648
TWO_PI = 2 * np.pi
PI_A = 6.28125
PI_B = 0.0019350051879882812
PI_C = TWO_PI - PI_A - PI_B
CONV_W = 4


def rotary_tables(nc, S, io, cos, sin):
    R = ROPE
    with ExitStack() as ctx, stage(nc, "pos_in", "reduced", "done", "chain") as (pos_in, reduced, done, chain):
        ints = ctx.enter_context(nc.sbuf_tensor("pos_i", [R, SEQ], I32))
        turns = ctx.enter_context(nc.sbuf_tensor("turns_i", [R, SEQ], I32))
        ang = ctx.enter_context(nc.sbuf_tensor("ang", [R, SEQ], F32))
        k = ctx.enter_context(nc.sbuf_tensor("turns_f", [R, SEQ], F32))
        f0 = VEC["inv_freq"][0]
        with nc.Block() as block:
            @block.sync
            def _(sp):
                sp.dma_start(ints[:, :], io["positions"][0, :].partition_broadcast(R)).then_inc(pos_in, 16)

            @block.vector
            def _(dve):
                link = Chain(dve, chain)
                ts, stt = nc.vector.tensor_scalar, nc.vector.scalar_tensor_tensor

                def into_half_turn(a):
                    link(ts(k[:, :], a, float(np.pi), -TWO_PI, ALU.is_gt, ALU.mult))
                    link(nc.vector.tensor_tensor(a, a, k[:, :], ALU.add))
                    link(ts(k[:, :], a, -float(np.pi), TWO_PI, ALU.is_lt, ALU.mult))
                    link(nc.vector.tensor_tensor(a, a, k[:, :], ALU.add))
                    link(ts(a, a, 3.1415925, -3.1415925, ALU.min, ALU.max))

                dve.wait_ge(pos_in, 16)
                link(nc.vector.tensor_copy(ang[:, :], ints[:, :]))
                link(ts(ang[:, :], ang[:, :], S.vec[0:R, f0:f0 + 1], None, ALU.mult))
                link(ts(k[:, :], ang[:, :], float(1 / TWO_PI), None, ALU.mult))
                link(nc.vector.tensor_copy(turns[:, :], k[:, :]))
                link(nc.vector.tensor_copy(k[:, :], turns[:, :]))
                for part in (PI_A, PI_B, PI_C):
                    link(stt(ang[:, :], k[:, :], -part, ang[:, :], ALU.mult, ALU.add))
                into_half_turn(ang[:, :])
                link(ts(cos[0:R, :], ang[:, :], float(np.pi / 2), None, ALU.add))
                into_half_turn(cos[0:R, :])
                dve.sem_inc(reduced, 1)

            @block.scalar
            def _(act):
                act.wait_ge(reduced, 1)
                nc.scalar.activation(sin[0:R, :], ang[:, :], ACT.Sin)
                nc.scalar.activation(cos[0:R, :], cos[0:R, :], ACT.Sin).then_inc(done, 1)


def latent_projections(nc, S, w, uT, lat, k_pe):
    with ExitStack() as ctx, stage(nc, "tile_done", "evacuated") as (tile_done, evacuated):
        n_out = 2 * LORA + ROPE
        ps = [ctx.enter_context(nc.psum_tensor(f"ps_lat{b}", [P, 2, BANK], F32)) for b in range(4)]
        with nc.Block() as block:
            @block.tensor
            def _(pe):
                for m in range(5):
                    rows = min(P, n_out - m * P)
                    if m >= 4:
                        pe.wait_ge(evacuated, m - 3)
                    for c in range(2):
                        for k in range(KT):
                            last = nc.tensor.matmul(ps[m % 4][0:rows, c, :], w[:, k, m * P:m * P + rows],
                                                    uT[:, k, c * BANK:(c + 1) * BANK], start=(k == 0), stop=(k == KT - 1))
                    last.then_inc(tile_done, 1)

            @block.vector
            def _(dve):
                for m in range(5):
                    dve.wait_ge(tile_done, m + 1)
                    out = lat[:, m, :] if m < 4 else k_pe[0:ROPE, :]
                    nc.vector.tensor_copy(out.rearrange("p (a c) -> p a c", a=2),
                                          ps[m % 4][0:out.shape[0], :, :]).then_inc(evacuated, 1)


def head_projections(nc, S, io, h0, lat, qk, v):
    with ExitStack() as ctx, stage(nc, "w_loaded", "unit_done", "evacuated") as (w_loaded, unit_done, evacuated):
        wq = ctx.enter_context(nc.sbuf_tensor(f"w_q{h0}", [P, LT, 2 * QK], F32))
        wkv = ctx.enter_context(nc.sbuf_tensor(f"w_kv{h0}", [P, LT, 2, NOPE + DV], F32))
        ps = [ctx.enter_context(nc.psum_tensor(f"ps_hp{h0}{b}", [P, 2, BANK], F32)) for b in range(4)]
        units = []
        for h in range(2):
            units += [(lambda k, h=h: wq[:, k, h * QK:h * QK + NOPE], 0, NOPE, qk[:, h, 0, :]),
                      (lambda k, h=h: wq[:, k, h * QK + NOPE:(h + 1) * QK], 0, ROPE, qk[0:ROPE, h, 1, :]),
                      (lambda k, h=h: wkv[:, k, h, 0:NOPE], LT, NOPE, qk[:, h, 2, :])]
        with nc.Block() as block:
            @block.sync
            def _(sp):
                sp.dma_start(wq[:, :, :], feature_tiles(io["w_uq_2"])[:, :, h0 * QK:(h0 + 2) * QK]).then_inc(w_loaded, 16)
                sp.dma_start(wkv[:, :, :, :].rearrange("p k h c -> p k (h c)"), feature_tiles(io["w_ukv_2"])[
                    :, :, h0 * (NOPE + DV):(h0 + 2) * (NOPE + DV)]).then_inc(w_loaded, 16)

            @block.tensor
            def _(pe):
                pe.wait_ge(w_loaded, 32)
                for u, (weights, first, rows, _out) in enumerate(units):
                    if u >= 4:
                        pe.wait_ge(evacuated, u - 3)
                    for c in range(2):
                        for k in range(LT):
                            last = nc.tensor.matmul(ps[u % 4][0:rows, c, :], weights(k),
                                                    lat[:, first + k, c * BANK:(c + 1) * BANK], start=(k == 0), stop=(k == LT - 1))
                    last.then_inc(unit_done, 1)
                for g in range(2):
                    u = len(units) + g
                    pe.wait_ge(evacuated, u - 3)
                    for t in range(4):
                        for k in range(LT):
                            at = (g * 4 + t) * P
                            last = nc.tensor.matmul(ps[u % 4][:, t // 2, t % 2 * 256:t % 2 * 256 + 256].rearrange(
                                "p (h c) -> p h c", h=2), lat[:, LT + k, at:at + P], wkv[:, k, :, NOPE:NOPE + DV],
                                start=(k == 0), stop=(k == LT - 1))
                    last.then_inc(unit_done, 1)

            @block.vector
            def _(dve):
                for u in range(len(units) + 2):
                    dve.wait_ge(unit_done, u + 1)
                    if u < len(units):
                        out = units[u][3].rearrange("p (a c) -> p a c", a=2)
                    else:
                        g = u - len(units)
                        out = v[:, g * 4:g * 4 + 4, :].rearrange("p (a t) c -> p a (t c)", a=2)
                    nc.vector.tensor_copy(out, ps[u % 4][0:out.shape[0], :, :]).then_inc(evacuated, 1)


def rotate(nc, S, tag, tiles, cos, sin):
    parts = [t[:, c * BANK:(c + 1) * BANK] for t in tiles for c in range(2)]
    cols = lambda u: slice(u % 2 * BANK, (u % 2 + 1) * BANK)
    with ExitStack() as ctx, stage(nc, "turned", "times_cos", "times_sin", "rotated") as (turned, times_cos, times_sin, rotated):
        ps = [ctx.enter_context(nc.psum_tensor(f"ps_rot{tag}{b}", [P, BANK], F32)) for b in range(4)]
        tmp = ctx.enter_context(nc.sbuf_tensor(f"rot_tmp{tag}", [P, 2, BANK], F32))
        with nc.Block() as block:
            @block.tensor
            def _(pe):
                for u, x in enumerate(parts):
                    if u >= 4:
                        pe.wait_ge(times_sin, u - 3)
                    nc.tensor.matmul(ps[u % 4][0:ROPE, :], S.mat[0:ROPE, MAT["rope"], 0:ROPE], x,
                                     start=True, stop=True).then_inc(turned, 1)

            @block.gpsimd
            def _(pool):
                for u, x in enumerate(parts):
                    pool.wait_ge(turned, u + 1)
                    nc.gpsimd.tensor_tensor(x, x, cos[0:ROPE, cols(u)], ALU.mult).then_inc(times_cos, 1)

            @block.vector
            def _(dve):
                for u in range(len(parts) + 1):
                    if u < len(parts):
                        dve.wait_ge(turned, u + 1)
                        if u >= 2:
                            dve.wait_ge(rotated, u - 1)
                        nc.vector.tensor_tensor(tmp[0:ROPE, u % 2, :], ps[u % 4][0:ROPE, :], sin[0:ROPE, cols(u)],
                                                ALU.mult).then_inc(times_sin, 1)
                    if u >= 1:
                        x = parts[u - 1]
                        dve.wait_ge(times_sin, u)
                        dve.wait_ge(times_cos, u)
                        nc.vector.tensor_tensor(x, x, tmp[0:ROPE, (u - 1) % 2, :], ALU.add).then_inc(rotated, 1)


def attention(nc, S, h0, qk, v, oT):
    scale = float(QK) ** -0.5
    units = [(h, b) for h in range(2) for b in range(NX)]
    U = len(units)
    with ExitStack() as ctx, stage(nc, "scores_done", "max_done", "exp_done", "probs_done", "turned", "turned_out",
                                   "pv_done", "o_copied", "chain", "mask_ready") as (
            scores_done, max_done, exp_done, probs_done, turned, turned_out, pv_done, o_copied, chain, mask_ready):
        p = ctx.enter_context(nc.sbuf_tensor(f"probs{h0}", [P, 2, SEQ], F32))
        pT = ctx.enter_context(nc.sbuf_tensor(f"probsT{h0}", [P, 2, SEQ], F32))
        st = ctx.enter_context(nc.sbuf_tensor(f"stat{h0}", [P, 2, 4], F32))
        one = ctx.enter_context(nc.sbuf_tensor(f"r_ident{h0}", [P, P], F32))
        mask = ctx.enter_context(nc.sbuf_tensor(f"r_mask{h0}", [P, P], F32))
        sc = [ctx.enter_context(nc.psum_tensor(f"ps_sc{h0}{b}", [P, 2 * BANK], F32)) for b in range(2)]
        tr = ctx.enter_context(nc.psum_tensor(f"ps_tr{h0}", [P, 2 * BANK], F32))
        po = [ctx.enter_context(nc.psum_tensor(f"ps_o{h0}{b}", [P, P], F32)) for b in range(2)]
        with nc.Block() as block:
            @block.tensor
            def _(pe):
                def scores(u):
                    h, b = units[u]
                    q_cols = slice(b * P, (b + 1) * P)
                    if u >= 2:
                        pe.wait_ge(exp_done, u - 1)
                    for at, n in chunks_of((b + 1) * P):
                        out, final = sc[u % 2][:, at:at + n], at + n == (b + 1) * P
                        nc.tensor.matmul(out, qk[:, h, 0, q_cols], qk[:, h, 2, at:at + n], start=True, stop=False)
                        last = nc.tensor.matmul(out, qk[0:ROPE, h, 1, q_cols], qk[0:ROPE, h, 3, at:at + n], start=False, stop=not final)
                    if u == 0:
                        pe.wait_ge(mask_ready, 1)
                    last = nc.tensor.matmul(sc[u % 2][:, b * P:(b + 1) * P], rounded(one[:, :]), rounded(mask[:, :]),
                                            start=False, stop=True)
                    last.then_inc(scores_done, 1)

                def turn(u):
                    pe.wait_ge(probs_done, u + 1)
                    if u >= 1:
                        pe.wait_ge(turned_out, u)
                    for t in range(units[u][1] + 1):
                        last = nc.tensor.transpose(tr[:, t * P:(t + 1) * P], p[:, u % 2, t * P:(t + 1) * P], S.ident)
                    last.then_inc(turned, 1)

                def values(u):
                    h, b = units[u]
                    pe.wait_ge(turned_out, u + 1)
                    if u >= 2:
                        pe.wait_ge(o_copied, u - 1)
                    for t in range(b + 1):
                        last = nc.tensor.matmul(po[u % 2][:, :], v[:, t, h * DV:(h + 1) * DV], pT[:, u % 2, t * P:(t + 1) * P],
                                                start=(t == 0), stop=(t == b))
                    last.then_inc(pv_done, 1)

                scores(0)
                for u in range(U + 1):
                    if u + 1 < U:
                        scores(u + 1)
                    if u < U:
                        turn(u)
                    if u >= 1:
                        values(u - 1)

            @block.vector
            def _(dve):
                link = Chain(dve, chain)
                nc.vector.tensor_copy(rounded(one[:, :]), S.ident)
                nc.vector.tensor_copy(rounded(mask[:, :]), S.mat[:, MAT["neg1"], :]).then_inc(mask_ready, 1)
                for u in range(U + 2):
                    if u < U:
                        n = (units[u][1] + 1) * P
                        dve.wait_ge(scores_done, u + 1)
                        link(nc.vector.reduce_max(st[:, u % 2, 0:1], sc[u % 2][:, 0:n], AX.X))
                        nc.vector.tensor_scalar(st[:, u % 2, 1:2], st[:, u % 2, 0:1], -scale, None, ALU.mult).then_inc(max_done, 1)
                    if u >= 2:
                        w = u - 2
                        h, b = units[w]
                        dve.wait_ge(pv_done, w + 1)
                        nc.vector.tensor_copy(oT[:, h0 + h, b * P:(b + 1) * P], po[w % 2][:, :]).then_inc(o_copied, 1)
                    if u < U:
                        dve.wait_ge(exp_done, u + 1)
                        link(nc.vector.reciprocal(st[:, u % 2, 3:4], st[:, u % 2, 2:3]))
                        nc.vector.tensor_scalar(p[:, u % 2, 0:n], p[:, u % 2, 0:n], st[:, u % 2, 3:4], None,
                                                ALU.mult).then_inc(probs_done, 1)

            @block.scalar
            def _(act):
                for u in range(U + 1):
                    if u < U:
                        n = (units[u][1] + 1) * P
                        act.wait_ge(max_done, u + 1)
                        if u >= 2:
                            act.wait_ge(turned, u - 1)
                        nc.scalar.activation(p[:, u % 2, 0:n], sc[u % 2][:, 0:n], ACT.Exp, bias=st[:, u % 2, 1:2],
                                             scale=scale, accum_out=st[:, u % 2, 2:3]).then_inc(exp_done, 1)
                    if u >= 1:
                        w = u - 1
                        n = (units[w][1] + 1) * P
                        act.wait_ge(turned, w + 1)
                        if w >= 2:
                            act.wait_ge(pv_done, w - 1)
                        nc.scalar.activation(pT[:, w % 2, 0:n], tr[:, 0:n], ACT.Copy).then_inc(turned_out, 1)


def gated_linear(nc, S, tag, w_gate, gate_src, w_value, value_src, out, add, spare):
    UN, sets = 4, 4
    with ExitStack() as ctx, stage(nc, *LINEAR_SEMS, "high_done", "low_done", "gate_done", "chain") as sems:
        L, (high_done, low_done, gate_done, chain) = Linear(nc, ctx, tag, sems, KT, 2, sets, places=[spare[:, 1, :], spare[:, 2, :]]), sems[N_LINEAR:]
        gate = spare[:, 0, :].rearrange("p (a c) -> p a c", a=2)
        halves = lambda ap: ap.rearrange("p (a c) -> p a c", a=2)
        with nc.Block() as block:
            @block.sync
            def _(sp):
                sp.sem_inc(L.w_split, 2)
                for m in range(2 * KT):
                    sp.wait_ge(L.w_split, m + 1)
                    sp.dma_start(L.raw[m % 2][:, :, :], feature_tiles((w_gate, w_value)[m % 2])[
                        :, :, m // 2 * P:(m // 2 + 1) * P]).then_inc(L.w_in[m % 2], 16)

            @block.gpsimd
            def _(pool):
                L.split(pool, 2 * KT // UN, UN)

            @block.tensor
            def _(pe):
                L.multiply(pe, 2 * KT // UN, UN, lambda b: (gate_src, value_src)[b % 2], chunks_of(SEQ), low_done)

            @block.scalar
            def _(act):
                high_parts(nc, act, value_src, high_done)
                for m in range(KT):
                    L.wait_tile(act, 2 * m)
                    if m >= 1:
                        act.wait_ge(L.ps_free, sets + 2 * m)
                    nc.scalar.activation(gate[:, :, :], L.ps[2 * m % sets][:, :, :], ACT.Sigmoid).then_inc(gate_done, 1)

            @block.vector
            def _(dve):
                low_parts(nc, dve, value_src, high_done, low_done)
                link = Chain(dve, chain)
                for m in range(KT):
                    dve.wait_ge(gate_done, m + 1)
                    L.wait_tile(dve, 2 * m + 1)
                    g, value = gate[:, :, :], L.ps[(2 * m + 1) % sets][:, :, :]
                    if add:
                        link(nc.vector.tensor_tensor(g, g, value, ALU.mult))
                        last = nc.vector.tensor_tensor(halves(out[:, m, :]), halves(out[:, m, :]), g, ALU.add)
                    else:
                        last = nc.vector.tensor_tensor(halves(out[:, m, :]), g, value, ALU.mult)
                    last.then_inc(L.ps_free, 2)


def causal_projection(nc, S, io, uT, xr):
    UN, pad = 4, CONV_W - 1
    cw, cb = VEC["conv_w_2"][0], VEC["conv_b_2"][0]
    with ExitStack() as ctx, stage(nc, *LINEAR_SEMS, "convolved", "zeroed", "chain") as sems:
        L, (convolved, zeroed, chain) = Linear(nc, ctx, "xr", sems, KT, 2, 2), sems[N_LINEAR:]
        row = ctx.enter_context(nc.sbuf_tensor("row_xr", [P, 2, SEQ + pad], F32))
        with nc.Block() as block:
            @block.sync
            def _(sp):
                L.load(sp, KT // UN, UN, lambda i, b: feature_tiles(io["w_in_2"])[:, :, bass.ds((i * UN + b) * P, P)])

            @block.gpsimd
            def _(pool):
                L.split(pool, KT // UN, UN)

            @block.tensor
            def _(pe):
                L.multiply(pe, KT // UN, UN, lambda b: uT, chunks_of(SEQ))

            @block.scalar
            def _(act):
                act.wait_ge(zeroed, 1)
                for m in range(KT):
                    L.wait_tile(act, m)
                    if m >= 2:
                        act.wait_ge(convolved, m - 1)
                    nc.scalar.activation(row[:, m % 2, pad:pad + SEQ].rearrange("p (a c) -> p a c", a=2),
                                         L.ps[m % 2][:, :, :], ACT.Copy).then_inc(L.ps_free, 1)

            @block.vector
            def _(dve):
                link = Chain(dve, chain)
                nc.vector.memset(row[:, :, 0:pad], 0.0).then_inc(zeroed, 1)
                for m in range(KT):
                    dve.wait_ge(L.ps_free, 2 + m + 1)
                    tap = lambda j: S.vec[:, cw + j * KT + m:cw + j * KT + m + 1]
                    out = xr[:, m, :]
                    link(nc.vector.tensor_scalar(out, row[:, m % 2, 0:SEQ], tap(0), S.vec[:, cb + m:cb + m + 1], ALU.mult, ALU.add))
                    for j in range(1, CONV_W):
                        last = nc.vector.scalar_tensor_tensor(out, row[:, m % 2, j:j + SEQ], tap(j), out, ALU.mult, ALU.add)
                        if j < CONV_W - 1:
                            link(last)
                    last.then_inc(convolved, 1)


def recurrent_unit(nc, S, io, xr):
    with ExitStack() as ctx, stage(nc, "w_loaded", "rates", "lam_exp", "lam_done", "gates_full", "sig_done", "exps_done",
                                   "mult_ready", "rooted", "scanned", "chain", "doubled") as (
            w_loaded, rates, lam_exp, lam_done, gates_full, sig_done, exps_done, mult_ready, rooted, scanned, chain, doubled):
        w = ctx.enter_context(nc.sbuf_tensor("w_lru", [P, 2, KT, P], F32))
        t = {n: ctx.enter_context(nc.sbuf_tensor(f"lam_{n}", [P, KT], F32)) for n in ("e", "m", "q", "z", "z2", "p")}
        fac = ctx.enter_context(nc.sbuf_tensor("lam_fac", [P, 3, KT], F32))
        r = ctx.enter_context(nc.sbuf_tensor("lru_r", [P, 2, SEQ], F32))
        g = ctx.enter_context(nc.sbuf_tensor("lru_i", [P, 2, SEQ], F32))
        a = ctx.enter_context(nc.sbuf_tensor("lru_a", [P, 2, SEQ], F32))
        e2 = ctx.enter_context(nc.sbuf_tensor("lru_e2", [P, 2, SEQ], F32))
        ps = [ctx.enter_context(nc.psum_tensor(f"ps_lru{b}", [P, 2, 2 * BANK], F32)) for b in range(2)]
        lam0, ba, bx = VEC["lru_lambda_2"][0], VEC["lru_ba_2"][0], VEC["lru_bx_2"][0]
        lam = S.vec[:, lam0:lam0 + KT]
        flat = lambda n: t[n][:, :]
        with nc.Block() as block:
            @block.sync
            def _(sp):
                for j, n in enumerate(("lru_wa_2", "lru_wx_2")):
                    sp.dma_start(w[:, j, :, :], io[n].rearrange("n k j -> k n j")).then_inc(w_loaded, 16)

            @block.tensor
            def _(pe):
                pe.wait_ge(w_loaded, 32)
                for n in range(KT):
                    if n >= 2:
                        pe.wait_ge(sig_done, n - 1)
                    for j in range(2):
                        for c in range(2):
                            last = nc.tensor.matmul(ps[n % 2][:, j, c * BANK:(c + 1) * BANK], w[:, j, n, :],
                                                    xr[:, n, c * BANK:(c + 1) * BANK], start=True, stop=True)
                    last.then_inc(gates_full, 1)

            @block.scalar
            def _(act):
                act.wait_ge(chain, 2)
                nc.scalar.activation(flat("e"), flat("e"), ACT.Exp).then_inc(lam_exp, 1)
                for n in range(KT):
                    act.wait_ge(gates_full, n + 1)
                    if n >= 2:
                        act.wait_ge(scanned, n - 1)
                    nc.scalar.activation(r[:, n % 2, :], ps[n % 2][:, 0, :], ACT.Sigmoid, bias=S.vec[:, ba + n:ba + n + 1])
                    nc.scalar.activation(g[:, n % 2, :], ps[n % 2][:, 1, :], ACT.Sigmoid,
                                         bias=S.vec[:, bx + n:bx + n + 1]).then_inc(sig_done, 1)
                    if n == 0:
                        act.wait_ge(lam_done, 1)
                    act.wait_ge(sig_done, n + 1)
                    nc.scalar.activation(a[:, n % 2, :], r[:, n % 2, :], ACT.Exp, scale=fac[:, 0, n:n + 1])
                    nc.scalar.activation(e2[:, n % 2, :], r[:, n % 2, :], ACT.Exp, scale=fac[:, 1, n:n + 1])
                    nc.scalar.activation(r[:, n % 2, :], r[:, n % 2, :], ACT.Tanh, scale=fac[:, 2, n:n + 1]).then_inc(exps_done, 1)
                    act.wait_ge(mult_ready, n + 1)
                    nc.scalar.activation(e2[:, n % 2, :], e2[:, n % 2, :], ACT.Sqrt).then_inc(rooted, 1)

            @block.vector
            def _(dve):
                tt, stt, ts = nc.vector.tensor_tensor, nc.vector.scalar_tensor_tensor, nc.vector.tensor_scalar
                link = Chain(dve, chain)
                link(ts(flat("m"), lam, -1.0, 0.0, ALU.mult, ALU.max))
                link(stt(flat("e"), flat("m"), -2.0, lam, ALU.mult, ALU.subtract))
                dve.wait_ge(lam_exp, 1)
                log1p_series(nc, link, flat)
                link(stt(flat("m"), flat("z2"), 2.0, flat("m"), ALU.mult, ALU.add))
                for j, c in enumerate((-8.0, -16.0, 8.0)):
                    last = ts(fac[:, j, :], flat("m"), c, None, ALU.mult)
                last.then_inc(lam_done, 1)
                for n in range(KT):
                    b = n % 2
                    dve.wait_ge(exps_done, n + 1)
                    stt(e2[:, b, :], e2[:, b, :], 1.0, r[:, b, :], ALU.add, ALU.mult).then_inc(mult_ready, 1)
                    link(tt(g[:, b, :], g[:, b, :], xr[:, n, :], ALU.mult))
                    dve.wait_ge(rooted, n + 1)
                    link(tt(g[:, b, :], g[:, b, :], e2[:, b, :], ALU.mult))
                    nc.vector.tensor_tensor_scan(xr[:, n, :], a[:, b, :], g[:, b, :], 0.0, ALU.mult, ALU.add).then_inc(scanned, 1)


def gelu_projection(nc, S, io, uT, xr):
    UN = 4
    with ExitStack() as ctx, stage(nc, *LINEAR_SEMS, "multiplied") as sems:
        L, multiplied = Linear(nc, ctx, "yr", sems, KT, 2, 2), sems[N_LINEAR]
        act_row = ctx.enter_context(nc.sbuf_tensor("gelu_row", [P, 2, 2, BANK], F32))
        with nc.Block() as block:
            @block.sync
            def _(sp):
                L.load(sp, KT // UN, UN, lambda i, b: feature_tiles(io["w_in_2"])[:, :, bass.ds((i * UN + b) * P + IN2_Y, P)])

            @block.gpsimd
            def _(pool):
                L.split(pool, KT // UN, UN)

            @block.tensor
            def _(pe):
                L.multiply(pe, KT // UN, UN, lambda b: uT, chunks_of(SEQ))

            @block.scalar
            def _(act):
                for m in range(KT):
                    L.wait_tile(act, m)
                    if m >= 2:
                        act.wait_ge(multiplied, m - 1)
                    nc.scalar.activation(act_row[:, m % 2, :, :], L.ps[m % 2][:, :, :], ACT.Gelu_apprx_tanh).then_inc(L.ps_free, 1)

            @block.vector
            def _(dve):
                for m in range(KT):
                    dve.wait_ge(L.ps_free, 2 + m + 1)
                    out = xr[:, m, :].rearrange("p (a c) -> p a c", a=2)
                    nc.vector.tensor_tensor(out, out, act_row[:, m % 2, :, :], ALU.mult).then_inc(multiplied, 1)
def store_rows(nc, S, tag, src, out_dram):
    with ExitStack() as ctx, stage(nc, "transposed", "copied", "stored0", "stored1") as (transposed, copied, st0, st1):
        stored = [st0, st1]
        rows = ctx.enter_context(nc.sbuf_tensor(f"rows_{tag}", [P, 2, D], F32))
        ps = [ctx.enter_context(nc.psum_tensor(f"ps_{tag}{b}", [P, D], F32)) for b in range(2)]
        with nc.Block() as block:
            @block.tensor
            def _(pe):
                for t in range(NX):
                    if t >= 2:
                        pe.wait_ge(copied, t - 1)
                    for k in range(KT):
                        last = nc.tensor.transpose(ps[t % 2][:, k * P:(k + 1) * P], src[:, k, t * P:(t + 1) * P], S.ident)
                    last.then_inc(transposed, 1)

            @block.vector
            def _(dve):
                for t in range(NX):
                    dve.wait_ge(transposed, t + 1)
                    if t >= 2:
                        dve.wait_ge(stored[t % 2], 16 * (t // 2))
                    nc.vector.tensor_copy(rows[:, t % 2, :], ps[t % 2][:, :]).then_inc(copied, 1)

            @block.sync
            def _(sp):
                for t in range(NX):
                    sp.wait_ge(copied, t + 1)
                    sp.dma_start(out_dram[t * P:(t + 1) * P, :], rows[:, t % 2, :]).then_inc(stored[t % 2], 16)
                sp.wait_ge(st0, 16 * NX // 2)
                sp.wait_ge(st1, 16 * NX // 2)


def route(nc, S, io, xnT, gates, dest, block_expert):
    E, J = NE, EPG
    with ExitStack() as ctx, stage(nc, "w_loaded", "logits_done", "diff_ready", "exp_done", "choice_ready", "counted",
                                   "chain", "ids_ready", "zero_ready", "zero_stored", "dest_ready", "scattered") as (
            w_loaded, logits_done, diff_ready, exp_done, choice_ready, counted, chain, ids_ready, zero_ready, zero_stored,
            dest_ready, scattered):
        tile = lambda n, shape, dt=F32: ctx.enter_context(nc.sbuf_tensor(f"rt_{n}", shape, dt))
        w = tile("w", [P, KT, NG + NE])
        L = tile("logits", [P, NX, NG + NE])
        desc = tile("desc", [P, J])
        top = tile("top", [P, 4, NX])
        eq, diff, eg = tile("eq", [P, NX, J]), tile("diff", [P, NX, J]), tile("eg", [P, NX, J])
        hot = [tile(f"hot{n}", [P, NX, J]) for n in range(3)]
        spread = tile("spread", [P, NX, NG, J])
        pick = [tile(f"pick{n}", [P, NX, E]) for n in range(2)]
        both = tile("both", [P, NX, E])
        prob = tile("prob", [P, 4, NX])
        cnt, blocks, ends, starts = [tile(n, [P, E]) for n in ("cnt", "blocks", "ends", "starts")]
        dest_f, rank, whole = [tile(n, [P, 2 * NX]) for n in ("dest_f", "rank", "whole")]
        cmp = tile("cmp", [1, MOE_BLOCKS, E])
        be_f = tile("be_f", [1, MOE_BLOCKS])
        ids = tile("ids", [P, NX], I32)
        zeros = tile("zeros", [P, MOE_BLOCKS], I32)
        ps = ctx.enter_context(nc.psum_tensor("ps_logits", [P, NX, P], F32))
        ps_rank = ctx.enter_context(nc.psum_tensor("ps_rank", [P, NX, E], F32))
        ps_cnt = ctx.enter_context(nc.psum_tensor("ps_cnt", [P, E], F32))
        with nc.Block() as block:
            @block.sync
            def _(sp):
                sp.dma_start(w[:, :, :], io["router_w"].rearrange("(k p) m -> p k m", p=P)).then_inc(w_loaded, 16)
                sp.wait_ge(zero_ready, 1)
                sp.dma_start(S.slot_dram.rearrange("(p b) o -> p (b o)", p=P), zeros[:, :]).then_inc(zero_stored, 16)
                sp.wait_ge(zero_stored, 16)

            @block.gpsimd
            def _(pool):
                nc.gpsimd.memset(zeros[:, :], 0).then_inc(zero_ready, 1)
                nc.gpsimd.iota(ids[:, :], pattern=[[P, NX]], base=0, channel_multiplier=1).then_inc(ids_ready, 1)
                pool.wait_ge(ids_ready, 1)
                pool.wait_ge(zero_stored, 16)
                pool.wait_ge(dest_ready, 1)
                for c in range(2 * NX):
                    nc.gpsimd.indirect_dma_start(out=S.slot_dram, out_offset=bass.IndirectOffsetOnAxis(
                        ap=dest[:, c:c + 1], axis=0), in_=ids[:, c % NX:c % NX + 1], in_offset=None).then_inc(scattered, 16)
                pool.wait_ge(scattered, 16 * 2 * NX)

            @block.tensor
            def _(pe):
                pe.wait_ge(w_loaded, 16)
                for t in range(NX):
                    for k in range(KT):
                        last = nc.tensor.matmul(ps[:, t, 0:NG + NE], xnT[:, k, t * P:(t + 1) * P], w[:, k, :],
                                                start=(k == 0), stop=(k == KT - 1))
                last.then_inc(logits_done, 1)
                pe.wait_ge(choice_ready, 1)
                for t in range(NX):
                    for u in range(t + 1):
                        nc.tensor.matmul(ps_rank[:, t, :], S.ones if u < t else S.mat[:, MAT["before"], :], both[:, u, :],
                                         start=(u == 0), stop=(u == t))
                for t in range(NX):
                    last = nc.tensor.matmul(ps_cnt[:, :], S.ones, both[:, t, :], start=(t == 0), stop=(t == NX - 1))
                last.then_inc(counted, 1)

            @block.scalar
            def _(act):
                act.wait_ge(diff_ready, 1)
                nc.scalar.activation(diff[:, :, :], diff[:, :, :], ACT.Exp)
                nc.scalar.activation(prob[:, 1, :], prob[:, 1, :], ACT.Exp).then_inc(exp_done, 1)

            @block.vector
            def _(dve):
                tt, ts, stt = nc.vector.tensor_tensor, nc.vector.tensor_scalar, nc.vector.scalar_tensor_tensor
                link = Chain(dve, chain)
                r0, i0, s0 = ROW["router_b"][0], ROW["expert_iota"][0], ROW["block_start"][0]
                wide = [P, NX, J]

                def first_of_max(x, m, out):
                    link(nc.vector.reduce_max(m, x, AX.X))
                    link(tt(eq[:, :, :], x, over(m, wide), ALU.is_equal))
                    link(tt(eq[:, :, :], eq[:, :, :], under(desc[:, :], NX, J), ALU.mult))
                    link(nc.vector.reduce_max(top[:, 3, :], eq[:, :, :], AX.X))
                    link(tt(out, eq[:, :, :], over(top[:, 3, :], wide), ALU.is_equal))

                link(ts(desc[:, :], S.row[:, i0:i0 + J], -1.0, float(J), ALU.mult, ALU.add))
                dve.wait_ge(logits_done, 1)
                link(tt(L[:, :, :], ps[:, :, 0:NG + NE], under(S.row[:, r0:r0 + NG + NE], NX, NG + NE), ALU.add))
                g, e = L[:, :, 0:NG], L[:, :, NG:NG + NE].rearrange("p t (g j) -> p t g j", g=NG)
                first_of_max(g, top[:, 0, :], hot[0][:, :, :])
                link(tt(diff[:, :, :], g, over(top[:, 0, :], wide), ALU.subtract))
                link(tt(spread[:, :, :, :], e, hot[0][:, :, :].unsqueeze(3).to_broadcast([P, NX, NG, J]), ALU.mult))
                link(nc.vector.reduce_sum(eg[:, :, :], spread[:, :, :, :].rearrange("p t g j -> p t j g"), AX.X))
                first_of_max(eg[:, :, :], top[:, 1, :], hot[1][:, :, :])
                link(stt(eg[:, :, :], hot[1][:, :, :], -1e30, eg[:, :, :], ALU.mult, ALU.add))
                first_of_max(eg[:, :, :], top[:, 2, :], hot[2][:, :, :])
                link(tt(prob[:, 1, :], top[:, 2, :], top[:, 1, :], ALU.subtract))
                for n in range(2):
                    link(tt(pick[n][:, :, :].rearrange("p t (g j) -> p t g j", g=NG),
                            hot[0][:, :, :].unsqueeze(3).to_broadcast([P, NX, NG, J]),
                            hot[1 + n][:, :, :].unsqueeze(2).to_broadcast([P, NX, NG, J]), ALU.mult))
                dve.sem_inc(diff_ready, 1)
                tt(both[:, :, :], pick[0][:, :, :], pick[1][:, :, :], ALU.add).then_inc(choice_ready, 1)
                dve.wait_ge(exp_done, 1)
                link(nc.vector.reduce_sum(prob[:, 0, :], diff[:, :, :], AX.X))
                link(ts(prob[:, 2, :], prob[:, 1, :], 1.0, None, ALU.add))
                link(tt(prob[:, 0, :], prob[:, 0, :], prob[:, 2, :], ALU.mult))
                link(nc.vector.reciprocal(gates[:, 0:NX], prob[:, 0, :]))
                link(tt(gates[:, NX:2 * NX], gates[:, 0:NX], prob[:, 1, :], ALU.mult))
                dve.wait_ge(counted, 1)
                link(nc.vector.tensor_copy(cnt[:, :], ps_cnt[:, :]))
                link(ts(blocks[:, :], cnt[:, :], 0.0, None, ALU.is_gt))
                for n in range(1, NX):
                    link(stt(blocks[:, :], cnt[:, :], float(n * P), blocks[:, :], ALU.is_gt, ALU.add))
                link(nc.vector.tensor_tensor_scan(ends[:, :], S.ones[:, 0:E], blocks[:, :], 0.0, ALU.mult, ALU.add))
                link(tt(starts[:, :], ends[:, :], blocks[:, :], ALU.subtract))
                for n in range(2):
                    at = slice(n * NX, (n + 1) * NX)
                    link(tt(both[:, :, :], pick[n][:, :, :], ps_rank[:, :, :], ALU.mult))
                    link(nc.vector.reduce_sum(rank[:, at], both[:, :, :], AX.X))
                    link(tt(both[:, :, :], pick[n][:, :, :], under(starts[:, :], NX, E), ALU.mult))
                    link(nc.vector.reduce_sum(dest_f[:, at], both[:, :, :], AX.X))
                link(ts(whole[:, :], rank[:, :], float(P), None, ALU.is_ge))
                for n in range(2, NX):
                    link(stt(whole[:, :], rank[:, :], float(n * P), whole[:, :], ALU.is_ge, ALU.add))
                link(stt(dest_f[:, :], rank[:, :], float(MOE_BLOCKS), dest_f[:, :], ALU.mult, ALU.add))
                link(stt(dest_f[:, :], whole[:, :], float(1 - P * MOE_BLOCKS), dest_f[:, :], ALU.mult, ALU.add))
                link(nc.vector.tensor_copy(dest[:, :], dest_f[:, :]))
                dve.sem_inc(dest_ready, 1)
                link(tt(cmp[:, :, :], ends[0:1, :].unsqueeze(1).to_broadcast([1, MOE_BLOCKS, E]),
                        S.row[0:1, s0:s0 + MOE_BLOCKS].unsqueeze(2).to_broadcast([1, MOE_BLOCKS, E]), ALU.is_le))
                link(nc.vector.reduce_sum(be_f[:, :], cmp[:, :, :], AX.X))
                link(ts(be_f[:, :], be_f[:, :], float(NE - 1), None, ALU.min))
                link(nc.vector.tensor_copy(block_expert[:, :], be_f[:, :]))


def expert_blocks(nc, S, io, block_expert):
    N, B = MOE_BLOCKS, 4
    with ExitStack() as ctx, stage(nc, *[f"{n}{b}" for n in ("x_in", "w13_in", "w2_in") for b in range(B)], "ids_in",
                                   "x_turned", "xT_ready", "h_done", "s_ready", "g_ready", "g_turned", "gT_ready",
                                   "y_done", "y_ready", "st0", "st1", "picked", "gathers") as sems:
        x_in, w13_in, w2_in = sems[0:B], sems[B:2 * B], sems[2 * B:3 * B]
        ids_in, x_turned, xT_ready, h_done, s_ready, g_ready, g_turned, gT_ready, y_done, y_ready, st0, st1, picked, gathers = (
            sems[3 * B:])
        stored = [st0, st1]
        tile = lambda n, shape, many=2: [ctx.enter_context(nc.sbuf_tensor(f"{n}{b}", shape, F32)) for b in range(many)]
        ids = ctx.enter_context(nc.sbuf_tensor("mo_ids", [P, N], I32))
        column = ctx.enter_context(nc.sbuf_tensor("mo_column", [P, B], I32))
        x, xT = tile("mo_x", [P, D], B), tile("mo_xT", [P, KT, P])
        w13, w2 = tile("mo_w13", [P, KT, 2 * DE], B), tile("mo_w2", [P, 2, D], B)
        s, g, gT, y = tile("mo_s", [P, DE]), tile("mo_g", [P, DE]), tile("mo_gT", [P, 2, P]), tile("mo_y", [P, D])
        ps_x = ctx.enter_context(nc.psum_tensor("ps_mx", [P, KT, P], F32))
        ps_h = [ctx.enter_context(nc.psum_tensor(f"ps_mh{b}", [P, BANK], F32)) for b in range(2)]
        ps_g = ctx.enter_context(nc.psum_tensor("ps_mg", [P, 2, P], F32))
        ps_y = ctx.enter_context(nc.psum_tensor("ps_my", [P, 2, BANK], F32))
        with nc.Block() as block:
            @block.sync
            def _(sp):
                sp.dma_start(ids[:, :], S.slot_dram.rearrange("(p b) o -> p (b o)", p=P)).then_inc(ids_in, 16)
                sp.sem_inc(h_done, B)
                sp.sem_inc(y_done, B)
                with sp.Fori(0, N // B) as i:
                    for q in range(B):
                        e = sp.value_load(block_expert[0:1, bass.ds(B * i + q, 1)], min_val=0, max_val=NE - 1)
                        sp.wait_ge(h_done, B * i + q + 1)
                        for j, n in enumerate(("exp_w1_2", "exp_w3_2")):
                            sp.dma_start(w13[q][:, :, j * DE:(j + 1) * DE], io[n][bass.ds(e, 1), :, :].rearrange(
                                "o (k p) m -> p (o k) m", p=P)).then_inc(w13_in[q], 16)
                        sp.wait_ge(y_done, B * i + q + 1)
                        sp.dma_start(w2[q][:, :, :], io["exp_w2_2"][bass.ds(e, 1), :, :].rearrange(
                            "o (k p) m -> p (o k) m", p=P)).then_inc(w2_in[q], 16)

            @block.gpsimd
            def _(pool):
                pool.wait_ge(ids_in, 16)
                pool.sem_inc(x_turned, B)
                with pool.Fori(0, N // B) as i:
                    for q in range(B):
                        pool.wait_ge(x_turned, B * i + q + 1)
                        nc.gpsimd.tensor_copy(column[:, q:q + 1], ids[:, bass.ds(B * i + q, 1)]).then_inc(picked, 1)
                        pool.wait_ge(picked, B * i + q + 1)
                        pool.sem_inc(gathers, 1)
                        nc.gpsimd.indirect_dma_start(out=x[q][:, :], out_offset=None, in_=S.xn_dram, in_offset=
                                                     bass.IndirectOffsetOnAxis(ap=column[:, q:q + 1], axis=0)
                                                     ).then_inc(x_in[q], 16)

            def in_turns(eng, step):
                for q in range(B):
                    step(q, 0, q, first=(q == 0))
                with eng.Fori(1, N // B) as i:
                    for q in range(B):
                        step(B * i + q, i, q)

            @block.tensor
            def _(pe):
                def turn_x(b, turn, q):
                    pe.wait_ge(x_in[q], turn * 16 + 16)
                    pe.wait_ge(xT_ready, b + 1)
                    for k in range(KT):
                        last = nc.tensor.transpose(ps_x[:, k, :], x[q][:, k * P:(k + 1) * P], S.ident)
                    last.then_inc(x_turned, 1)

                def second_product(b, turn, q):
                    pe.wait_ge(w2_in[q], turn * 16 + 16)
                    pe.wait_ge(gT_ready, b + 1)
                    pe.wait_ge(y_ready, b + 1)
                    for c in range(2):
                        for k in range(2):
                            last = nc.tensor.matmul(ps_y[:, c, :], gT[q % 2][:, k, :], w2[q][:, k, c * BANK:(c + 1) * BANK],
                                                    start=(k == 0), stop=(k == 1))
                    last.then_inc(y_done, 1)

                def step(b, turn, q, first=False, final=False):
                    pe.wait_ge(w13_in[q], turn * 32 + 32)
                    pe.wait_ge(xT_ready, b + 2)
                    for k in range(KT):
                        last = nc.tensor.matmul(ps_h[q % 2][:, :], xT[q % 2][:, k, :], w13[q][:, k, :],
                                                start=(k == 0), stop=(k == KT - 1))
                    last.then_inc(h_done, 1)
                    if not final:
                        turn_x(b + 1, turn + (q + 1) // B, (q + 1) % B)
                    if not first:
                        second_product(b - 1, turn - (1 if q == 0 else 0), (q - 1) % B)
                    pe.wait_ge(g_ready, b + 1)
                    for k in range(2):
                        last = nc.tensor.transpose(ps_g[:, k, :], g[q % 2][:, k * P:(k + 1) * P], S.ident)
                    last.then_inc(g_turned, 1)

                pe.sem_inc(y_ready, 1)
                pe.sem_inc(xT_ready, 1)
                turn_x(0, 0, 0)
                for q in range(B):
                    step(q, 0, q, first=(q == 0))
                with pe.Fori(1, N // B - 1) as i:
                    for q in range(B):
                        step(B * i + q, i, q)
                for q in range(B):
                    step(N - B + q, N // B - 1, q, final=(q == B - 1))
                second_product(N - 1, N // B - 1, B - 1)

            @block.scalar
            def _(act):
                def outputs(b, turns, q):
                    act.wait_ge(y_done, b + B + 1)
                    act.wait_ge(stored[q], turns * 16 + 16)
                    nc.scalar.activation(y[q][:, :], ps_y[:, :, :].rearrange("p a c -> p (a c)"), ACT.Copy).then_inc(y_ready, 1)
                    act.wait_ge(y_ready, b + 2)
                    act.dma_start(y_rows[bass.ds(b, 1), :, :].rearrange("o p d -> (o p) d"), y[q][:, :]).then_inc(stored[q], 16)

                def step(b, turn, q, first=False):
                    act.wait_ge(h_done, b + B + 1)
                    nc.scalar.activation(s[q % 2][:, :], ps_h[q % 2][:, 0:DE], ACT.Silu).then_inc(s_ready, 1)
                    if not first:
                        outputs(b - 1, turn * 2 + (q - 1) // 2, (q - 1) % 2)
                    act.wait_ge(g_turned, b + 1)
                    nc.scalar.activation(gT[q % 2][:, :, :], ps_g[:, :, :], ACT.Copy).then_inc(gT_ready, 1)

                y_rows = S.y_dram.rearrange("(p b) d -> b p d", p=P)
                act.sem_inc(st0, 16)
                act.sem_inc(st1, 16)
                in_turns(act, step)
                outputs(N - 1, N // 2 - 1, 1)
                act.wait_ge(st0, 16 * (N // 2 + 1))
                act.wait_ge(st1, 16 * (N // 2 + 1))

            @block.vector
            def _(dve):
                with dve.Fori(0, N // 2) as i:
                    for q in range(2):
                        b = 2 * i + q
                        dve.wait_ge(x_turned, b + B + 1)
                        nc.vector.tensor_copy(xT[q][:, :, :], ps_x[:, :, :]).then_inc(xT_ready, 1)
                        dve.wait_ge(s_ready, b + 1)
                        nc.vector.tensor_tensor(g[q][:, :], s[q][:, :], ps_h[q][:, DE:2 * DE], ALU.mult).then_inc(g_ready, 1)


def combine(nc, S, io, xT, gates, dest):
    with ExitStack() as ctx, stage(nc, "y_in0", "y_in1", "turned", "added", "stored0", "stored1", "chain") as (
            y_in0, y_in1, turned, added, st0, st1, chain):
        y_in, stored = [y_in0, y_in1], [st0, st1]
        ys = [[ctx.enter_context(nc.sbuf_tensor(f"cy{b}{n}", [P, D], F32)) for n in range(2)] for b in range(2)]
        rows = ctx.enter_context(nc.sbuf_tensor("c_rows", [P, 2, D], F32))
        ps = [ctx.enter_context(nc.psum_tensor(f"ps_c{b}", [P, D], F32)) for b in range(2)]
        with nc.Block() as block:
            @block.gpsimd
            def _(pool):
                for t in range(NX):
                    if t >= 2:
                        pool.wait_ge(added, t - 1)
                    for n in range(2):
                        nc.gpsimd.indirect_dma_start(out=ys[t % 2][n][:, :], out_offset=None, in_=S.y_dram, in_offset=
                                                     bass.IndirectOffsetOnAxis(ap=dest[:, n * NX + t:n * NX + t + 1], axis=0)
                                                     ).then_inc(y_in[t % 2], 16)

            @block.tensor
            def _(pe):
                for t in range(NX):
                    if t >= 2:
                        pe.wait_ge(added, t - 1)
                    for k in range(KT):
                        last = nc.tensor.transpose(ps[t % 2][:, k * P:(k + 1) * P], xT[:, k, t * P:(t + 1) * P], S.ident)
                    last.then_inc(turned, 1)

            @block.vector
            def _(dve):
                stt = nc.vector.scalar_tensor_tensor
                link = Chain(dve, chain)
                for t in range(NX):
                    dve.wait_ge(turned, t + 1)
                    dve.wait_ge(y_in[t % 2], 32 * (t // 2 + 1))
                    if t >= 2:
                        dve.wait_ge(stored[t % 2], 16 * (t // 2))
                    row = rows[:, t % 2, :]
                    link(stt(row, ys[t % 2][0][:, :], gates[:, t:t + 1], ps[t % 2][:, :], ALU.mult, ALU.add))
                    stt(row, ys[t % 2][1][:, :], gates[:, NX + t:NX + t + 1], row, ALU.mult, ALU.add).then_inc(added, 1)

            @block.sync
            def _(sp):
                for t in range(NX):
                    sp.wait_ge(added, t + 1)
                    sp.dma_start(io["out"][t * P:(t + 1) * P, :], rows[:, t % 2, :]).then_inc(stored[t % 2], 16)
                sp.wait_ge(st0, 16 * NX // 2)
                sp.wait_ge(st1, 16 * NX // 2)
def build_program(nc, io):
    with ExitStack() as ctx:
        dram = lambda n, shape: nc.dram_tensor(n, shape, F32, kind="Internal").ap()
        tile = lambda n, shape, dt=F32: ctx.enter_context(nc.sbuf_tensor(n, shape, dt))
        S = Shared()
        S.mat, S.vec, S.row = tile("mat", [P, NMAT, P]), tile("vec", [P, NVEC]), tile("row", [P, NROW])
        S.mod, S.fac = tile("mod", [P, 2, 48]), tile("fac", [P, 3, KT])
        S.xT_dram = dram("xT_scratch", (P, KT, T))
        S.z_dram = dram("z_scratch", (NX, P, 2 * GW))
        S.feat_dram = dram("feat_scratch", (SLOTS, P, N_FEAT * P))
        S.tok_dram = dram("tok_scratch", (SLOTS, P, TOK_W))
        S.xn_dram = dram("xn_scratch", (SEQ, D))
        S.y_dram = dram("y_scratch", (MOE_BLOCKS * P, D))
        S.slot_dram = nc.dram_tensor("slot_scratch", (MOE_BLOCKS * P, 1), I32, kind="Internal").ap()
        S.ident, S.ones = S.mat[:, MAT["ident"], :], S.mat[:, MAT["ones"], :]
        vec = lambda n, k=0: S.vec[:, VEC[n][0] + k:VEC[n][0] + k + 1]
        load_constants(nc, S, io)
        modulation(nc, S, io)
        with ExitStack() as mixer:
            convT = mixer.enter_context(nc.sbuf_tensor("convT", [P, NCONV, T], F32))
            small = mixer.enter_context(nc.sbuf_tensor("small", [P, NT, 2, NSMALL], F32))
            chunks = chunks_of(T, CTX)
            with nc.sbuf_tensor("hT", [P, KT, T], F32) as hT:
                xT = convT[:, 0:KT, :]
                load_transposed(nc, S, io, xT)
                piece = lambda a: lambda c, k: a[:, k, chunks[c][0]:chunks[c][0] + chunks[c][1]]
                with nc.sbuf_tensor("w_z", [P, KT, 2 * GW], F32) as wz, nc.sbuf_tensor("w_small", [P, KT, 32], F32) as ws:
                    w_in = feature_tiles(io["w_in"])
                    rms_features(nc, S, "n1", piece(xT), piece(hT), KT, [n for _, n in chunks],
                                 lambda c, k: S.fac[:, 1 if c == 0 else 0, k:k + 1],
                                 lambda c, k: S.mod[:, 1 if c == 0 else 0, k:k + 1], moves=[
                                     (ws[:, :, :], feature_tiles(io["w_small"])),
                                     (wz[:, :, 0:GW], w_in[:, :, IN_ZG:IN_ZG + GW]),
                                     (wz[:, :, GW:2 * GW], w_in[:, :, IN_ZS:IN_ZS + GW]),
                                     (S.xT_dram, xT)])
                    token_projections(nc, S, hT, small, wz, ws)
                conv_projection(nc, S, "qkv", io["w_in"][:, IN_QKV:IN_QKV + NQKV * P], NQKV, hT, convT, 0,
                                VEC["gdn_conv_w"][0], None)
                conv_projection(nc, S, "xbc", io["w_in"][:, IN_XBC:IN_XBC + NXBC * P], NXBC, hT, convT, NQKV,
                                VEC["ssm_conv_w"][0], VEC["ssm_conv_b"][0])
            parts = [(m, at, n) for m in range(2 * GH) for at, n in chunks]
            part = lambda c, k: convT[:, parts[c][0], parts[c][1]:parts[c][1] + parts[c][2]]
            rms_features(nc, S, "l2", part, part, 1, [n for _, _, n in parts],
                         lambda c, k: P ** -0.5 if parts[c][0] < GH else 1.0, divisor=1, on_pool=GH * len(chunks))
            pack_tiles(nc, S, convT, small)
        chunks = chunks_of(SEQ)
        piece = lambda a: lambda c, k: a[:, k, c * BANK:(c + 1) * BANK]
        pieces = [BANK] * (SEQ // BANK)
        stream = S.xT_dram[:, :, CTX:T]
        bytes_of = lambda kt: kt * SEQ * 4
        offset = {}

        @contextmanager
        def features(n, kt=KT):
            with nc.sbuf_tensor(n, [P, kt, SEQ], F32) as t:
                offset[n] = nc.sbuf_base - bytes_of(kt)
                yield t

        def source(n, high, x, place, kt=KT):
            at = lambda part, where, kt: nc.alloc_sbuf_tensor_at(f"{n}_{part}", [P, kt, SEQ], F32, offset=offset[where])
            return Source(at("high", high, KT), x, at("low", place, kt))

        acc = tile("acc", [P, SLOTS, 2 * GW])
        offset["stream"] = nc.sbuf_base - bytes_of(SLOTS)
        recurrences(nc, S, acc)
        xT, spare = acc[:, 0:KT, :], acc[:, KT:SLOTS, :]
        with features("mixT") as mixT:
            gate_mix(nc, S, acc, mixT)
            with features("mix_high"):
                residual_linear(nc, S, "wout", io["w_out"], source("mix", "mix_high", mixT, "mixT"), xT, lambda m: S.mod[:, 0, 16 + m:17 + m],
                                bring=stream, keep=stream)
        with features("guT", FT) as guT, features("ffn_high"):
            rms_features(nc, S, "n2", piece(xT), piece(xT), KT, pieces, lambda c, k: S.fac[:, 2, k:k + 1],
                         lambda c, k: S.mod[:, 0, 24 + k:25 + k])
            gated_unit(nc, S, io, source("ffn_in", "ffn_high", xT, "stream"), guT, spare)
            hidden = source("hidden", "ffn_high", guT, "guT", FT)
            for first, n in ((0, 8), (8, 7), (15, 7)):
                residual_linear(nc, S, f"wdown{first}", io["ffn_w_down"][first * P:(first + n) * P, :],
                                hidden.part(first, n), xT,
                                lambda m: S.mod[:, 0, 40 + m:41 + m], bring=stream if first == 0 else None)
        rms_features(nc, S, "nf", piece(xT), piece(xT), KT, pieces, lambda c, k: vec("final_norm_g", k))
        with features("oT") as oT, features("uT") as uT:
            with ExitStack() as mla:
                lat = spare
                k_pe, cos, sin = [mla.enter_context(nc.sbuf_tensor(n, [P, SEQ], F32)) for n in ("k_pe", "cos", "sin")]
                with nc.sbuf_tensor("w_latent", [P, KT, 2 * LORA + ROPE], F32) as w_lat:
                    rms_features(nc, S, "n1b", piece(xT), piece(uT), KT, pieces, lambda c, k: vec("norm1_g_2", k), moves=[
                        (w_lat[:, :, :], feature_tiles(io["w_in_2"])[:, :, IN2_CQ:IN2_CQ + 2 * LORA + ROPE]), (stream, xT)])
                    rotary_tables(nc, S, io, cos, sin)
                    latent_projections(nc, S, w_lat, uT, lat, k_pe)
                for first, g in ((0, "q_norm_g_2"), (LT, "kv_norm_g_2")):
                    part = piece(lat[:, first:first + LT, :])
                    rms_features(nc, S, g, part, part, LT, pieces, lambda c, k: vec(g, k))
                qk = mla.enter_context(nc.sbuf_tensor("qk", [P, 2, 4, SEQ], F32))
                v = mla.enter_context(nc.sbuf_tensor("v", [P, NX, 2 * DV], F32))
                for h0 in range(0, NH, 2):
                    head_projections(nc, S, io, h0, lat, qk, v)
                    units = [(h, w, c) for h in range(2) for w in range(2) for c in range(2)]
                    rows = (P, ROPE)
                    place = lambda u, k: qk[0:rows[k], units[u][0], 2 * units[u][1] + k,
                                            units[u][2] * BANK:(units[u][2] + 1) * BANK]
                    before = lambda u, k: (k_pe[0:ROPE, units[u][2] * BANK:(units[u][2] + 1) * BANK]
                                           if k == 1 and units[u][1] == 1 else place(u, k))
                    gain = lambda u, k: vec(("q_g_", "k_g_")[units[u][1]] + ("nope", "rope")[k])[0:rows[k], :]
                    rms_features(nc, S, f"qk{h0}", before, place, 2, [BANK] * len(units), gain, divisor=QK)
                    rotate(nc, S, h0, [qk[0:ROPE, h, w, :] for h in range(2) for w in (1, 3)], cos, sin)
                    attention(nc, S, h0, qk, v, oT)
            with features("merged") as merged:
                u = source("u", "stream", uT, "uT")
                split_stage(nc, u)
                gate_b = io["w_in_2"][:, IN2_GB:IN2_GB + D]
                with features("o_high"):
                    gated_linear(nc, S, "mla", gate_b, u, io["w_mla_o_2"], source("o", "o_high", oT, "oT"), merged, False, spare)
                xr = oT
                causal_projection(nc, S, io, u, xr)
                recurrent_unit(nc, S, io, xr)
                gelu_projection(nc, S, io, u, xr)
                gate_a = io["w_in_2"][:, IN2_GA:IN2_GA + D]
                with features("xr_high"):
                    gated_linear(nc, S, "rnn", gate_a, u, io["w_rnn_o_2"], source("xr", "xr_high", xr, "oT"), merged, True, spare)
                residual_linear(nc, S, "wout2", io["w_out_2"], source("merged", "oT", merged, "merged"), xT, None, bring=stream)
        gates, dest = tile("gates", [P, 2 * NX]), tile("dest", [P, 2 * NX], U32)
        block_expert = tile("block_expert", [1, MOE_BLOCKS], I32)
        with nc.sbuf_tensor("xnT", [P, KT, SEQ], F32) as xnT:
            rms_features(nc, S, "n2b", piece(xT), piece(xnT), KT, pieces, lambda c, k: vec("norm2_g_2", k))
            store_rows(nc, S, "xn", xnT, S.xn_dram)
            route(nc, S, io, xnT, gates, dest, block_expert)
        expert_blocks(nc, S, io, block_expert)
        combine(nc, S, io, xT, gates, dest)


def _columns(a):
    return a.reshape(-1, P).T


def _constants():
    i, j = np.arange(P)[:, None], np.arange(P)[None, :]
    m = np.zeros((NMAT, P, P), np.float32)
    m[MAT["ident"]] = i == j
    m[MAT["ones"]] = 1
    m[MAT["tri0"]] = i <= j
    m[MAT["tri1"]] = i >= j
    m[MAT["neg0"]] = np.where(i <= j, 0, -1e30)
    m[MAT["neg1"]] = np.where(i >= j, 0, -1e30)
    m[MAT["before"]] = i < j
    half = ROPE // 2
    m[MAT["rope"]] = np.where((j < half) & (i == j + half), -1, 0) + np.where((j >= half) & (j < ROPE) & (i == j - half), 1, 0)
    for level in range(7):
        n = 1 << level
        low = (i // (2 * n) == j // (2 * n)) & (i // n % 2 == 1) & (j // n % 2 == 0)
        m[MAT[f"lvl0_{level}"]] = low
        m[MAT[f"lvl1_{level}"]] = low.T
    return np.ascontiguousarray(m.transpose(1, 0, 2))


def _layout(a):
    f = lambda n: np.asarray(a[n])[0]
    vec = {n: _columns(f(n)) for n in ("b_ada", "norm1_g", "norm2_g", "gdn_norm_g", "ssm_norm_g", "ffn_conv_b",
                                       "norm1_g_2", "conv_b_2", "lru_ba_2", "lru_bx_2", "lru_lambda_2", "q_norm_g_2",
                                       "kv_norm_g_2", "norm2_g_2", "ssm_conv_b")}
    vec["c"] = _columns(np.asarray(a["c"])[0])
    vec["c_ctx"] = _columns(np.asarray(a["c_ctx"]))
    vec["final_norm_g"] = _columns(np.asarray(a["final_norm_g"]))
    for n in ("gdn_conv_w", "ssm_conv_w", "ffn_conv_w", "conv_w_2"):
        vec[n] = _columns(f(n).reshape(-1))
    for n, to in (("qk_norm_q_g_2", "q_g"), ("qk_norm_k_g_2", "k_g")):
        vec[to + "_nope"] = f(n)[:NOPE, None]
        vec[to + "_rope"] = np.concatenate([f(n)[NOPE:], np.zeros(P - ROPE, np.float32)])[:, None]
    vec["eps"] = np.full((P, 1), EPS, np.float32)
    freq = (10000.0 ** (-np.arange(0, ROPE, 2, dtype=np.float32) / ROPE)).astype(np.float32)
    vec["inv_freq"] = np.tile(freq, P // len(freq))[:, None]
    vecs = np.zeros((P, NVEC), np.float32)
    for n, (at, w) in VEC.items():
        vecs[:, at:at + w] = vec[n]
    row = {n: f(n).reshape(-1) for n in ("gdn_dt_bias", "ssm_dt_bias", "gdn_A_log", "ssm_A_log", "ssm_D")}
    row["router_b"] = np.concatenate([f("router_bg_2"), f("router_be_2")])
    row["expert_iota"] = np.arange(NE, dtype=np.float32)
    row["block_start"] = np.arange(MOE_BLOCKS, dtype=np.float32)
    rows = np.zeros((1, NROW), np.float32)
    for n, (at, w) in ROW.items():
        rows[0, at:at + w] = row[n]
    w_in = f("w_in")
    out = dict(mats=_constants(), vecs=vecs, rows=rows, x=f("x"), ctx=f("ctx"), w_ada=f("w_ada"), w_in=w_in,
               w_small=np.concatenate([w_in[:, IN_AB:IN_AB + 16], w_in[:, IN_DT:IN_DT + 16]], axis=1),
               positions=np.asarray(a["positions_2"]).astype(np.int32),
               router_w=np.concatenate([f("router_wg_2"), f("router_we_2")], axis=1))
    for n in ("w_out", "ffn_w_gate", "ffn_w_up", "ffn_w_down", "w_in_2", "lru_wa_2", "lru_wx_2", "w_rnn_o_2", "w_uq_2",
              "w_ukv_2", "w_mla_o_2", "w_out_2", "exp_w1_2", "exp_w3_2", "exp_w2_2"):
        out[n] = f(n)
    return {n: np.ascontiguousarray(v) for n, v in out.items()}


def kernel(**inputs):
    import concourse.bacc as bacc
    from concourse.bass_utils import run_bass_kernel_spmd

    nc = bacc.Bacc("TRN2", target_bir_lowering=False, num_devices=1)
    arrays = {f"in_{n}_dram": v for n, v in _layout(inputs).items()}
    io = {n[3:-5]: nc.dram_tensor(n, v.shape, mybir.dt.from_np(v.dtype), kind="ExternalInput").ap()
          for n, v in arrays.items()}
    io["out"] = nc.dram_tensor("out_0_dram", (SEQ, D), F32, kind="ExternalOutput").ap()
    build_program(nc, io)
    result = run_bass_kernel_spmd(nc, [arrays], core_ids=[0])
    return result.results[0]["out_0_dram"].reshape(1, SEQ, D)
```
